# Optimizing a Trainium2 kernel written in Bass

```python
import math
import jax
import jax.numpy as jnp
from jax import lax
import numpy as np

D_MODEL = 1024
BATCH = 1
SEQ = 128
DEPTH = 2
DEC_BATCH = 1
DEC_SEQ = 512
PAST_LEN = 128

GRID_W = 64
POS_BASE = 10000.0
EPS = 1e-6
A_HEADS = 4
A_DK = 128
A_DV = 128
A_DIM = A_HEADS * A_DV
SHORT_CONV = 7
CHUNK = 64
B_CH = D_MODEL // 2
B_CONV = 31
MIX_WIDTH = A_DIM + B_CH
P_AB = 4 * A_DIM + 4 * A_HEADS + 2 * B_CH
C_GROUPS = 8
PEER_HEADS = 8
PEER_KEYS = 128
PEER_N = PEER_KEYS * PEER_KEYS
PEER_DK = 128
PEER_TOPK = 16
PEER_BLOCK = 128

kernel_name = 'hybrid_deltanet_conformer_fnet_peer_diffusion_step'

F32 = jnp.float32

def rmsnorm(x, g):
    xf = x.astype(F32)
    y = xf * lax.rsqrt(jnp.mean(xf * xf, axis=-1, keepdims=True) + EPS) * g.astype(F32)
    return y.astype(x.dtype)

def layernorm(x, g, b):
    xf = x.astype(F32)
    mu = jnp.mean(xf, axis=-1, keepdims=True)
    var = jnp.mean(jnp.square(xf - mu), axis=-1, keepdims=True)
    return ((xf - mu) * lax.rsqrt(var + EPS) * g.astype(F32) + b.astype(F32)).astype(x.dtype)

def l2norm(x):
    xf = x.astype(F32)
    return xf * lax.rsqrt(jnp.sum(xf * xf, axis=-1, keepdims=True) + EPS)

def depthwise_conv(x, w):
    k, ch = w.shape
    return lax.conv_general_dilated(x, w.astype(x.dtype)[:, None, :], window_strides=(1,),
                                    padding=[(k // 2, k // 2)],
                                    dimension_numbers=('NWC', 'WIO', 'NWC'),
                                    feature_group_count=ch)

def grid_pos_emb(n_tokens):
    rows = n_tokens // GRID_W
    r = jnp.repeat(jnp.arange(rows, dtype=F32), GRID_W)
    col = jnp.tile(jnp.arange(GRID_W, dtype=F32), rows)
    nf = D_MODEL // 4
    freqs = jnp.exp(-math.log(POS_BASE) * jnp.arange(nf, dtype=F32) / nf)
    ar = r[:, None] * freqs
    ac = col[:, None] * freqs
    return jnp.concatenate([jnp.sin(ar), jnp.cos(ar), jnp.sin(ac), jnp.cos(ac)], axis=-1)

def gated_delta_chunked(q, k, v, log_g, beta, s0):
    b, s, h, dk = q.shape
    dv = v.shape[-1]
    n = s // CHUNK

    def to_blocks(t):
        t = t.astype(F32).reshape(b, n, CHUNK, h, *t.shape[3:])
        return jnp.moveaxis(t, 3, 1)

    qb, kb, vb = to_blocks(q), to_blocks(k), to_blocks(v)
    lg, bt = to_blocks(log_g), to_blocks(beta)
    gam = jnp.cumsum(lg, axis=-1)
    idx = jnp.arange(CHUNK)
    incl = idx[:, None] >= idx[None, :]
    strict = idx[:, None] > idx[None, :]
    diff = gam[..., :, None] - gam[..., None, :]
    decay = jnp.where(incl, jnp.exp(jnp.where(incl, diff, 0.0)), 0.0)
    kk = jnp.einsum('bhntd,bhnid->bhnti', kb, kb)
    a_mat = jnp.where(strict, bt[..., :, None] * decay * kk, 0.0) + jnp.eye(CHUNK, dtype=F32)
    rhs = jnp.concatenate([kb * (bt * jnp.exp(gam))[..., None], vb * bt[..., None]], axis=-1)
    sol = lax.linalg.triangular_solve(a_mat, rhs, left_side=True, lower=True, unit_diagonal=True)
    w_blk, u_blk = sol[..., :dk], sol[..., dk:]
    p_blk = decay * jnp.einsum('bhntd,bhnid->bhnti', qb, kb)
    q_dec = qb * jnp.exp(gam)[..., None]
    k_dec = kb * jnp.exp(gam[..., -1:] - gam)[..., None]
    g_last = jnp.exp(gam[..., -1])

    def step(state, xs):
        w_c, u_c, p_c, q_c, k_c, g_c = xs
        u = u_c - jnp.einsum('bhcd,bhde->bhce', w_c, state)
        o = jnp.einsum('bhcd,bhde->bhce', q_c, state) + jnp.einsum('bhti,bhie->bhte', p_c, u)
        state = g_c[..., None, None] * state + jnp.einsum('bhcd,bhce->bhde', k_c, u)
        return state, o

    xs = tuple(jnp.moveaxis(t, 2, 0) for t in (w_blk, u_blk, p_blk, q_dec, k_dec, g_last))
    s_fin, o = lax.scan(step, s0.astype(F32), xs)
    o = jnp.transpose(o, (1, 0, 3, 2, 4)).reshape(b, s, h, dv)
    return o, s_fin

def delta_mixer(qkv, z, alpha, beta_raw, conv_w, a_log, dt_bias, norm_g, s0):
    b, s, _ = qkv.shape
    qkv = jax.nn.silu(depthwise_conv(qkv, conv_w))
    q, k, v = jnp.split(qkv, 3, axis=-1)
    q = l2norm(q.reshape(b, s, A_HEADS, A_DK)) * (A_DK ** -0.5)
    k = l2norm(k.reshape(b, s, A_HEADS, A_DK))
    v = v.reshape(b, s, A_HEADS, A_DV)
    beta = jax.nn.sigmoid(beta_raw.astype(F32)).reshape(b, s, 2, A_HEADS)
    alpha = alpha.astype(F32).reshape(b, s, 2, A_HEADS)
    log_g = -jnp.exp(a_log.astype(F32)) * jax.nn.softplus(alpha + dt_bias.astype(F32))
    o_f, s_f = gated_delta_chunked(q, k, v, log_g[:, :, 0], beta[:, :, 0], s0[:, 0])
    fl = lambda t: jnp.flip(t, axis=1)
    o_b, s_b = gated_delta_chunked(fl(q), fl(k), fl(v), fl(log_g[:, :, 1]), fl(beta[:, :, 1]), s0[:, 1])
    o = o_f + fl(o_b)
    o = (o * lax.rsqrt(jnp.mean(o * o, axis=-1, keepdims=True) + EPS) * norm_g.astype(F32)
         * jax.nn.silu(z.astype(F32).reshape(b, s, A_HEADS, A_DV)))
    return o.reshape(b, s, A_DIM).astype(qkv.dtype), jnp.stack([s_f, s_b], axis=1)

def conformer_conv(u, dw_w, dw_b, ln_g, ln_b):
    a, gt = jnp.split(u, 2, axis=-1)
    hh = a * jax.nn.sigmoid(gt)
    hh = depthwise_conv(hh, dw_w) + dw_b.astype(hh.dtype)
    return jax.nn.silu(layernorm(hh, ln_g, ln_b))

def fourier_mix(h):
    b, s, d = h.shape
    hg = h.astype(F32).reshape(b, s, C_GROUPS, d // C_GROUPS)
    f = jnp.fft.fft2(hg, axes=(1, 3), norm='ortho').real
    return f.reshape(b, s, d).astype(h.dtype)

def peer(h, wq, k1, k2, u_tab, v_tab):
    b, s, d = h.shape
    t = b * s
    x = h.reshape(t, d)
    q = (x @ wq).reshape(t, PEER_HEADS, 2, PEER_DK).astype(F32)
    s1 = jnp.einsum('thd,hnd->thn', q[:, :, 0], k1.astype(F32))
    s2 = jnp.einsum('thd,hnd->thn', q[:, :, 1], k2.astype(F32))
    v1, i1 = lax.top_k(s1, PEER_TOPK)
    v2, i2 = lax.top_k(s2, PEER_TOPK)
    cand = (v1[..., :, None] + v2[..., None, :]).reshape(t, PEER_HEADS, PEER_TOPK * PEER_TOPK)
    cidx = (i1[..., :, None] * PEER_KEYS + i2[..., None, :]).reshape(t, PEER_HEADS, PEER_TOPK * PEER_TOPK)
    sv, si = lax.top_k(cand, PEER_TOPK)
    eidx = jnp.take_along_axis(cidx, si, axis=-1)
    gates = jax.nn.softmax(sv, axis=-1).astype(h.dtype)
    nb = t // PEER_BLOCK

    def block(args):
        xb, eb, gb = args
        act = jax.nn.gelu(jnp.einsum('phkd,pd->phk', u_tab[eb], xb))
        return jnp.einsum('phk,phkd->pd', gb * act, v_tab[eb])

    out = lax.map(block, (x.reshape(nb, PEER_BLOCK, d),
                          eidx.reshape(nb, PEER_BLOCK, PEER_HEADS, PEER_TOPK),
                          gates.reshape(nb, PEER_BLOCK, PEER_HEADS, PEER_TOPK)))
    return out.reshape(b, s, d)

def trunk(x, cond, s0, prm):
    states = []
    for l in range(DEPTH):
        mod = (jax.nn.silu(cond) @ prm['ada_w'][l] + prm['ada_b'][l])[:, None, :]
        sh1, sc1, g1, sh2, sc2, g2 = jnp.split(mod, 6, axis=-1)
        h = rmsnorm(x, prm['norm1_g'][l]) * (1 + sc1) + sh1
        e = l // 2
        if l % 2 == 0:
            p = h @ prm['w_in_ab'][e]
            o4 = 4 * A_DIM
            o_a, st = delta_mixer(p[..., :3 * A_DIM], p[..., 3 * A_DIM:o4],
                                  p[..., o4:o4 + 2 * A_HEADS], p[..., o4 + 2 * A_HEADS:o4 + 4 * A_HEADS],
                                  prm['conv_qkv_w'][e], prm['a_log'][e], prm['dt_bias'][e],
                                  prm['delta_norm_g'][e], s0[:, e])
            o_b = conformer_conv(p[..., o4 + 4 * A_HEADS:], prm['conf_dw_w'][e], prm['conf_dw_b'][e],
                                 prm['conf_ln_g'][e], prm['conf_ln_b'][e])
            mix = jnp.concatenate([o_a, o_b], axis=-1) @ prm['w_out_ab'][e]
            states.append(st)
        else:
            mix = fourier_mix(h) @ prm['w_out_c'][e]
        x = x + g1 * mix
        h = rmsnorm(x, prm['norm2_g'][l]) * (1 + sc2) + sh2
        x = x + g2 * peer(h, prm['peer_wq'][l], prm['peer_k1'][l], prm['peer_k2'][l],
                          prm['peer_u'][l], prm['peer_v'][l])
    return rmsnorm(x, prm['final_norm_g']), jnp.stack(states, axis=1)

def setup_inputs(seed: int = 0) -> dict:
    key = jax.random.key(seed)
    ks = jax.random.split(key, 32)
    ne = (DEPTH + 1) // 2
    no = DEPTH // 2
    nrm = lambda i, shape, scale: jax.random.normal(ks[i], shape, F32) * scale
    dt = jnp.exp(jax.random.uniform(ks[12], (ne, 2, A_HEADS), F32, math.log(1e-3), math.log(0.1)))
    return {
        'x_prompt': nrm(0, (BATCH, SEQ, D_MODEL), 1.0),
        'x_sample': nrm(1, (DEC_BATCH, DEC_SEQ, D_MODEL), 1.0),
        'state_delta': nrm(2, (DEC_BATCH, ne, 2, A_HEADS, A_DK, A_DV), 0.1),
        'c': nrm(3, (DEC_BATCH, D_MODEL), 1.0),
        'c_ctx': nrm(4, (D_MODEL,), 1.0),
        'ada_w': nrm(5, (DEPTH, D_MODEL, 6 * D_MODEL), 0.5 * D_MODEL ** -0.5),
        'ada_b': nrm(6, (DEPTH, 6 * D_MODEL), 0.02),
        'norm1_g': 1.0 + nrm(7, (DEPTH, D_MODEL), 0.02),
        'norm2_g': 1.0 + nrm(8, (DEPTH, D_MODEL), 0.02),
        'w_in_ab': nrm(9, (ne, D_MODEL, P_AB), D_MODEL ** -0.5),
        'conv_qkv_w': nrm(10, (ne, SHORT_CONV, 3 * A_DIM), SHORT_CONV ** -0.5),
        'a_log': jnp.log(jax.random.uniform(ks[11], (ne, 2, A_HEADS), F32, 1.0, 16.0)),
        'dt_bias': dt + jnp.log(-jnp.expm1(-dt)),
        'delta_norm_g': 1.0 + nrm(13, (ne, A_DV), 0.02),
        'conf_dw_w': nrm(14, (ne, B_CONV, B_CH), B_CONV ** -0.5),
        'conf_dw_b': nrm(15, (ne, B_CH), 0.02),
        'conf_ln_g': 1.0 + nrm(16, (ne, B_CH), 0.02),
        'conf_ln_b': nrm(17, (ne, B_CH), 0.02),
        'w_out_ab': nrm(18, (ne, MIX_WIDTH, D_MODEL), MIX_WIDTH ** -0.5),
        'w_out_c': nrm(19, (no, D_MODEL, D_MODEL), D_MODEL ** -0.5),
        'peer_wq': nrm(20, (DEPTH, D_MODEL, PEER_HEADS * 2 * PEER_DK), D_MODEL ** -0.5),
        'peer_k1': nrm(21, (DEPTH, PEER_HEADS, PEER_KEYS, PEER_DK), PEER_DK ** -0.5),
        'peer_k2': nrm(22, (DEPTH, PEER_HEADS, PEER_KEYS, PEER_DK), PEER_DK ** -0.5),
        'peer_u': nrm(23, (DEPTH, PEER_N, D_MODEL), D_MODEL ** -0.5),
        'peer_v': nrm(24, (DEPTH, PEER_N, D_MODEL), 0.5),
        'final_norm_g': 1.0 + nrm(25, (D_MODEL,), 0.02),
    }

def reference(x_prompt, x_sample, state_delta, c, c_ctx, ada_w, ada_b, norm1_g, norm2_g,
              w_in_ab, conv_qkv_w, a_log, dt_bias, delta_norm_g, conf_dw_w, conf_dw_b,
              conf_ln_g, conf_ln_b, w_out_ab, w_out_c, peer_wq, peer_k1, peer_k2,
              peer_u, peer_v, final_norm_g):
    prm = {'ada_w': ada_w, 'ada_b': ada_b, 'norm1_g': norm1_g, 'norm2_g': norm2_g,
           'w_in_ab': w_in_ab, 'conv_qkv_w': conv_qkv_w, 'a_log': a_log, 'dt_bias': dt_bias,
           'delta_norm_g': delta_norm_g, 'conf_dw_w': conf_dw_w, 'conf_dw_b': conf_dw_b,
           'conf_ln_g': conf_ln_g, 'conf_ln_b': conf_ln_b, 'w_out_ab': w_out_ab,
           'w_out_c': w_out_c, 'peer_wq': peer_wq, 'peer_k1': peer_k1, 'peer_k2': peer_k2,
           'peer_u': peer_u, 'peer_v': peer_v, 'final_norm_g': final_norm_g}
    ne = (DEPTH + 1) // 2
    s0_ctx = jnp.zeros((x_prompt.shape[0], ne, 2, A_HEADS, A_DK, A_DV), x_prompt.dtype)
    y_prompt, ctx_states = trunk(x_prompt, c_ctx[None, :], s0_ctx, prm)
    new_state_delta = ctx_states.astype(x_prompt.dtype)
    xs = x_sample + grid_pos_emb(x_sample.shape[1]).astype(x_sample.dtype)[None]
    y_sample, _ = trunk(xs, c, state_delta, prm)
    return (y_prompt, y_sample, new_state_delta)


_drawn_inputs = setup_inputs


def setup_inputs(seed=0):
    import zlib

    import numpy as np

    out = dict(_drawn_inputs(seed))
    spreads = {}
    factors = {'state_delta': 5.589,
     'norm2_g': 19.276,
     'delta_norm_g': 75.809,
     'conf_dw_b': 5.543,
     'conf_ln_g': 74.504,
     'conf_ln_b': 75.687,
     'final_norm_g': 23.697}
    for name, (base, spread) in spreads.items():
        noise = np.random.default_rng([zlib.crc32(name.encode()), seed]).standard_normal(out[name].shape)
        drawn = base * np.exp(spread * noise) if base else spread * noise
        out[name] = jnp.asarray(drawn.astype(out[name].dtype))
    for name, factor in factors.items():
        out[name] = (out[name] * factor).astype(out[name].dtype)
    return out
```

```python
from contextlib import ExitStack

import numpy as np
import concourse.bass as bass
from concourse import mybir

F32 = mybir.dt.float32
F32R = mybir.dt.float32r
U32 = mybir.dt.uint32
ALU = mybir.AluOpType
ACT = mybir.ActivationFunctionType
AX = mybir.AxisListType

P = 128
D = 1024
NC = D // P
S_CTX, S_DEC = 128, 512
T = S_CTX + S_DEC
TILES = T // P
SEGS = ((0, S_CTX), (S_CTX, T))
DEPTH = 2
EPS = 1e-6
HEADS = 4
DK = 128
TAPS_A = 7
TAPS_B = 31
PAD_A = TAPS_A // 2
PAD_B = TAPS_B // 2
LEN_A = T + 3 * PAD_A
LEN_B = T + 3 * PAD_B
B_CH = D // 2
PEER_HEADS = 8
TOPK = 16
NSC = 2 * PEER_HEADS
GRID_W = 64
POS_BASE = 10000.0
LEVELS = 7
NEG = -3.0e38


class Sems:

    def __init__(self, nc, stage):
        self.nc, self.stage, self.taken = nc, stage, []

    def __call__(self, name):
        self.taken.append(self.nc.alloc_semaphore(f"{self.stage}_{name}"))
        return self.taken[-1]

    def close(self):
        self.nc.clear_and_free_semaphores(self.taken)
        self.nc.all_engine_barrier()


class Steps:

    def __init__(self, eng, sem):
        self.eng, self.sem, self.n = eng, sem, 0

    def done(self, ins):
        ins.then_inc(self.sem, 1)
        self.n += 1
        return self.n

    def wait(self, n=None):
        self.eng.wait_ge(self.sem, self.n if n is None else n)

    def link(self, ins):
        self.done(ins)
        self.wait()


def hold(eng, sem, value):
    eng.wait_ge(sem, value)
    eng.nop(nofuse=True)


def load_stage(nc, m, d):
    sm = Sems(nc, "load")
    loaded, added = sm("loaded"), sm("added")
    with nc.sbuf_tensor("pos", [P, NC, S_DEC], F32) as pos:
        with nc.Block() as block:
            @block.sync
            def _(sp):
                for dst, src in ((m["xT"], d["xT"]), (m["mats"], d["mats"]), (m["gains"], d["gains"]),
                                 (pos, d["pos"])):
                    sp.dma_start(dst[:], src).then_inc(loaded, 16)

            @block.vector
            def _(dve):
                dve.wait_ge(loaded, 64)
                for c in range(NC):
                    x = m["xT"][:, c, S_CTX:T]
                    nc.vector.tensor_tensor(x, x, pos[:, c, :], ALU.add).then_inc(added, 1)
                nc.vector.memset(m["ones"][:], 1.0).then_inc(added, 1)
                dve.wait_ge(added, NC + 1)
    sm.close()


def ada_stage(nc, m, d):
    sm = Sems(nc, "ada")
    HALF = 512
    NH = 6 * D // HALF
    slab_full = [sm(f"slab_full{j}") for j in range(2)]
    slab_used = [sm(f"slab_used{j}") for j in range(2)]
    cond_full, cond_ready, steps = sm("cond_full"), sm("cond_ready"), sm("steps")
    with nc.sbuf_tensor("slab", [P, 2, NC, HALF], F32) as slab, \
            nc.sbuf_tensor("cond", [P, NC, 2], F32) as cond, \
            nc.sbuf_tensor("condact", [P, NC, 2], F32) as condact, \
            nc.sbuf_tensor("adab", [P, DEPTH, 48], F32) as adab, \
            nc.psum_tensor("mod0", [P, 96], F32) as mod0, nc.psum_tensor("mod1", [P, 96], F32) as mod1:
        with nc.Block() as block:
            @block.sync
            def _(sp):
                sp.dma_start(cond[:], d["cond"]).then_inc(cond_full, 16)
                sp.dma_start(adab[:], d["adab"]).then_inc(cond_full, 16)
                for n in range(DEPTH * NH):
                    if n >= 2:
                        sp.wait_ge(slab_used[n % 2], n // 2)
                    sp.dma_start(slab[:, n % 2], d["ada_w"][n]).then_inc(slab_full[n % 2], 16)

            @block.scalar
            def _(act):
                act.wait_ge(cond_full, 32)
                nc.scalar.activation(condact[:], cond[:], ACT.Silu).then_inc(cond_ready, 1)

            @block.tensor
            def _(pe):
                pe.wait_ge(cond_ready, 1)
                for n in range(DEPTH * NH):
                    ps = (mod0, mod1)[n // NH]
                    pe.wait_ge(slab_full[n % 2], 16 * (n // 2 + 1))
                    for b in range(HALF // P):
                        col = 2 * ((n % NH) * (HALF // P) + b)
                        for c in range(NC):
                            mm = nc.tensor.matmul(ps[:, col:col + 2], slab[:, n % 2, c, b * P:(b + 1) * P],
                                                  condact[:, c, :], start=c == 0, stop=c == NC - 1)
                    mm.then_inc(slab_used[n % 2], 1)

            @block.vector
            def _(dve):
                st = Steps(dve, steps)
                for s in slab_used:
                    dve.wait_ge(s, DEPTH * NH // 2)
                for l, ps in enumerate((mod0, mod1)):
                    st.done(nc.vector.tensor_tensor(
                        m["mod"][:, l].rearrange("p a c k -> p (a c) k"), ps[:].rearrange("p (b k) -> p b k", k=2),
                        adab[:, l, :].unsqueeze(2).to_broadcast([P, 48, 2]), ALU.add))
                st.wait()
                for l in range(DEPTH):
                    for n in range(2):
                        st.done(nc.vector.scalar_tensor_tensor(
                            out=m["amul"][:, l, n], in0=m["mod"][:, l, 1 + 3 * n], scalar=1.0,
                            in1=m["gains"][:, 2 * l + n, :].unsqueeze(2).to_broadcast([P, NC, 2]),
                            op0=ALU.add, op1=ALU.mult))
                st.wait()
    sm.close()


def sum_of_squares(nc, pe, ones, sq, sq_ready, sq_used, psums, n):
    for c in range(n):
        pe.wait_ge(sq_ready, c + 1)
        for (a, b), ps in zip(SEGS, psums):
            mm = nc.tensor.matmul(ps[:, 0:b - a], ones[:], sq[:, c % 2, a:b], start=c == 0, stop=c == n - 1)
        mm.then_inc(sq_used, 1)


def norm_stage(nc, m, tag, mul, add, out):
    sm = Sems(nc, tag)
    sq_ready, sq_used, var_ready, std_ready, steps = (sm(x) for x in ("sq_ready", "sq_used", "var_ready", "std_ready", "steps"))
    h_ready, hi_ready, h_used = sm("h_ready"), sm("hi_ready"), sm("h_used")
    xT = m["xT"]
    final = not isinstance(out, tuple)
    with nc.sbuf_tensor(tag + "sq", [P, 2, T], F32) as sq, nc.sbuf_tensor(tag + "var", [P, T], F32) as var, \
            nc.sbuf_tensor(tag + "rstd", [P, T], F32) as rstd, nc.sbuf_tensor(tag + "xn", [P, 2, T], F32) as xn, \
            nc.sbuf_tensor(tag + "h", [P, 2, T], F32) as h, \
            nc.psum_tensor(tag + "ssA", [P, 128], F32) as ssA, nc.psum_tensor(tag + "ssB", [P, 512], F32) as ssB:
        with nc.Block() as block:
            @block.scalar
            def _(act):
                for c in range(NC):
                    if c >= 2:
                        act.wait_ge(sq_used, c - 1)
                    nc.scalar.activation(sq[:, c % 2, :], xT[:, c, :], ACT.Square).then_inc(sq_ready, 1)
                act.wait_ge(var_ready, 2)
                nc.scalar.activation(rstd[:], var[:], ACT.Sqrt).then_inc(std_ready, 1)
                if not final:
                    for c in range(NC):
                        act.wait_ge(h_ready, 2 * (c + 1))
                        nc.scalar.copy(out[0][:, c, :], h[:, c % 2, :]).then_inc(hi_ready, 1)

            @block.tensor
            def _(pe):
                sum_of_squares(nc, pe, m["ones"], sq, sq_ready, sq_used, (ssA, ssB), NC)

            @block.vector
            def _(dve):
                st = Steps(dve, steps)
                dve.wait_ge(sq_used, NC)
                for (a, b), ps in zip(SEGS, (ssA, ssB)):
                    nc.vector.tensor_scalar(var[:, a:b], ps[:, 0:b - a], 1.0 / D, EPS, ALU.mult, ALU.add).then_inc(var_ready, 1)
                dve.wait_ge(std_ready, 1)
                st.link(nc.vector.reciprocal(var[:], rstd[:]))
                for c in range(NC):
                    st.link(nc.vector.tensor_tensor(xn[:, c % 2, :], xT[:, c, :], var[:], ALU.mult))
                    if c >= 2:
                        dve.wait_ge(h_used, (16 if final else 1) * (c - 1))
                    for k, (a, b) in enumerate(SEGS):
                        nc.vector.tensor_scalar(h[:, c % 2, a:b], xn[:, c % 2, a:b], mul(c, k), add(c, k),
                                                ALU.mult, ALU.add if add(c, k) is not None else ALU.bypass).then_inc(h_ready, 1)

            if final:
                @block.sync
                def _(sp):
                    for c in range(NC):
                        sp.wait_ge(h_ready, 2 * (c + 1))
                        sp.dma_start(out[:, c, :], h[:, c % 2, :]).then_inc(h_used, 16)
                        sp.wait_ge(h_used, 16 * (c + 1))
            else:
                @block.gpsimd
                def _(pool):
                    for c in range(NC):
                        pool.wait_ge(hi_ready, c + 1)
                        nc.gpsimd.tensor_tensor(out[1][:, c, :], h[:, c % 2, :], out[0][:, c, :].bitcast(F32),
                                                ALU.subtract).then_inc(h_used, 1)
                    pool.wait_ge(h_used, NC)
    sm.close()


def credit(eng, sems, n=1):
    for s in sems:
        eng.sem_inc(s, n)


def run_ahead(eng, n_it, prepare, take):
    prepare(0, 0)
    with eng.Fori(0, n_it - 1) as i:
        prepare(i, 1)
        take(i, 0)
        prepare(i + 1, 0)
        take(i, 1)
    prepare(n_it - 1, 1)
    take(n_it - 1, 0)
    take(n_it - 1, 1)


def project_stage(nc, tag, w_dram, nb, hi, lo, on_act, evacuate, store=None):
    sm = Sems(nc, tag)
    raw_full, hi_done, split, mm_done, evac_done = (
        [sm(f"{x}{j}") for j in range(2)] for x in ("raw_full", "hi_done", "split", "mm_done", "evac_done"))
    stored = [sm(f"stored{j}") for j in range(2)] if store is not None else None
    n_it = nb // 2
    with nc.sbuf_tensor(tag + "raw", [P, 2, NC * P], F32) as raw, nc.sbuf_tensor(tag + "whi", [P, 2, NC * P], F32R) as whi, \
            nc.sbuf_tensor(tag + "wlo", [P, 2, NC * P], F32R) as wlo, \
            nc.psum_tensor(tag + "a0", [P, 128], F32) as a0, nc.psum_tensor(tag + "b0", [P, 512], F32) as b0, \
            nc.psum_tensor(tag + "a1", [P, 128], F32) as a1, nc.psum_tensor(tag + "b1", [P, 512], F32) as b1:
        psums = ((a0, b0), (a1, b1))

        def take(eng, i, j):
            eng.wait_ge(mm_done[j], i + 2)
            if store is not None:
                eng.wait_ge(stored[j], (i + 1) * 16)
            eng.nop(nofuse=True)
            evacuate(i * 2 + j, j, psums[j]).then_inc(evac_done[j], 1)
            if store is not None:
                hold(eng, evac_done[j], i + 2)
                buf, dram = store
                eng.dma_start(dram[bass.ds(i * 2 + j, 1)].rearrange("o p n -> p (o n)"), buf[:, j]).then_inc(stored[j], 16)

        with nc.Block() as block:
            @block.sync
            def _(sp):
                credit(sp, split + mm_done + evac_done)
                if store is not None:
                    credit(sp, stored, 16)
                with sp.Fori(0, n_it) as i:
                    for j in range(2):
                        hold(sp, split[j], i + 1)
                        sp.dma_start(raw[:, j], w_dram[bass.ds(i * 2 + j, 1)].rearrange("o p n -> p (o n)")).then_inc(raw_full[j], 16)

            @block.scalar
            def _(act):
                def split_hi(i, j):
                    act.wait_ge(raw_full[j], (i + 1) * 16)
                    act.wait_ge(mm_done[j], i + 1)
                    nc.scalar.copy(whi[:, j, :], raw[:, j, :]).then_inc(hi_done[j], 1)

                if on_act:
                    run_ahead(act, n_it, split_hi, lambda i, j: take(act, i, j))
                    for x in stored or ():
                        act.wait_ge(x, 16 * (n_it + 1))
                else:
                    with act.Fori(0, n_it) as i:
                        for j in range(2):
                            split_hi(i, j)

            @block.vector
            def _(dve):
                def split_lo(i, j):
                    dve.wait_ge(hi_done[j], i + 1)
                    nc.vector.tensor_tensor(wlo[:, j, :], raw[:, j, :], whi[:, j, :].bitcast(F32), ALU.subtract).then_inc(split[j], 1)

                if on_act:
                    with dve.Fori(0, n_it) as i:
                        for j in range(2):
                            split_lo(i, j)
                else:
                    run_ahead(dve, n_it, split_lo, lambda i, j: take(dve, i, j))

            @block.tensor
            def _(pe):
                with pe.Fori(0, n_it) as i:
                    for j in range(2):
                        pe.wait_ge(split[j], i + 2)
                        pe.wait_ge(evac_done[j], i + 1)
                        for (a, b), ps in zip(SEGS, psums[j]):
                            for c in range(NC):
                                w = slice(c * P, (c + 1) * P)
                                for n, (x, y) in enumerate(((whi, hi), (whi, lo), (wlo, hi))):
                                    mm = nc.tensor.matmul(ps[:, 0:b - a], x[:, j, w], y[:, c, a:b],
                                                          start=c == 0 and n == 0, stop=c == NC - 1 and n == 2)
                        mm.then_inc(mm_done[j], 1)
    sm.close()


def copy_out(nc, dst, first=0):
    def evacuate(n, j, psums):
        for (a, b), ps in zip(SEGS, psums):
            last = nc.scalar.copy(dst[:, bass.ds(n + first, 1), a:b].rearrange("p o t -> p (o t)"), ps[:, 0:b - a])
        return last
    return evacuate


def add_to_x(nc, m, gate):
    def evacuate(n, j, psums):
        for k, ((a, b), ps) in enumerate(zip(SEGS, psums)):
            x = m["xT"][:, bass.ds(n, 1), a:b].rearrange("p o t -> p (o t)")
            g = gate[:, bass.ds(n, 1), k:k + 1].rearrange("p o t -> p (o t)")
            last = nc.vector.scalar_tensor_tensor(out=x, in0=ps[:, 0:b - a], scalar=g, in1=x, op0=ALU.mult, op1=ALU.add)
        return last
    return evacuate


def score_stage(nc, m, tag, d, l, qT, tops):
    sm = Sems(nc, tag)
    keys_full, scored, s_taken, s_used, turned, t_taken, steps, exp_ready, exp_done, ready = (
        sm(x) for x in ("keys_full", "scored", "s_taken", "s_used", "turned", "t_taken", "steps", "exp_ready", "exp_done", "ready"))
    with ExitStack() as es:
        sb = lambda n, shape, dt=F32: es.enter_context(nc.sbuf_tensor(tag + n, shape, dt))
        keys = sb("keys", [P, NSC, P])
        sc = sb("sc", [P, NSC * P])
        sc2 = sb("sc2", [P, 2, 256])
        val = sb("val", [P, NSC, TOPK])
        idx = sb("idx", [P, NSC, TOPK], U32)
        idxf = sb("idxf", [P, NSC, TOPK])
        cand = sb("cand", [P, PEER_HEADS, TOPK * TOPK])
        eq = sb("eq", [P, PEER_HEADS * TOPK, TOPK])
        pick = sb("pick", [P, 2, PEER_HEADS * TOPK], U32)
        sv = sb("sv", [P, PEER_HEADS, TOPK])
        si = sb("si", [P, PEER_HEADS, TOPK], U32)
        picked = sb("picked", [P, 2, PEER_HEADS * TOPK])
        pickf = sb("pickf", [P, 2, PEER_HEADS * TOPK])
        ex = sb("ex", [P, PEER_HEADS, TOPK])
        den = sb("den", [P, PEER_HEADS])
        rden = sb("rden", [P, PEER_HEADS])
        gate = sb("gate", [P, PEER_HEADS, TOPK])
        ps = [es.enter_context(nc.psum_tensor(f"{tag}ps{k}", [P, 512], F32)) for k in range(4)]
        pt = es.enter_context(nc.psum_tensor(tag + "pt", [P, 3, P], F32))
        ident = m["mats"][:, IDENT, :]
        iota = m["mats"][:, IOTA, 0:TOPK]
        block = es.enter_context(nc.Block())

        @block.sync
        def _(sp):
            sp.dma_start(keys[:], d["keys"][l]).then_inc(keys_full, 16)

        @block.tensor
        def _(pe):
            pe.wait_ge(keys_full, 16)

            def score(t):
                if t:
                    pe.wait_ge(s_taken, 4 * t)
                for h in range(NSC):
                    mm = nc.tensor.matmul(ps[h // 4][:, (h % 4) * P:(h % 4 + 1) * P], qT[:, h, t * P:(t + 1) * P],
                                          keys[:, h, :], start=True, stop=True)
                mm.then_inc(scored, 1)

            score(0)
            for t in range(TILES):
                if t + 1 < TILES:
                    score(t + 1)
                pe.wait_ge(ready, t + 1)
                if t:
                    pe.wait_ge(t_taken, t)
                for w, src in enumerate((picked[:, 0, :], picked[:, 1, :], gate[:].rearrange("p h k -> p (h k)"))):
                    mm = nc.tensor.transpose(pt[:, w, :], src, ident)
                mm.then_inc(turned, 1)

        @block.scalar
        def _(act):
            for t in range(TILES):
                act.wait_ge(scored, t + 1)
                if t:
                    act.wait_ge(s_used, t)
                for k in range(4):
                    nc.scalar.copy(sc[:, k * 512:(k + 1) * 512], ps[k][:]).then_inc(s_taken, 1)
                act.wait_ge(exp_ready, t + 1)
                nc.scalar.activation(ex[:], ex[:], ACT.Exp).then_inc(exp_done, 1)
                act.wait_ge(turned, t + 1)
                nc.scalar.copy(tops[:, :, t * P:(t + 1) * P], pt[:]).then_inc(t_taken, 1)

        @block.vector
        def _(dve):
            st = Steps(dve, steps)
            v = nc.vector

            def top16(values, scratch, out_v, out_i):
                st.link(v.max(out_v[:, 0:8], values))
                st.done(v.max_index(out_i[:, 0:8], out_v[:, 0:8], values))
                st.link(v.match_replace(scratch, out_v[:, 0:8], values, NEG))
                st.link(v.max(out_v[:, 8:16], scratch))
                st.done(v.max_index(out_i[:, 8:16], out_v[:, 8:16], scratch))

            for t in range(TILES):
                dve.wait_ge(s_taken, 4 * (t + 1))
                for h in range(NSC):
                    top16(sc[:, h * P:(h + 1) * P], sc2[:, h % 2, 0:P], val[:, h], idx[:, h])
                st.wait()
                v.tensor_copy(idxf[:], idx[:]).then_inc(s_used, 1)
                dve.wait_ge(s_used, t + 1)
                v1 = val[:, 0:NSC:2, :].unsqueeze(3).to_broadcast([P, PEER_HEADS, TOPK, TOPK])
                v2 = val[:, 1:NSC:2, :].unsqueeze(2).to_broadcast([P, PEER_HEADS, TOPK, TOPK])
                st.link(v.tensor_tensor(cand[:].rearrange("p h (a b) -> p h a b", a=TOPK), v1, v2, ALU.add))
                for h in range(PEER_HEADS):
                    top16(cand[:, h, :], sc2[:, h % 2, :], sv[:, h], si[:, h])
                st.wait()
                v.tensor_tensor(ex[:], sv[:], sv[:, :, 0:1].to_broadcast([P, PEER_HEADS, TOPK]), ALU.subtract).then_inc(exp_ready, 1)
                flat = si[:].rearrange("p h k -> p (h k)")
                st.done(v.tensor_single_scalar(pick[:, 0, :], flat, 4, op=ALU.logical_shift_right))
                st.link(v.tensor_single_scalar(pick[:, 1, :], flat, TOPK - 1, op=ALU.bitwise_and))
                st.link(v.tensor_copy(pickf[:], pick[:]))
                for w in range(2):
                    one_hot = eq[:]
                    st.link(v.tensor_tensor(one_hot, pickf[:, w, :].unsqueeze(2).to_broadcast([P, P, TOPK]),
                                            iota.unsqueeze(1).to_broadcast([P, P, TOPK]), ALU.is_equal))
                    rows = idxf[:, w:NSC:2, :].unsqueeze(2).to_broadcast([P, PEER_HEADS, TOPK, TOPK])
                    st.link(v.tensor_tensor(one_hot.rearrange("p (h k) a -> p h k a", h=PEER_HEADS),
                                            one_hot.rearrange("p (h k) a -> p h k a", h=PEER_HEADS), rows, ALU.mult))
                    if t and w == 0:
                        dve.wait_ge(turned, t)
                    st.link(v.tensor_reduce(picked[:, w, :], one_hot, AX.X, ALU.add))
                dve.wait_ge(exp_done, t + 1)
                st.link(v.tensor_reduce(den[:], ex[:], AX.X, ALU.add))
                st.link(v.reciprocal(rden[:], den[:]))
                v.tensor_tensor(gate[:], ex[:], rden[:].unsqueeze(2).to_broadcast([P, PEER_HEADS, TOPK]), ALU.mult).then_inc(ready, 1)
                dve.wait_ge(ready, t + 1)
    sm.close()


QUAD = 4


def gates_stage(nc, m, tag, tops, g_dram):
    sm = Sems(nc, tag)
    NQ = P // QUAD
    one1, one2, made, taken = ([sm(f"{x}{j}") for j in range(2)] for x in ("one1", "one2", "made", "taken"))
    stored = [sm(f"stored{j}") for j in range(2)]
    with ExitStack() as es:
        sb = lambda n, shape, dt=F32: es.enter_context(nc.sbuf_tensor(tag + n, shape, dt))
        oh1 = sb("oh1", [P, 2, QUAD, P])
        oh2 = sb("oh2", [P, 2, QUAD, P])
        g = sb("g", [P, 2, P, P])
        ps = [es.enter_context(nc.psum_tensor(f"{tag}ps{k}", [P, QUAD, P], F32)) for k in range(2)]
        iota = m["mats"][:, IOTA, :]
        block = es.enter_context(nc.Block())

        @block.tensor
        def _(pe):
            credit(pe, made + taken)
            with pe.Fori(0, T // QUAD // 2) as i:
                for j in range(2):
                    pe.wait_ge(one1[j], i + 1)
                    pe.wait_ge(one2[j], i + 1)
                    pe.wait_ge(taken[j], i + 1)
                    for q in range(QUAD):
                        mm = nc.tensor.matmul(ps[j][:, q, :], oh1[:, j, q, :], oh2[:, j, q, :], start=True, stop=True)
                    mm.then_inc(made[j], 1)

        @block.vector
        def _(dve):
            with dve.Fori(0, T // QUAD // 2) as i:
                for j in range(2):
                    dve.wait_ge(made[j], i + 1)
                    dve.nop(nofuse=True)
                    nc.vector.tensor_tensor(oh1[:, j], iota.unsqueeze(1).to_broadcast([P, QUAD, P]),
                                            tops[:, 0, bass.ds((i * 2 + j) * QUAD, QUAD)].unsqueeze(2).to_broadcast([P, QUAD, P]),
                                            ALU.is_equal).then_inc(one1[j], 1)
                    for q in range(QUAD):
                        t = (i * 2 + j) * QUAD + q
                        last = nc.vector.tensor_scalar(oh2[:, j, q, :], iota, tops[:, 1, bass.ds(t, 1)],
                                                       tops[:, 2, bass.ds(t, 1)], ALU.is_equal, ALU.mult)
                    last.then_inc(one2[j], 1)

        @block.scalar
        def _(act):
            for t in range(TILES):
                if t >= 2:
                    act.wait_ge(stored[t % 2], 16 * (t // 2))
                with act.Fori(0, NQ // 2) as i:
                    for j in range(2):
                        hold(act, made[j], i + (t * NQ // 2 + 2))
                        dst = g[:, t % 2, :, bass.ds((i * 2 + j) * QUAD, QUAD)].rearrange("p i t -> p t i")
                        nc.scalar.copy(dst, ps[j][:]).then_inc(taken[j], 1)
                for j in range(2):
                    act.wait_ge(taken[j], (t + 1) * NQ // 2 + 1)
                act.dma_start(g_dram[:, :, t * P:(t + 1) * P].rearrange("i p t -> p i t"), g[:, t % 2]).then_inc(stored[t % 2], 16)
            for j in range(2):
                act.wait_ge(stored[j], 16 * ((TILES + 1 - j) // 2))
    sm.close()


def experts_out_stage(nc, m, tag, v_dram, g_dram, a_dram, gate):
    sm = Sems(nc, tag)
    GRP = 4
    N_IT = P // (2 * GRP)
    v_full, g_full, v_hi, v_split, w_ready, w_hi, w_split, evac_done = (
        [sm(f"{x}{j}") for j in range(2)]
        for x in ("v_full", "g_full", "v_hi", "v_split", "w_ready", "w_hi", "w_split", "evac_done"))
    chunk_done = [[sm(f"chunk_done{g}{j}") for j in range(2)] for g in range(2)]
    with ExitStack() as es:
        sb = lambda n, shape, dt=F32: es.enter_context(nc.sbuf_tensor(tag + n, shape, dt))
        raw = sb("raw", [P, 2, D])
        vhi = sb("vhi", [P, 2 * GRP, D], F32R)
        vlo = sb("vlo", [P, 2 * GRP, D], F32R)
        ga = sb("ga", [P, 2, 2, T])
        w = sb("w", [P, 2, T])
        whi = sb("whi", [P, 2 * GRP, T], F32R)
        wlo = sb("wlo", [P, 2 * GRP, T], F32R)
        psums = [[es.enter_context(nc.psum_tensor(f"{tag}ps{j}{k}", [P, b - a], F32)) for k, (a, b) in enumerate(SEGS)]
                 for j in range(2)]
        block = es.enter_context(nc.Block())

        @block.sync
        def _(sp):
            credit(sp, v_split + w_ready + w_split + evac_done + chunk_done[0] + chunk_done[1])
            with sp.Fori(0, N_IT) as i:
                for s in range(2 * GRP):
                    r, u = s % 2, i * GRP + s // 2
                    hold(sp, v_split[r], u + 1)
                    sp.dma_start(raw[:, r], v_dram[bass.ds(i * 2 * GRP + s, 1)].rearrange("o p n -> p (o n)")).then_inc(v_full[r], 16)
                    hold(sp, w_ready[r], u + 1)
                    for k, src in enumerate((g_dram, a_dram)):
                        sp.dma_start(ga[:, r, k], src[bass.ds(i * 2 * GRP + s, 1)].rearrange("o p n -> p (o n)")).then_inc(g_full[r], 16)

        @block.scalar
        def _(act):
            with act.Fori(0, N_IT) as i:
                for s in range(2 * GRP):
                    r, u = s % 2, i * GRP + s // 2
                    act.wait_ge(v_full[r], (u + 1) * 16)
                    act.wait_ge(chunk_done[s // GRP][1], i * (NC // 2) + 1)
                    nc.scalar.copy(vhi[:, s, :], raw[:, r, :]).then_inc(v_hi[r], 1)
                    act.wait_ge(w_ready[r], u + 2)
                    nc.scalar.copy(whi[:, s, :], w[:, r, :]).then_inc(w_hi[r], 1)

        @block.gpsimd
        def _(pool):
            with pool.Fori(0, N_IT) as i:
                for s in range(2 * GRP):
                    r, u = s % 2, i * GRP + s // 2
                    hold(pool, v_hi[r], u + 1)
                    nc.gpsimd.tensor_tensor(vlo[:, s, :], raw[:, r, :], vhi[:, s, :].bitcast(F32), ALU.subtract).then_inc(v_split[r], 1)

        @block.vector
        def _(dve):
            def prepare(i, s):
                r, u = s % 2, i * GRP + s // 2
                dve.wait_ge(g_full[r], (u + 1) * 32)
                dve.wait_ge(w_split[r], u + 1)
                nc.vector.tensor_tensor(w[:, r, :], ga[:, r, 0, :], ga[:, r, 1, :], ALU.mult).then_inc(w_ready[r], 1)
                dve.wait_ge(w_hi[r], u + 1)
                nc.vector.tensor_tensor(wlo[:, s, :], w[:, r, :], whi[:, s, :].bitcast(F32), ALU.subtract).then_inc(w_split[r], 1)

            def evacuate(i, grp, c):
                j, n = c % 2, (i * 2 + grp) * (NC // 2) + c // 2
                dve.wait_ge(chunk_done[grp][j], i * (NC // 2) + (c // 2 + 2))
                dve.wait_ge(evac_done[j], n + 1)
                for k, (a, b) in enumerate(SEGS):
                    x = m["xT"][:, c, a:b]
                    last = nc.vector.scalar_tensor_tensor(out=x, in0=psums[j][k][:], scalar=gate[:, c, k:k + 1], in1=x,
                                                          op0=ALU.mult, op1=ALU.add)
                last.then_inc(evac_done[j], 1)

            for s in range(GRP):
                prepare(0, s)
            with dve.Fori(0, N_IT - 1) as i:
                for grp in range(2):
                    for b in range(GRP):
                        evacuate(i, grp, 2 * b)
                        evacuate(i, grp, 2 * b + 1)
                        prepare(i + grp, (1 - grp) * GRP + b)
            i = N_IT - 1
            for grp in range(2):
                for b in range(GRP):
                    if grp == 0:
                        prepare(i, GRP + b)
                for c in range(NC):
                    evacuate(i, grp, c)
            for j in range(2):
                dve.wait_ge(evac_done[j], N_IT * NC + 1)

        @block.tensor
        def _(pe):
            with pe.Fori(0, N_IT) as i:
                for grp in range(2):
                    for r in range(2):
                        u = i * GRP + (grp + 1) * (GRP // 2)
                        pe.wait_ge(w_split[r], u + 1)
                        pe.wait_ge(v_split[r], u + 1)
                    for c in range(NC):
                        j = c % 2
                        pe.wait_ge(evac_done[j], (i * 2 + grp) * (NC // 2) + (c // 2 + 1))
                        for k, (a, b) in enumerate(SEGS):
                            for q in range(GRP):
                                s = grp * GRP + q
                                for n, (x, y) in enumerate(((vhi, whi), (vhi, wlo), (vlo, whi))):
                                    mm = nc.tensor.matmul(psums[j][k][:], x[:, s, c * P:(c + 1) * P], y[:, s, a:b],
                                                          start=q == 0 and n == 0, stop=q == GRP - 1 and n == 2)
                        mm.then_inc(chunk_done[grp][j], 1)
    sm.close()


IDENT, IOTA, INCL, NMATS = 0, 1, 2, 4
STRICT, LEVEL = 0, 2
NMASKS = LEVEL + 2 * LEVELS


def constants():
    r, c = np.arange(P)[:, None], np.arange(P)[None, :]
    mats = [r == c, np.broadcast_to(c, (P, P)), r <= c, r >= c, r < c, r > c]
    for level in range(LEVELS):
        s = 1 << level
        pair = r // (2 * s) == c // (2 * s)
        lower = pair & (r // s % 2 == 1) & (c // s % 2 == 0)
        mats += [lower, lower.T]
    mats = np.stack(mats, 1).astype(np.float32)
    return np.ascontiguousarray(mats[:, :NMATS]), np.ascontiguousarray(mats[:, NMATS:])


def col_a(t):
    return t if t < S_CTX else t + PAD_A


def decay_stage(nc, m, d, hi, lo, lg, beta, gcol):
    sm = Sems(nc, "decay")
    full, wsplit, made, steps, act_steps, summed = (sm(x) for x in ("full", "wsplit", "made", "steps", "act_steps", "summed"))
    with nc.sbuf_tensor("wab", [P, NC, 16], F32) as wab, nc.sbuf_tensor("wabhi", [P, NC, 16], F32R) as wabhi, \
            nc.sbuf_tensor("wablo", [P, NC, 16], F32R) as wablo, nc.sbuf_tensor("alog", [P, 2, 8], F32) as alog, \
            nc.sbuf_tensor("alpha", [P, TILES, 8], F32) as alpha, nc.sbuf_tensor("abuf", [P, 3, TILES, 8], F32) as abuf, \
            nc.psum_tensor("abps", [P, TILES, 16], F32) as abps, nc.psum_tensor("gps", [P, TILES, 8], F32) as gps:
        with nc.Block() as block:
            @block.sync
            def _(sp):
                sp.dma_start(wab[:], d["w_ab"]).then_inc(full, 16)
                sp.dma_start(alog[:], d["alog"]).then_inc(full, 16)

            @block.tensor
            def _(pe):
                pe.wait_ge(wsplit, 2)
                for t in range(TILES):
                    for c in range(NC):
                        for n, (x, y) in enumerate(((hi, wabhi), (hi, wablo), (lo, wabhi))):
                            mm = nc.tensor.matmul(abps[:, t, :], x[:, c, t * P:(t + 1) * P], y[:, c, :],
                                                  start=c == 0 and n == 0, stop=c == NC - 1 and n == 2)
                mm.then_inc(made, 1)
                pe.wait_ge(steps, 5)
                for dr in range(2):
                    for t in range(TILES):
                        mm = nc.tensor.matmul(gps[:, t, dr * 4:dr * 4 + 4], m["mats"][:, INCL + dr, :], lg[:, t, dr * 4:dr * 4 + 4],
                                              start=True, stop=True)
                mm.then_inc(summed, 1)

            @block.scalar
            def _(act):
                st = Steps(act, act_steps)
                act.wait_ge(full, 32)
                nc.scalar.copy(wabhi[:], wab[:]).then_inc(wsplit, 1)
                act.wait_ge(steps, 1)
                st.link(nc.scalar.activation(abuf[:, 0], alpha[:], ACT.Abs))
                st.link(nc.scalar.activation(abuf[:, 0], abuf[:, 0], ACT.Exp, scale=-1.0))
                st.done(nc.scalar.activation(abuf[:, 1], abuf[:, 0], ACT.Ln, bias=1.0))
                st.done(nc.scalar.activation(abuf[:, 2, 0, :], alog[:, 0, :], ACT.Exp))
                st.done(nc.scalar.activation(beta[:], abps[:, :, 8:16], ACT.Sigmoid))
                st.wait()

            @block.vector
            def _(dve):
                st = Steps(dve, steps)
                dve.wait_ge(wsplit, 1)
                nc.vector.tensor_tensor(wablo[:], wab[:], wabhi[:].bitcast(F32), ALU.subtract).then_inc(wsplit, 1)
                dve.wait_ge(made, 1)
                st.link(nc.vector.tensor_tensor(alpha[:], abps[:, :, 0:8], alog[:, 1:2, :].to_broadcast([P, TILES, 8]), ALU.add))
                dve.wait_ge(act_steps, 1)
                st.link(nc.vector.tensor_scalar(alpha[:], alpha[:], 0.0, None, ALU.max))
                dve.wait_ge(act_steps, 5)
                st.link(nc.vector.tensor_tensor(alpha[:], alpha[:], abuf[:, 1], ALU.add))
                st.link(nc.vector.tensor_tensor(alpha[:], alpha[:], abuf[:, 2, 0:1, :].to_broadcast([P, TILES, 8]), ALU.mult))
                st.link(nc.vector.tensor_scalar(lg[:], alpha[:], -1.0, None, ALU.mult))
                dve.wait_ge(summed, 1)
                st.link(nc.vector.tensor_copy(gcol[:], gps[:]))
    sm.close()


def short_conv_stage(nc, m, d, src, dst):
    sm = Sems(nc, "conv")
    NB = 3 * HEADS
    N = LEN_A - TAPS_A + 1
    padded, full, conv, sq_ready, sq_used, var_ready, std_ready, inv_ready, normed, silued = (
        sm(x) for x in ("padded", "full", "conv", "sq_ready", "sq_used", "var_ready", "std_ready", "inv_ready", "normed", "silued"))
    with nc.sbuf_tensor("convw", [P, NB, TAPS_A], F32) as w, nc.sbuf_tensor("csq", [P, 2, N], F32) as sq, \
            nc.sbuf_tensor("cvar", [P, 2, T], F32) as var, nc.sbuf_tensor("cstd", [P, 2, T], F32) as std, \
            nc.psum_tensor("cA", [P, 512], F32) as cA, nc.psum_tensor("cB", [P, 512], F32) as cB, \
            nc.psum_tensor("cC", [P, 512], F32) as cC, nc.psum_tensor("cD", [P, 512], F32) as cD:
        psums = ((cA, cB), (cC, cD))
        with nc.Block() as block:
            @block.sync
            def _(sp):
                sp.dma_start(w[:], d["conv_w"]).then_inc(full, 16)

            @block.vector
            def _(dve):
                zeros = ((0, PAD_A), (PAD_A + S_CTX, 2 * PAD_A + S_CTX), (LEN_A - PAD_A, LEN_A))
                for a, e in zeros:
                    nc.vector.memset(src[:, :, a:e], 0.0).then_inc(padded, 1)
                dve.wait_ge(padded, 3)
                dve.wait_ge(full, 16)
                for tap in range(TAPS_A):
                    for b in range(NB):
                        x, wt = src[:, b, tap:tap + N], w[:, b, tap:tap + 1]
                        if tap == 0:
                            ins = nc.vector.tensor_scalar(dst[:, b, :], x, wt, None, ALU.mult)
                        else:
                            dve.wait_ge(conv, (tap - 1) * NB + b + 1)
                            ins = nc.vector.scalar_tensor_tensor(out=dst[:, b, :], in0=x, scalar=wt, in1=dst[:, b, :],
                                                                 op0=ALU.mult, op1=ALU.add)
                        ins.then_inc(conv, 1)
                for b in range(2 * HEADS):
                    j = b % 2
                    dve.wait_ge(sq_used, b + 1)
                    f = float(DK) if b < HEADS else 1.0
                    if b >= 2:
                        dve.wait_ge(std_ready, b - 1)
                    for (a0, a1), ps in zip(SEGS, psums[j]):
                        nc.vector.tensor_scalar(var[:, j, a0:a1], ps[:, 0:a1 - a0], f, f * EPS, ALU.mult, ALU.add).then_inc(var_ready, 1)
                    dve.wait_ge(std_ready, b + 1)
                    nc.vector.reciprocal(var[:, j, :], std[:, j, :]).then_inc(inv_ready, 1)
                    dve.wait_ge(inv_ready, b + 1)
                    for a0, a1 in SEGS:
                        x = dst[:, b, col_a(a0):col_a(a0) + a1 - a0]
                        nc.vector.tensor_tensor(x, x, var[:, j, a0:a1], ALU.mult).then_inc(normed, 1)
                dve.wait_ge(normed, 4 * HEADS)

            def root(act, b):
                act.wait_ge(var_ready, 2 * (b + 1))
                if b >= 2:
                    act.wait_ge(inv_ready, b - 1)
                nc.scalar.activation(std[:, b % 2, :], var[:, b % 2, :], ACT.Sqrt).then_inc(std_ready, 1)

            @block.scalar
            def _(act):
                for b in range(NB):
                    act.wait_ge(conv, NB * (TAPS_A - 1) + b + 1)
                    nc.scalar.activation(dst[:, b, :], dst[:, b, :], ACT.Silu).then_inc(silued, 1)
                for b in range(2 * HEADS):
                    act.wait_ge(silued, b + 1)
                    if b >= 2:
                        act.wait_ge(sq_used, b - 1)
                    nc.scalar.activation(sq[:, b % 2, :], dst[:, b, :], ACT.Square).then_inc(sq_ready, 1)
                    if b >= 1:
                        root(act, b - 1)
                root(act, 2 * HEADS - 1)
                act.wait_ge(silued, NB)

            @block.tensor
            def _(pe):
                for b in range(2 * HEADS):
                    pe.wait_ge(sq_ready, b + 1)
                    if b >= 2:
                        pe.wait_ge(var_ready, 2 * (b - 1))
                    for (a0, a1), ps in zip(SEGS, psums[b % 2]):
                        mm = nc.tensor.matmul(ps[:, 0:a1 - a0], m["ones"][:], sq[:, b % 2, col_a(a0):col_a(a0) + a1 - a0],
                                              start=True, stop=True)
                    mm.then_inc(sq_used, 1)
    sm.close()


def conformer_stage(nc, m, d, conf, hi, lo, first):
    sm = Sems(nc, "conf")
    NB = B_CH // P
    N = LEN_B - TAPS_B + 1
    full, sig, conv, sq_ready, sq_used, steps, act_steps, sum_done, centred, var_done, scaled, split = (
        sm(x) for x in ("full", "sig", "conv", "sq_ready", "sq_used", "steps", "act_steps", "sum_done", "centred",
                        "var_done", "scaled", "split"))
    with nc.sbuf_tensor("hh", [P, NB, LEN_B], F32) as hh, nc.sbuf_tensor("acc", [P, NB, N], F32) as acc, \
            nc.sbuf_tensor("bw", [P, NB, TAPS_B + 3], F32) as w, nc.sbuf_tensor("bsq", [P, 2, N], F32) as sq, \
            nc.sbuf_tensor("bmean", [P, N], F32) as mean, nc.sbuf_tensor("brstd", [P, N], F32) as rstd, \
            nc.sbuf_tensor("bout", [P, NB, T], F32) as out, \
            nc.psum_tensor("bA", [P, 512], F32) as bA, nc.psum_tensor("bB", [P, 512], F32) as bB:
        cols = ((0, 0, S_CTX), (S_CTX + PAD_B, S_CTX, T))
        with nc.Block() as block:
            @block.sync
            def _(sp):
                sp.dma_start(w[:], d["conf_w"]).then_inc(full, 16)

            @block.scalar
            def _(act):
                st = Steps(act, act_steps)
                for b in range(NB):
                    nc.scalar.activation(conf[:, NB + b, :], conf[:, NB + b, :], ACT.Sigmoid).then_inc(sig, 1)
                act.wait_ge(centred, NB)
                for b in range(NB):
                    if b >= 2:
                        act.wait_ge(sq_used, b - 1)
                    nc.scalar.activation(sq[:, b % 2, :], acc[:, b, :], ACT.Square).then_inc(sq_ready, 1)
                act.wait_ge(var_done, 2)
                st.link(nc.scalar.activation(mean[:], rstd[:], ACT.Sqrt))
                act.wait_ge(scaled, NB)
                for b in range(NB):
                    for c0, a, e in cols:
                        st.done(nc.scalar.activation(out[:, b, a:e], acc[:, b, c0:c0 + e - a], ACT.Silu))
                st.wait()
                for b in range(NB):
                    nc.scalar.copy(hi[:, first + b, :], out[:, b, :]).then_inc(split, 1)
                act.wait_ge(split, NB)

            @block.tensor
            def _(pe):
                for c0, a, e in cols:
                    ps = bA if a == 0 else bB
                    pe.wait_ge(conv, NB * (TAPS_B + 2) + 4)
                    for b in range(NB):
                        mm = nc.tensor.matmul(ps[:, 0:e - a], m["ones"][:], acc[:, b, c0:c0 + e - a], start=b == 0, stop=b == NB - 1)
                mm.then_inc(sum_done, 1)
                for b in range(NB):
                    pe.wait_ge(sq_ready, b + 1)
                    for c0, a, e in cols:
                        mm = nc.tensor.matmul((bA if a == 0 else bB)[:, 0:e - a], m["ones"][:], sq[:, b % 2, c0:c0 + e - a],
                                              start=b == 0, stop=b == NB - 1)
                    mm.then_inc(sq_used, 1)

            @block.vector
            def _(dve):
                st = Steps(dve, steps)
                v = nc.vector
                zeros = ((0, PAD_B), (PAD_B + S_CTX, 2 * PAD_B + S_CTX), (LEN_B - PAD_B, LEN_B))
                for a, e in zeros:
                    v.memset(hh[:, :, a:e], 0.0).then_inc(conv, 1)
                v.memset(rstd[:], 1.0).then_inc(conv, 1)
                dve.wait_ge(sig, NB)
                for b in range(NB):
                    for k, (a, e) in enumerate(SEGS):
                        c0 = a + PAD_B * (k + 1)
                        v.tensor_tensor(hh[:, b, c0:c0 + e - a], conf[:, b, a:e], conf[:, NB + b, a:e], ALU.mult).then_inc(conv, 1)
                dve.wait_ge(full, 16)
                base = 4 + 2 * NB
                dve.wait_ge(conv, base)
                for tap in range(TAPS_B):
                    for b in range(NB):
                        x, wt = hh[:, b, tap:tap + N], w[:, b, tap:tap + 1]
                        if tap == 0:
                            ins = v.tensor_scalar(acc[:, b, :], x, wt, w[:, b, TAPS_B:TAPS_B + 1], ALU.mult, ALU.add)
                        else:
                            dve.wait_ge(conv, base + (tap - 1) * NB + b + 1)
                            ins = v.scalar_tensor_tensor(out=acc[:, b, :], in0=x, scalar=wt, in1=acc[:, b, :], op0=ALU.mult, op1=ALU.add)
                        ins.then_inc(conv, 1)
                dve.wait_ge(conv, base + TAPS_B * NB)
                dve.wait_ge(sum_done, 1)
                for c0, a, e in cols:
                    st.done(v.tensor_scalar(mean[:, c0:c0 + e - a], (bA if a == 0 else bB)[:, 0:e - a], 1.0 / B_CH, None, ALU.mult))
                st.done(v.memset(mean[:, S_CTX:S_CTX + PAD_B], 0.0))
                st.wait()
                for b in range(NB):
                    v.tensor_tensor(acc[:, b, :], acc[:, b, :], mean[:], ALU.subtract).then_inc(centred, 1)
                dve.wait_ge(centred, NB)
                dve.wait_ge(sq_used, NB)
                for c0, a, e in cols:
                    v.tensor_scalar(rstd[:, c0:c0 + e - a], (bA if a == 0 else bB)[:, 0:e - a], 1.0 / B_CH, EPS,
                                    ALU.mult, ALU.add).then_inc(var_done, 1)
                dve.wait_ge(act_steps, 1)
                st.link(v.reciprocal(rstd[:], mean[:]))
                for b in range(NB):
                    st.done(v.tensor_tensor(acc[:, b, :], acc[:, b, :], rstd[:], ALU.mult))
                st.wait()
                for b in range(NB):
                    v.tensor_scalar(acc[:, b, :], acc[:, b, :], w[:, b, TAPS_B + 1:TAPS_B + 2], w[:, b, TAPS_B + 2:TAPS_B + 3],
                                    ALU.mult, ALU.add).then_inc(scaled, 1)
                for b in range(NB):
                    dve.wait_ge(split, b + 1)
                    st.done(v.tensor_tensor(lo[:, first + b, :], out[:, b, :], hi[:, first + b, :].bitcast(F32), ALU.subtract))
                st.wait()
    sm.close()


def tokens_stage(nc, m, qkv, tok):
    sm = Sems(nc, "tok")
    made, taken = ([sm(f"{x}{j}") for j in range(2)] for x in ("made", "taken"))
    with nc.psum_tensor("tA", [P, HEADS, P], F32) as tA, nc.psum_tensor("tB", [P, HEADS, P], F32) as tB:
        work = [(w, t) for w in range(2) for t in range(TILES)]
        with nc.Block() as block:
            @block.tensor
            def _(pe):
                for n, (w, t) in enumerate(work):
                    if n >= 2:
                        pe.wait_ge(taken[n % 2], n // 2)
                    c0 = col_a(t * P)
                    for h in range(HEADS):
                        mm = nc.tensor.transpose((tA, tB)[n % 2][:, h, :], qkv[:, (w + 1) * HEADS + h, c0:c0 + P], m["mats"][:, IDENT, :])
                    mm.then_inc(made[n % 2], 1)

            @block.scalar
            def _(act):
                for n, (w, t) in enumerate(work):
                    act.wait_ge(made[n % 2], n // 2 + 1)
                    nc.scalar.copy(tok[:, w, t], (tA, tB)[n % 2][:]).then_inc(taken[n % 2], 1)
                for j in range(2):
                    act.wait_ge(taken[j], len(work) // 2)
    sm.close()


def delta_stage(nc, m, d, qkv, tok, lg, beta, gcol, o_acc, state_out):
    sm = Sems(nc, "delta")
    names = ("full", "zeroed", "wide", "gsum", "prod", "diff", "gcopy", "exped", "decayed", "nmat", "ptmat", "scaled",
             "staged", "qt_mm", "qt", "xz_mm", "xz", "w_mm", "wneg", "u_mm", "u", "o_mm", "o_add", "s_mm", "s_new", "st_out", "small")
    full, zeroed, wide, gsum, prod, diff, gcopy, exped, decayed, nmat, ptmat, scaled, staged, qt_mm, qt_done, xz_mm, xz, w_mm, \
        wneg_done, u_mm, u_done, o_mm, o_add, s_mm, s_new, st_out, small = (sm(x) for x in names)
    masked_in = sm("masked_in")
    DH = 2 * HEADS
    with ExitStack() as es:
        sb = lambda n, shape, dt=F32: es.enter_context(nc.sbuf_tensor("dl_" + n, shape, dt))
        lgb, betab = sb("lgb", [P, DH, P]), sb("betab", [P, DH, P])
        egbc, dt_, nm, pt = sb("egbc", [P, DH, P]), sb("dt", [P, DH, P]), sb("nm", [P, DH, P]), sb("pt", [P, DH, P])
        X, Z, Qt = sb("X", [P, DH, P]), sb("Z", [P, DH, P]), sb("Qt", [P, DH, P])
        kb, vb, kdec, qdec = sb("kb", [P, DH, P]), sb("vb", [P, DH, P]), sb("kdec", [P, DH, P]), sb("qdec", [P, DH, P])
        wneg, u = lgb, betab
        states = (sb("sctx", [P, DH, P]), sb("sdec", [P, DH, P]))
        gl, kd, eg, egl, beg = (sb(n, [P, DH]) for n in ("gl", "kd", "eg", "egl", "beg"))
        masks = sb("masks", [P, NMASKS, P])
        banks = [es.enter_context(nc.psum_tensor(f"dl_ps{k}", [P, DH, P], F32)) for k in range(4)]
        gbc, bbc, kk, kq = banks
        ident = m["mats"][:, IDENT, :]
        mats = m["mats"]
        block = es.enter_context(nc.Block())
        units = [((t, TILES - t) if t else (0, 0), 1 if t else 0) for t in range(TILES)]
        heads = lambda dr: slice(dr * HEADS, (dr + 1) * HEADS)
        cols = lambda t: slice(col_a(t * P), col_a(t * P) + P)

        @block.sync
        def _(sp):
            sp.dma_start(masks[:], d["masks"]).then_inc(masked_in, 16)
            sp.dma_start(states[1][:], d["state"]).then_inc(full, 16)
            sp.wait_ge(s_new, DH)
            sp.dma_start(state_out.rearrange("k d v -> d k v"), states[0][:]).then_inc(st_out, 16)
            sp.wait_ge(st_out, 16)

        @block.tensor
        def _(pe):
            for n, (tiles, k) in enumerate(units):
                S = states[k]
                pe.wait_ge(wide, 4 * (n + 1))
                if n:
                    pe.wait_ge(o_add, 2 * n)
                    pe.wait_ge(s_new, DH * n)
                    pe.wait_ge(u_done, 2 * n)
                for dh in range(DH):
                    nc.tensor.matmul(gbc[:, dh, :], lgb[:, dh, :], mats[:, INCL + dh // HEADS, :], start=True, stop=True)
                    mm = nc.tensor.matmul(bbc[:, dh, :], betab[:, dh, :], ident, start=True, stop=True)
                mm.then_inc(gsum, 1)
                for dh in range(DH):
                    h, t = dh % HEADS, tiles[dh // HEADS]
                    kT = qkv[:, HEADS + h, cols(t)]
                    nc.tensor.matmul(kk[:, dh, :], kT, kT, start=True, stop=True)
                    mm = nc.tensor.matmul(kq[:, dh, :], kT, qkv[:, h, cols(t)], start=True, stop=True)
                mm.then_inc(prod, 1)
                for level in range(LEVELS):
                    a = n * LEVELS + level
                    pe.wait_ge(nmat, 4 * (n + 1))
                    pe.wait_ge(xz, 2 * (a + 1) + 2 * n)
                    for dh in range(DH):
                        mm = nc.tensor.matmul(gbc[:, dh, :], nm[:, dh, :], Z[:, dh, :], start=True, stop=True)
                    mm.then_inc(qt_mm, 1)
                    pe.wait_ge(qt_done, a + 1)
                    for dh in range(DH):
                        nc.tensor.matmul(bbc[:, dh, :], Qt[:, dh, :], X[:, dh, :], start=True, stop=True)
                        mm = nc.tensor.matmul(kk[:, dh, :], X[:, dh, :], Qt[:, dh, :], start=True, stop=True)
                    mm.then_inc(xz_mm, 1)
                pe.wait_ge(xz, 2 * (n + 1) * (LEVELS + 1))
                pe.wait_ge(scaled, 8 * (n + 1))
                pe.wait_ge(ptmat, n + 1)
                for dh in range(DH):
                    mm = nc.tensor.matmul(kq[:, dh, :], kb[:, dh, :], X[:, dh, :], start=True, stop=True)
                mm.then_inc(w_mm, 1)
                pe.wait_ge(wneg_done, n + 1)
                if n == 0:
                    pe.wait_ge(zeroed, 1)
                if n == 1:
                    pe.wait_ge(full, 16)
                for dh in range(DH):
                    nc.tensor.matmul(gbc[:, dh, :], X[:, dh, :], vb[:, dh, :], start=True, stop=False)
                    mm = nc.tensor.matmul(gbc[:, dh, :], wneg[:, dh, :], S[:, dh, :], start=False, stop=True)
                mm.then_inc(u_mm, 1)
                pe.wait_ge(u_done, 2 * (n + 1))
                for dh in range(DH):
                    nc.tensor.matmul(bbc[:, dh, :], S[:, dh, :], qdec[:, dh, :], start=True, stop=False)
                    mm = nc.tensor.matmul(bbc[:, dh, :], u[:, dh, :], pt[:, dh, :], start=False, stop=True)
                mm.then_inc(o_mm, 1)
                for dh in range(DH):
                    mm = nc.tensor.matmul(kk[:, dh, :], kdec[:, dh, :], u[:, dh, :], start=True, stop=True)
                mm.then_inc(s_mm, 1)

        @block.scalar
        def _(act):
            for n in range(TILES):
                act.wait_ge(gsum, n + 1)
                if n:
                    act.wait_ge(o_mm, n)
                act.wait_ge(decayed, 5 * n + 2)
                nc.scalar.activation(egbc[:], gbc[:], ACT.Exp).then_inc(exped, 1)
                act.wait_ge(gcopy, 3 * (n + 1))
                for x in (kd, eg, egl):
                    nc.scalar.activation(x[:], x[:], ACT.Exp).then_inc(exped, 1)
                act.wait_ge(diff, DH * (n + 1))
                nc.scalar.activation(dt_[:], dt_[:], ACT.Exp).then_inc(exped, 1)
                act.wait_ge(w_mm, n + 1)
                nc.scalar.mul(wneg[:], kq[:], -1.0).then_inc(wneg_done, 1)
                act.wait_ge(u_mm, n + 1)
                for dr in range(2):
                    nc.scalar.copy(u[:, heads(dr), :], gbc[:, heads(dr), :]).then_inc(u_done, 1)

        @block.gpsimd
        def _(pool):
            for n, (tiles, _) in enumerate(units):
                pool.wait_ge(small, n + 1)
                if n:
                    pool.wait_ge(s_mm, n)
                for dr in range(2):
                    t, hs = tiles[dr], heads(dr)
                    per = lambda x: x.unsqueeze(2).to_broadcast([P, HEADS, P])
                    nc.gpsimd.tensor_tensor(kb[:, hs, :], tok[:, 0, t], per(beg[:, hs]), ALU.mult).then_inc(scaled, 1)
                    nc.gpsimd.tensor_tensor(vb[:, hs, :], tok[:, 1, t], per(beta[:, t, hs]), ALU.mult).then_inc(scaled, 1)
                    nc.gpsimd.tensor_tensor(kdec[:, hs, :], tok[:, 0, t], per(kd[:, hs]), ALU.mult).then_inc(scaled, 1)
                    nc.gpsimd.tensor_tensor(qdec[:, hs, :], qkv[:, 0:HEADS, cols(t)], egbc[:, hs, :], ALU.mult).then_inc(scaled, 1)

        @block.vector
        def _(dve):
            v = nc.vector
            v.memset(states[0][:], 0.0).then_inc(zeroed, 1)
            v.memset(o_acc[:], 0.0).then_inc(zeroed, 1)
            dve.wait_ge(zeroed, 2)
            dve.wait_ge(masked_in, 16)
            for n, (tiles, k) in enumerate(units):
                S = states[k]
                for dr in range(2):
                    t, hs = tiles[dr], heads(dr)
                    for dst, src in ((lgb, lg), (betab, beta)):
                        v.tensor_copy(dst[:, hs, :], src[:, t, hs].unsqueeze(2).to_broadcast([P, HEADS, P])).then_inc(wide, 1)
                for x in (X, Z):
                    v.tensor_copy(x[:], ident.unsqueeze(1).to_broadcast([P, DH, P])).then_inc(xz, 1)
                dve.wait_ge(gsum, n + 1)
                for dh in range(DH):
                    t = tiles[dh // HEADS]
                    v.tensor_scalar(dt_[:, dh, :], gbc[:, dh, :], gcol[:, t, dh:dh + 1], 0.0, ALU.subtract, ALU.min).then_inc(diff, 1)
                v.tensor_copy(gl[:, 0:HEADS], gbc[:, 0:HEADS, P - 1]).then_inc(decayed, 1)
                v.tensor_copy(gl[:, HEADS:DH], gbc[:, HEADS:DH, 0]).then_inc(decayed, 1)
                for dr in range(2):
                    v.tensor_copy(eg[:, heads(dr)], gcol[:, tiles[dr], heads(dr)]).then_inc(decayed, 1)
                dve.wait_ge(decayed, 5 * n + 4)
                if n:
                    dve.wait_ge(scaled, 8 * n)
                v.tensor_tensor(kd[:], gl[:], eg[:], ALU.subtract).then_inc(gcopy, 1)
                v.tensor_copy(egl[:], gl[:]).then_inc(gcopy, 2)
                dve.wait_ge(exped, 5 * (n + 1))
                for dr in range(2):
                    v.tensor_tensor(beg[:, heads(dr)], eg[:, heads(dr)], beta[:, tiles[dr], heads(dr)], ALU.mult).then_inc(
                        *((small, 1) if dr else (decayed, 1)))
                masked = dt_[:].rearrange("p (r h) t -> p r h t", r=2)
                both = lambda a, mats=masks: mats[:, a:a + 2, :].unsqueeze(2).to_broadcast([P, 2, HEADS, P])
                v.tensor_tensor(masked, masked, both(INCL, m["mats"]), ALU.mult).then_inc(nmat, 1)
                dve.wait_ge(nmat, 4 * n + 1)
                dve.wait_ge(prod, n + 1)
                v.tensor_tensor(pt[:], dt_[:], kq[:], ALU.mult).then_inc(ptmat, 1)
                dve.wait_ge(ptmat, n + 1)
                v.tensor_tensor(dt_[:], dt_[:], kk[:], ALU.mult).then_inc(nmat, 1)
                dve.wait_ge(nmat, 4 * n + 2)
                v.tensor_tensor(masked, masked, both(STRICT), ALU.mult).then_inc(nmat, 1)
                dve.wait_ge(nmat, 4 * n + 3)
                v.tensor_tensor(nm[:], dt_[:], bbc[:], ALU.mult).then_inc(nmat, 1)
                for level in range(LEVELS):
                    a = n * LEVELS + level
                    dve.wait_ge(qt_mm, a + 1)
                    v.tensor_tensor(Qt[:].rearrange("p (r h) t -> p r h t", r=2), gbc[:].rearrange("p (r h) t -> p r h t", r=2),
                                    both(LEVEL + 2 * level), ALU.mult).then_inc(qt_done, 1)
                    dve.wait_ge(xz_mm, a + 1)
                    v.tensor_tensor(X[:], X[:], bbc[:], ALU.subtract).then_inc(xz, 1)
                    v.tensor_tensor(Z[:], Z[:], kk[:], ALU.subtract).then_inc(xz, 1)
                dve.wait_ge(o_mm, n + 1)
                for dr in range(2):
                    if n == 0 and dr:
                        dve.wait_ge(o_add, 1)
                    o = o_acc[:, :, tiles[dr] * P:(tiles[dr] + 1) * P]
                    v.tensor_tensor(o, o, bbc[:, heads(dr), :], ALU.add).then_inc(o_add, 1)
                if n == 1:
                    dve.wait_ge(full, 16)
                dve.wait_ge(s_mm, n + 1)
                for dh in range(DH):
                    v.scalar_tensor_tensor(out=S[:, dh, :], in0=S[:, dh, :], scalar=egl[:, dh:dh + 1], in1=kk[:, dh, :],
                                           op0=ALU.mult, op1=ALU.add).then_inc(s_new, 1)
                dve.wait_ge(s_new, DH * (n + 1))
                dve.wait_ge(o_add, 2 * (n + 1))
    sm.close()


def gated_norm_stage(nc, m, o_acc, z, hi, lo):
    sm = Sems(nc, "onorm")
    sq_ready, made, var_ready, std_ready, steps, out_ready, hi_ready, root_used = (
        sm(x) for x in ("sq_ready", "made", "var_ready", "std_ready", "steps", "out_ready", "hi_ready", "root_used"))
    with nc.sbuf_tensor("osq", [P, HEADS, T], F32) as sq, nc.sbuf_tensor("ovar", [P, HEADS, T], F32) as var, \
            nc.psum_tensor("oA", [P, 512], F32) as oA, nc.psum_tensor("oB", [P, 512], F32) as oB:
        with nc.Block() as block:
            @block.scalar
            def _(act):
                for h in range(HEADS):
                    nc.scalar.activation(sq[:, h, :], o_acc[:, h, :], ACT.Square).then_inc(sq_ready, 1)
                act.wait_ge(var_ready, 2 * HEADS)
                nc.scalar.activation(sq[:], var[:], ACT.Sqrt).then_inc(std_ready, 1)
                for h in range(HEADS):
                    act.wait_ge(out_ready, h + 1)
                    nc.scalar.copy(hi[:, h, :], o_acc[:, h, :]).then_inc(hi_ready, 1)

            @block.tensor
            def _(pe):
                for h in range(HEADS):
                    pe.wait_ge(sq_ready, h + 1)
                    if h:
                        pe.wait_ge(var_ready, 2 * h)
                    for (a, b), ps in zip(SEGS, (oA, oB)):
                        mm = nc.tensor.matmul(ps[:, 0:b - a], m["ones"][:], sq[:, h, a:b], start=True, stop=True)
                    mm.then_inc(made, 1)

            @block.vector
            def _(dve):
                st = Steps(dve, steps)
                v = nc.vector
                for h in range(HEADS):
                    dve.wait_ge(made, h + 1)
                    for (a, b), ps in zip(SEGS, (oA, oB)):
                        v.tensor_scalar(var[:, h, a:b], ps[:, 0:b - a], 1.0 / DK, EPS, ALU.mult, ALU.add).then_inc(var_ready, 1)
                dve.wait_ge(std_ready, 1)
                st.link(v.reciprocal(var[:], sq[:]))
                st.link(v.scalar_tensor_tensor(out=o_acc[:], in0=o_acc[:], scalar=m["gains"][:, NORM_A, 0:1], in1=var[:],
                                               op0=ALU.mult, op1=ALU.mult))
                for h in range(HEADS):
                    v.tensor_tensor(o_acc[:, h, :], o_acc[:, h, :], z[:, h, :], ALU.mult).then_inc(out_ready, 1)
                for h in range(HEADS):
                    dve.wait_ge(hi_ready, h + 1)
                    st.done(v.tensor_tensor(lo[:, h, :], o_acc[:, h, :], hi[:, h, :].bitcast(F32), ALU.subtract))
                st.wait()
    sm.close()


def fourier_stage(nc, m, d, hi, lo, out_hi, out_lo):
    sm = Sems(nc, "dft")
    full, dhi, dlo, one_mm, one_hi, one_lo, two_mm, two_hi, two_lo, two_out = (
        sm(x) for x in ("full", "dhi", "dlo", "one_mm", "one_hi", "one_lo", "two_mm", "two_hi", "two_lo", "two_out"))
    NCHAN, NCTX, NSEQ = 2 * P, 2 * P, 8 * S_DEC
    NALL = NCHAN + NCTX + NSEQ
    with ExitStack() as es:
        sb = lambda n, shape, dt=F32: es.enter_context(nc.sbuf_tensor("ft_" + n, shape, dt))
        dft, dfthi, dftlo = sb("dft", [P, NALL]), sb("dfthi", [P, NALL], F32R), sb("dftlo", [P, NALL], F32R)
        f1, f1hi, f1lo = sb("f1", [P, TILES, NCHAN]), sb("f1hi", [P, TILES, NCHAN], F32R), sb("f1lo", [P, TILES, NCHAN], F32R)
        f2 = sb("f2", [P, T])
        ps1 = [es.enter_context(nc.psum_tensor(f"ft_a{k}", [P, 2, NCHAN], F32)) for k in range(3)]
        psA = es.enter_context(nc.psum_tensor("ft_pa", [P, 128], F32))
        psB = es.enter_context(nc.psum_tensor("ft_pb", [P, 512], F32))
        block = es.enter_context(nc.Block())
        triple = lambda a, al, b, bl: ((a, b), (a, bl), (al, b))

        @block.sync
        def _(sp):
            sp.dma_start(dft[:], d["dft"]).then_inc(full, 16)

        @block.scalar
        def _(act):
            act.wait_ge(full, 16)
            nc.scalar.copy(dfthi[:], dft[:]).then_inc(dhi, 1)
            for g in range(NC):
                act.wait_ge(one_mm, g + 1)
                if g:
                    act.wait_ge(one_lo, g)
                for t in range(TILES):
                    nc.scalar.copy(f1[:, t, :], ps1[t // 2][:, t % 2, :]).then_inc(one_hi, 1)
                act.wait_ge(one_hi, 6 * g + 5)
                if g:
                    act.wait_ge(two_mm, g)
                nc.scalar.copy(f1hi[:], f1[:]).then_inc(one_hi, 1)
                act.wait_ge(two_mm, g + 1)
                if g:
                    act.wait_ge(two_lo, g)
                for (a, b), ps in zip(SEGS, (psA, psB)):
                    nc.scalar.copy(f2[:, a:b], ps[:, 0:b - a]).then_inc(two_out, 1)
                act.wait_ge(two_out, 2 * (g + 1))
                nc.scalar.copy(out_hi[:, g, :], f2[:]).then_inc(two_hi, 1)

        @block.vector
        def _(dve):
            dve.wait_ge(dhi, 1)
            nc.vector.tensor_tensor(dftlo[:], dft[:], dfthi[:].bitcast(F32), ALU.subtract).then_inc(dlo, 1)
            for g in range(NC):
                dve.wait_ge(one_hi, 6 * (g + 1))
                nc.vector.tensor_tensor(f1lo[:], f1[:], f1hi[:].bitcast(F32), ALU.subtract).then_inc(one_lo, 1)
                dve.wait_ge(two_hi, g + 1)
                nc.vector.tensor_tensor(out_lo[:, g, :], f2[:], out_hi[:, g, :].bitcast(F32), ALU.subtract).then_inc(two_lo, 1)
            dve.wait_ge(two_lo, NC)

        @block.tensor
        def _(pe):
            pe.wait_ge(dlo, 1)
            def channels(g):
                if g:
                    pe.wait_ge(one_hi, 6 * g - 1)
                for t in range(TILES):
                    for n, (x, y) in enumerate(triple(hi, lo, dfthi, dftlo)):
                        mm = nc.tensor.matmul(ps1[t // 2][:, t % 2, :], x[:, g, t * P:(t + 1) * P], y[:, 0:NCHAN],
                                              start=n == 0, stop=n == 2)
                mm.then_inc(one_mm, 1)

            channels(0)
            for g in range(NC):
                pe.wait_ge(one_lo, g + 1)
                if g:
                    pe.wait_ge(two_out, 2 * g)
                for k, ps in enumerate((psA, psB)):
                    tiles = range(1) if k == 0 else range(1, TILES)
                    prods = [(t, part, x, y) for t in tiles for part in range(2) for x, y in triple(f1hi, f1lo, dfthi, dftlo)]
                    for n, (t, part, x, y) in enumerate(prods):
                        if k == 0:
                            c0, w = NCHAN + part * P, P
                        else:
                            c0, w = NCHAN + NCTX + ((t - 1) * 2 + part) * S_DEC, S_DEC
                        mm = nc.tensor.matmul(ps[:, 0:w], x[:, t, part * P:(part + 1) * P], y[:, c0:c0 + w],
                                              start=n == 0, stop=n == len(prods) - 1)
                mm.then_inc(two_mm, 1)
                if g + 1 < NC:
                    channels(g + 1)
    sm.close()


NORM_A = 2 * DEPTH + 1


def build(nc, d, out, stop=None):
    with ExitStack() as top:
        sb = lambda es, n, shape, dt=F32: es.enter_context(nc.sbuf_tensor(n, shape, dt))
        m = {
            "xT": sb(top, "xT", [P, NC, T]),
            "mats": sb(top, "mats", [P, NMATS, P]),
            "ones": sb(top, "ones", [P, P]),
            "gains": sb(top, "gains", [P, 2 * DEPTH + 2, NC]),
            "mod": sb(top, "mod", [P, DEPTH, 6, NC, 2]),
            "amul": sb(top, "amul", [P, DEPTH, 2, NC, 2]),
        }
        hi, lo = sb(top, "hi", [P, NC, T], F32R), sb(top, "lo", [P, NC, T], F32R)
        g_dram = nc.dram_tensor("g_scratch", [P, P, T], F32, kind="Internal").ap()
        a_dram = nc.dram_tensor("a_scratch", [P, P, T], F32, kind="Internal").ap()

        def norm(tag, l, n):
            norm_stage(nc, m, tag, lambda c, k: m["amul"][:, l, n, c, k:k + 1], lambda c, k: m["mod"][:, l, 3 * n, c, k:k + 1], (hi, lo))

        load_stage(nc, m, d)
        ada_stage(nc, m, d)
        if stop == "ada":
            return
        for l in range(DEPTH):
            norm(f"n1{l}", l, 0)
            if l % 2 == 0:
                even_mixer(nc, m, d, hi, lo, out["state"])
                w_out = d["w_out_ab"]
            else:
                fourier_stage(nc, m, d, hi, lo, hi, lo)
                w_out = d["w_out_c"]
            project_stage(nc, f"wo{l}", w_out, NC, hi, lo, False, add_to_x(nc, m, m["mod"][:, l, 2]))
            if stop == f"mix{l}":
                return
            norm(f"n2{l}", l, 1)
            peer(nc, m, d, f"p{l}", l, hi, lo, g_dram, a_dram)
            if stop == f"peer{l}":
                return
        norm_stage(nc, m, "fin", lambda c, k: m["gains"][:, 2 * DEPTH, c:c + 1], lambda c, k: None, out["yT"])


def even_mixer(nc, m, d, hi, lo, state_out):
    with ExitStack() as es:
        sb = lambda e, n, shape, dt=F32: e.enter_context(nc.sbuf_tensor(n, shape, dt))
        qkv = sb(es, "qkv", [P, 3 * HEADS, LEN_A - TAPS_A + 1])
        z = sb(es, "z", [P, HEADS, T])
        lg, beta, gcol = (sb(es, n, [P, TILES, 2 * HEADS]) for n in ("lg", "beta", "gcol"))
        with ExitStack() as inner:
            raw = sb(inner, "qkvraw", [P, 3 * HEADS, LEN_A])
            conf = sb(inner, "conf", [P, 2 * B_CH // P, T])

            def padded(n, j, psums):
                for k, ((a, b), ps) in enumerate(zip(SEGS, psums)):
                    c0 = a + PAD_A * (k + 1)
                    last = nc.scalar.copy(raw[:, bass.ds(n, 1), c0:c0 + b - a].rearrange("p o t -> p (o t)"), ps[:, 0:b - a])
                return last

            def silu_out(n, j, psums):
                for (a, b), ps in zip(SEGS, psums):
                    last = nc.scalar.activation(z[:, bass.ds(n, 1), a:b].rearrange("p o t -> p (o t)"), ps[:, 0:b - a], ACT.Silu)
                return last

            project_stage(nc, "wqkv", d["w_qkv"], 3 * HEADS, hi, lo, True, padded)
            project_stage(nc, "wz", d["w_z"], HEADS, hi, lo, True, silu_out)
            project_stage(nc, "wcf", d["w_conf"], 2 * B_CH // P, hi, lo, True, copy_out(nc, conf))
            decay_stage(nc, m, d, hi, lo, lg, beta, gcol)
            short_conv_stage(nc, m, d, raw, qkv)
            conformer_stage(nc, m, d, conf, hi, lo, HEADS)
        with ExitStack() as inner:
            tok = sb(inner, "tok", [P, 2, TILES, HEADS, P])
            o_acc = sb(inner, "o_acc", [P, HEADS, T])
            tokens_stage(nc, m, qkv, tok)
            delta_stage(nc, m, d, qkv, tok, lg, beta, gcol, o_acc, state_out)
            gated_norm_stage(nc, m, o_acc, z, hi, lo)


def peer(nc, m, d, tag, l, hi, lo, g_dram, a_dram):
    with ExitStack() as es:
        tops = es.enter_context(nc.sbuf_tensor(tag + "tops", [P, 3, T], F32))
        with nc.sbuf_tensor(tag + "qT", [P, NSC, T], F32) as qT:
            project_stage(nc, tag + "q", d["wq"][l], NSC, hi, lo, True, copy_out(nc, qT))
            score_stage(nc, m, tag + "s", d, l, qT, tops)
        gates_stage(nc, m, tag + "g", tops, g_dram)
    with nc.sbuf_tensor(tag + "act", [P, 2, T], F32) as act:
        def gelu_out(n, j, psums):
            for (a, b), ps in zip(SEGS, psums):
                last = nc.scalar.activation(act[:, j, a:b], ps[:, 0:b - a], ACT.Gelu_apprx_tanh)
            return last

        project_stage(nc, tag + "u", d["u"][l], P, hi, lo, True, gelu_out, store=(act, a_dram))
    experts_out_stage(nc, m, tag + "v", d["v"][l], g_dram, a_dram, m["mod"][:, l, 5])


def blocks(w):
    w = np.asarray(w)
    *lead, k, n = w.shape
    w = w.reshape(*lead, k // P, P, n // P, P)
    return np.ascontiguousarray(np.moveaxis(w, -2, -4).swapaxes(-3, -2)).reshape(*lead, n // P, P, k)


def position_embedding():
    t = np.arange(S_DEC, dtype=np.float32)
    nf = D // 4
    freqs = np.exp(np.float32(-np.log(POS_BASE)) * np.arange(nf, dtype=np.float32) / np.float32(nf)).astype(np.float32)
    ar = ((t // GRID_W)[:, None] * freqs).astype(np.float32)
    ac = ((t % GRID_W)[:, None] * freqs).astype(np.float32)
    emb = np.concatenate([np.sin(ar), np.cos(ar), np.sin(ac), np.cos(ac)], 1).astype(np.float32)
    return chunked(emb.T)


def chunked(xT):
    return np.ascontiguousarray(xT.reshape(-1, P, xT.shape[1]).swapaxes(0, 1))


def dft_matrices():
    def pair(n, rows):
        a = 2 * np.pi * (np.outer(rows, np.arange(n)) % n) / n
        return np.cos(a) / np.sqrt(n), np.sin(a) / np.sqrt(n)
    c, s = pair(P, np.arange(P))
    parts = [c, -s, *pair(S_CTX, np.arange(S_CTX))]
    for t in range(S_DEC // P):
        parts += pair(S_DEC, np.arange(t * P, (t + 1) * P))
    return np.ascontiguousarray(np.concatenate(parts, 1).astype(np.float32))


def layout(x_prompt, x_sample, state_delta, c, c_ctx, ada_w, ada_b, norm1_g, norm2_g, w_in_ab, conv_qkv_w, a_log, dt_bias,
           delta_norm_g, conf_dw_w, conf_dw_b, conf_ln_g, conf_ln_b, w_out_ab, w_out_c, peer_wq, peer_k1, peer_k2,
           peer_u, peer_v, final_norm_g):
    A = HEADS * DK
    g = np.asarray
    col = lambda v: g(v).reshape(-1, P).T
    w_in = g(w_in_ab)[0]
    z0, ab0, cf0 = 3 * A, 4 * A, 4 * A + 4 * HEADS
    gains = np.stack([x for l in range(DEPTH) for x in (col(norm1_g[l]), col(norm2_g[l]))] + [col(final_norm_g)]
                     + [np.repeat(g(delta_norm_g)[0][:, None], NC, 1)], 1)
    keys = np.stack([g(peer_k1), g(peer_k2)], 2)
    u = g(peer_u).reshape(DEPTH, P, P, NC, P)
    v = g(peer_v).reshape(DEPTH, P, P, D)
    ac = np.ascontiguousarray
    return {
        "xT": chunked(np.concatenate([g(x_prompt)[0], g(x_sample)[0]], 0).T),
        "pos": position_embedding(),
        "mats": constants()[0],
        "masks": constants()[1],
        "dft": dft_matrices(),
        "gains": ac(gains),
        "cond": chunked(np.stack([g(c_ctx), g(c)[0]], 1)),
        "adab": ac(g(ada_b).reshape(DEPTH, 48, P).transpose(2, 0, 1)),
        "ada_w": ac(g(ada_w).reshape(DEPTH, NC, P, 12, 512).transpose(0, 3, 2, 1, 4)).reshape(DEPTH * 12, P, NC, 512),
        "w_qkv": blocks(w_in[:, 0:z0]),
        "w_z": blocks(w_in[:, z0:ab0]),
        "w_ab": chunked(w_in[:, ab0:cf0]),
        "w_conf": blocks(w_in[:, cf0:]),
        "alog": ac(np.broadcast_to(np.stack([g(a_log)[0].reshape(-1), g(dt_bias)[0].reshape(-1)]), (P, 2, 2 * HEADS))),
        "conv_w": chunked(g(conv_qkv_w)[0].T),
        "conf_w": chunked(np.concatenate([g(conf_dw_w)[0].T, g(conf_dw_b)[0][:, None], g(conf_ln_g)[0][:, None], g(conf_ln_b)[0][:, None]], 1)),
        "state": ac(g(state_delta)[0, 0].reshape(2 * HEADS, DK, DK).transpose(1, 0, 2)),
        "w_out_ab": blocks(g(w_out_ab)[0]),
        "w_out_c": blocks(g(w_out_c)[0]),
        "wq": blocks(peer_wq),
        "keys": ac(keys.transpose(0, 4, 1, 2, 3)).reshape(DEPTH, P, NSC, P),
        "u": ac(u.transpose(0, 2, 4, 3, 1)).reshape(DEPTH, P, P, D),
        "v": ac(v.transpose(0, 2, 1, 3)),
    }


def kernel(**inputs):
    import concourse.bacc as bacc
    from concourse.bass_utils import run_bass_kernel_spmd

    arrays = {f"in_{k}": a for k, a in layout(**inputs).items()}
    nc = bacc.Bacc("TRN2", target_bir_lowering=False, num_devices=1)
    d = {k[3:]: nc.dram_tensor(k, a.shape, mybir.dt.from_np(a.dtype), kind="ExternalInput").ap() for k, a in arrays.items()}
    out = {"yT": nc.dram_tensor("out_yT", (P, NC, T), F32, kind="ExternalOutput").ap(),
           "state": nc.dram_tensor("out_state", (2 * HEADS, DK, DK), F32, kind="ExternalOutput").ap()}
    build(nc, d, out)
    r = run_bass_kernel_spmd(nc, [arrays], core_ids=[0]).results[0]
    y = r["out_yT"].transpose(2, 1, 0).reshape(T, D)
    return (y[:S_CTX].reshape(1, S_CTX, D), y[S_CTX:].reshape(1, S_DEC, D),
            r["out_state"].reshape(1, 1, 2, HEADS, DK, DK))
```

```python
from contextlib import ExitStack

import numpy as np
import concourse.bass as bass
from concourse import mybir

F32 = mybir.dt.float32
F32R = mybir.dt.float32r
U32 = mybir.dt.uint32
ALU = mybir.AluOpType
ACT = mybir.ActivationFunctionType
AX = mybir.AxisListType

P = 128
D = 1024
NC = D // P
S_CTX, S_DEC = 128, 512
T = S_CTX + S_DEC
TILES = T // P
SEGS = ((0, S_CTX), (S_CTX, T))
HALF = T // 2
PIECES = ((0, 0, S_CTX, 0), (0, S_CTX, HALF, 1), (1, HALF, T, 1))
DEPTH = 2
EPS = 1e-6
HEADS = 4
DK = 128
TAPS_A = 7
TAPS_B = 31
PAD_A = TAPS_A // 2
PAD_B = TAPS_B // 2
LEN_A = T + 3 * PAD_A
LEN_B = T + 3 * PAD_B
B_CH = D // 2
PEER_HEADS = 8
TOPK = 16
NSC = 2 * PEER_HEADS
GRID_W = 64
POS_BASE = 10000.0
LEVELS = 7
NEG = -3.0e38


class Sems:

    def __init__(self, nc, stage):
        self.nc, self.stage, self.taken = nc, stage, []

    def __call__(self, name):
        self.taken.append(self.nc.alloc_semaphore(f"{self.stage}_{name}"))
        return self.taken[-1]

    def close(self):
        self.nc.clear_and_free_semaphores(self.taken)
        self.nc.all_engine_barrier()


class Steps:

    def __init__(self, eng, sem):
        self.eng, self.sem, self.n = eng, sem, 0

    def done(self, ins):
        ins.then_inc(self.sem, 1)
        self.n += 1
        return self.n

    def wait(self, n=None):
        self.eng.wait_ge(self.sem, self.n if n is None else n)

    def link(self, ins):
        self.done(ins)
        self.wait()


class LoopSteps(Steps):

    def __init__(self, eng, sem, t, per):
        super().__init__(eng, sem)
        self.t, self.per = t, per

    def wait(self, n=None):
        self.eng.wait_ge(self.sem, self.t * self.per + (self.n if n is None else n))

    def close(self):
        assert self.n == self.per, self.n


def hold(eng, sem, value):
    eng.wait_ge(sem, value)
    eng.nop(nofuse=True)


def load_stage(nc, m, d):
    sm = Sems(nc, "load")
    loaded, added = sm("loaded"), sm("added")
    with nc.sbuf_tensor("pos", [P, NC, S_DEC], F32) as pos:
        with nc.Block() as block:
            @block.sync
            def _(sp):
                for dst, src in ((m["xT"], d["xT"]), (m["mats"], d["mats"]), (m["gains"], d["gains"]),
                                 (pos, d["pos"])):
                    sp.dma_start(dst[:], src).then_inc(loaded, 16)

            @block.vector
            def _(dve):
                dve.wait_ge(loaded, 64)
                for c in range(NC):
                    x = m["xT"][:, c, S_CTX:T]
                    nc.vector.tensor_tensor(x, x, pos[:, c, :], ALU.add).then_inc(added, 1)
                nc.vector.memset(m["ones"][:], 1.0).then_inc(added, 1)
                dve.wait_ge(added, NC + 1)
    sm.close()


def ada_stage(nc, m, d):
    sm = Sems(nc, "ada")
    HALF = 512
    NH = 6 * D // HALF
    slab_full = [sm(f"slab_full{j}") for j in range(2)]
    slab_used = [sm(f"slab_used{j}") for j in range(2)]
    cond_full, cond_ready, steps = sm("cond_full"), sm("cond_ready"), sm("steps")
    with nc.sbuf_tensor("slab", [P, 2, NC, HALF], F32) as slab, \
            nc.sbuf_tensor("cond", [P, NC, 2], F32) as cond, \
            nc.sbuf_tensor("condact", [P, NC, 2], F32) as condact, \
            nc.sbuf_tensor("adab", [P, DEPTH, 48], F32) as adab, \
            nc.psum_tensor("mod0", [P, 96], F32) as mod0, nc.psum_tensor("mod1", [P, 96], F32) as mod1:
        with nc.Block() as block:
            @block.sync
            def _(sp):
                sp.dma_start(cond[:], d["cond"]).then_inc(cond_full, 16)
                sp.dma_start(adab[:], d["adab"]).then_inc(cond_full, 16)
                for n in range(DEPTH * NH):
                    if n >= 2:
                        sp.wait_ge(slab_used[n % 2], n // 2)
                    sp.dma_start(slab[:, n % 2], d["ada_w"][n]).then_inc(slab_full[n % 2], 16)

            @block.scalar
            def _(act):
                act.wait_ge(cond_full, 32)
                nc.scalar.activation(condact[:], cond[:], ACT.Silu).then_inc(cond_ready, 1)

            @block.tensor
            def _(pe):
                pe.wait_ge(cond_ready, 1)
                for n in range(DEPTH * NH):
                    ps = (mod0, mod1)[n // NH]
                    pe.wait_ge(slab_full[n % 2], 16 * (n // 2 + 1))
                    for b in range(HALF // P):
                        col = 2 * ((n % NH) * (HALF // P) + b)
                        for c in range(NC):
                            mm = nc.tensor.matmul(ps[:, col:col + 2], slab[:, n % 2, c, b * P:(b + 1) * P],
                                                  condact[:, c, :], start=c == 0, stop=c == NC - 1)
                    mm.then_inc(slab_used[n % 2], 1)

            @block.vector
            def _(dve):
                st = Steps(dve, steps)
                for s in slab_used:
                    dve.wait_ge(s, DEPTH * NH // 2)
                for l, ps in enumerate((mod0, mod1)):
                    st.done(nc.vector.tensor_tensor(
                        m["mod"][:, l].rearrange("p a c k -> p (a c) k"), ps[:].rearrange("p (b k) -> p b k", k=2),
                        adab[:, l, :].unsqueeze(2).to_broadcast([P, 48, 2]), ALU.add))
                st.wait()
                for l in range(DEPTH):
                    for n in range(2):
                        st.done(nc.vector.scalar_tensor_tensor(
                            out=m["amul"][:, l, n], in0=m["mod"][:, l, 1 + 3 * n], scalar=1.0,
                            in1=m["gains"][:, 2 * l + n, :].unsqueeze(2).to_broadcast([P, NC, 2]),
                            op0=ALU.add, op1=ALU.mult))
                st.wait()
    sm.close()


def sum_of_squares(nc, pe, ones, sq, sq_ready, sq_used, psums, n):
    for c in range(n):
        pe.wait_ge(sq_ready, c + 1)
        for (a, b), ps in zip(SEGS, psums):
            mm = nc.tensor.matmul(ps[:, 0:b - a], ones[:], sq[:, c % 2, a:b], start=c == 0, stop=c == n - 1)
        mm.then_inc(sq_used, 1)


def norm_stage(nc, m, tag, mul, add, out):
    sm = Sems(nc, tag)
    sq_ready, sq_used, var_ready, std_ready, steps = (sm(x) for x in ("sq_ready", "sq_used", "var_ready", "std_ready", "steps"))
    h_ready, hi_ready, h_used = sm("h_ready"), sm("hi_ready"), sm("h_used")
    xT = m["xT"]
    final = not isinstance(out, tuple)
    with nc.sbuf_tensor(tag + "sq", [P, 2, T], F32) as sq, nc.sbuf_tensor(tag + "var", [P, T], F32) as var, \
            nc.sbuf_tensor(tag + "rstd", [P, T], F32) as rstd, nc.sbuf_tensor(tag + "xn", [P, 2, T], F32) as xn, \
            nc.sbuf_tensor(tag + "h", [P, 2, T], F32) as h, \
            nc.psum_tensor(tag + "ssA", [P, 128], F32) as ssA, nc.psum_tensor(tag + "ssB", [P, 512], F32) as ssB:
        with nc.Block() as block:
            @block.scalar
            def _(act):
                for c in range(NC):
                    if c >= 2:
                        act.wait_ge(sq_used, c - 1)
                    nc.scalar.activation(sq[:, c % 2, :], xT[:, c, :], ACT.Square).then_inc(sq_ready, 1)
                act.wait_ge(var_ready, 2)
                nc.scalar.activation(rstd[:], var[:], ACT.Sqrt).then_inc(std_ready, 1)
                if not final:
                    for c in range(NC):
                        act.wait_ge(h_ready, 2 * (c + 1))
                        nc.scalar.copy(out[0][:, c, :], h[:, c % 2, :]).then_inc(hi_ready, 1)

            @block.tensor
            def _(pe):
                sum_of_squares(nc, pe, m["ones"], sq, sq_ready, sq_used, (ssA, ssB), NC)

            @block.vector
            def _(dve):
                st = Steps(dve, steps)
                dve.wait_ge(sq_used, NC)
                for (a, b), ps in zip(SEGS, (ssA, ssB)):
                    nc.vector.tensor_scalar(var[:, a:b], ps[:, 0:b - a], 1.0 / D, EPS, ALU.mult, ALU.add).then_inc(var_ready, 1)
                dve.wait_ge(std_ready, 1)
                st.link(nc.vector.reciprocal(var[:], rstd[:]))
                for c in range(NC):
                    st.link(nc.vector.tensor_tensor(xn[:, c % 2, :], xT[:, c, :], var[:], ALU.mult))
                    if c >= 2:
                        dve.wait_ge(h_used, (16 if final else 1) * (c - 1))
                    for k, (a, b) in enumerate(SEGS):
                        nc.vector.tensor_scalar(h[:, c % 2, a:b], xn[:, c % 2, a:b], mul(c, k), add(c, k),
                                                ALU.mult, ALU.add if add(c, k) is not None else ALU.bypass).then_inc(h_ready, 1)

            if final:
                @block.sync
                def _(sp):
                    for c in range(NC):
                        sp.wait_ge(h_ready, 2 * (c + 1))
                        sp.dma_start(out[:, c, :], h[:, c % 2, :]).then_inc(h_used, 16)
                        sp.wait_ge(h_used, 16 * (c + 1))
            else:
                @block.gpsimd
                def _(pool):
                    for c in range(NC):
                        pool.wait_ge(hi_ready, c + 1)
                        nc.gpsimd.tensor_tensor(out[1][:, c, :], h[:, c % 2, :], out[0][:, c, :].bitcast(F32),
                                                ALU.subtract).then_inc(h_used, 1)
                    pool.wait_ge(h_used, NC)
    sm.close()


def credit(eng, sems, n=1):
    for s in sems:
        eng.sem_inc(s, n)


def run_ahead(eng, n_it, prepare, take):
    prepare(0, 0)
    with eng.Fori(0, n_it - 1) as i:
        prepare(i, 1)
        take(i, 0)
        prepare(i + 1, 0)
        take(i, 1)
    prepare(n_it - 1, 1)
    take(n_it - 1, 0)
    take(n_it - 1, 1)


def block_products(nc, ps, j, whi, wlo, hi, lo):
    for k in range(2):
        for c in range(NC):
            for n, (x, y) in enumerate(((whi, hi), (whi, lo), (wlo, hi))):
                mm = nc.tensor.matmul(ps[:, k, 0:HALF], x[:, j, c * P:(c + 1) * P], y[:, c, k * HALF:(k + 1) * HALF],
                                      start=c == 0 and n == 0, stop=c == NC - 1 and n == 2)
    return mm


def halves(x):
    return x.rearrange("p (k t) -> p k t", k=2)


def project_stage(nc, tag, w_dram, nb, hi, lo, on_act, evacuate, store=None):
    sm = Sems(nc, tag)
    raw_full, hi_done, split, mm_done, evac_done = (
        [sm(f"{x}{j}") for j in range(2)] for x in ("raw_full", "hi_done", "split", "mm_done", "evac_done"))
    stored = [sm(f"stored{j}") for j in range(2)] if store is not None else None
    n_it = nb // 2
    with nc.sbuf_tensor(tag + "raw", [P, 2, NC * P], F32) as raw, nc.sbuf_tensor(tag + "whi", [P, 2, NC * P], F32R) as whi, \
            nc.sbuf_tensor(tag + "wlo", [P, 2, NC * P], F32R) as wlo, \
            nc.psum_tensor(tag + "ps0", [P, 2, 512], F32) as ps0, nc.psum_tensor(tag + "ps1", [P, 2, 512], F32) as ps1:
        psums = (ps0, ps1)

        def take(eng, i, j):
            eng.wait_ge(mm_done[j], i + 2)
            if store is not None:
                eng.wait_ge(stored[j], (i + 1) * 16)
            eng.nop(nofuse=True)
            evacuate(i * 2 + j, j, psums[j]).then_inc(evac_done[j], 1)
            if store is not None:
                hold(eng, evac_done[j], i + 2)
                buf, dram = store
                eng.dma_start(dram[bass.ds(i * 2 + j, 1)].rearrange("o p n -> p (o n)"), buf[:, j]).then_inc(stored[j], 16)

        with nc.Block() as block:
            @block.sync
            def _(sp):
                credit(sp, split + mm_done + evac_done)
                if store is not None:
                    credit(sp, stored, 16)
                with sp.Fori(0, n_it) as i:
                    for j in range(2):
                        hold(sp, split[j], i + 1)
                        sp.dma_start(raw[:, j], w_dram[bass.ds(i * 2 + j, 1)].rearrange("o p n -> p (o n)")).then_inc(raw_full[j], 16)

            @block.scalar
            def _(act):
                def split_hi(i, j):
                    act.wait_ge(raw_full[j], (i + 1) * 16)
                    act.wait_ge(mm_done[j], i + 1)
                    nc.scalar.copy(whi[:, j, :], raw[:, j, :]).then_inc(hi_done[j], 1)

                if on_act:
                    run_ahead(act, n_it, split_hi, lambda i, j: take(act, i, j))
                    for x in stored or ():
                        act.wait_ge(x, 16 * (n_it + 1))
                else:
                    with act.Fori(0, n_it) as i:
                        for j in range(2):
                            split_hi(i, j)

            @block.vector
            def _(dve):
                def split_lo(i, j):
                    dve.wait_ge(hi_done[j], i + 1)
                    nc.vector.tensor_tensor(wlo[:, j, :], raw[:, j, :], whi[:, j, :].bitcast(F32), ALU.subtract).then_inc(split[j], 1)

                if on_act:
                    with dve.Fori(0, n_it) as i:
                        for j in range(2):
                            split_lo(i, j)
                else:
                    run_ahead(dve, n_it, split_lo, lambda i, j: take(dve, i, j))

            @block.tensor
            def _(pe):
                with pe.Fori(0, n_it) as i:
                    for j in range(2):
                        pe.wait_ge(split[j], i + 2)
                        pe.wait_ge(evac_done[j], i + 1)
                        block_products(nc, psums[j], j, whi, wlo, hi, lo).then_inc(mm_done[j], 1)
    sm.close()


def copy_out(nc, dst, first=0):
    def evacuate(n, j, ps):
        return nc.scalar.copy(halves(dst[:, bass.ds(n + first, 1), :].rearrange("p o t -> p (o t)")), ps[:, :, 0:HALF])
    return evacuate


def add_to_x(nc, m, gate):
    def evacuate(n, j, ps):
        for half, a, b, k in PIECES:
            x = m["xT"][:, bass.ds(n, 1), a:b].rearrange("p o t -> p (o t)")
            g = gate[:, bass.ds(n, 1), k:k + 1].rearrange("p o t -> p (o t)")
            last = nc.vector.scalar_tensor_tensor(out=x, in0=ps[:, half, a - half * HALF:b - half * HALF], scalar=g, in1=x,
                                                  op0=ALU.mult, op1=ALU.add)
        return last
    return evacuate


QUAD = 4
NQ = P // QUAD
TILE_BLOCKS = 24
VEC_STEPS = 5 * NSC + 5 * PEER_HEADS + 13


def experts_in_stage(nc, m, tag, d, l, hi, lo, q_dram, a_dram, g_dram):
    sm = Sems(nc, tag)
    raw_full, hi_done, split, mm_done, evac_done, stored, one1, one2, made, taken = (
        [sm(f"{x}{j}") for j in range(2)]
        for x in ("raw_full", "hi_done", "split", "mm_done", "evac_done", "stored", "one1", "one2", "made", "taken"))
    keys_full, q_full, scored, s_taken, steps, exp_ready, exp_done, ready, turned, t_taken, g_stored = (
        sm(x) for x in ("keys_full", "q_full", "scored", "s_taken", "steps", "exp_ready", "exp_done", "ready", "turned",
                        "t_taken", "g_stored"))
    USES = TILE_BLOCKS // 2
    REST = P - TILES * TILE_BLOCKS
    with ExitStack() as es:
        sb = lambda n, shape, dt=F32: es.enter_context(nc.sbuf_tensor(tag + n, shape, dt))
        raw = sb("raw", [P, 2, D])
        whi, wlo = sb("whi", [P, 2, D], F32R), sb("wlo", [P, 2, D], F32R)
        a_out = sb("a_out", [P, 2, T])
        keys, qt = sb("keys", [P, NSC, P]), sb("qt", [P, NSC, P])
        sc = sb("sc", [P, NSC * P])
        eq = sc[:].rearrange("p (n a) -> p n a", a=TOPK)
        rest = sb("rest", [P, 2, 2 * P])
        val, idx, idxf = sb("val", [P, NSC, TOPK]), sb("idx", [P, NSC, TOPK], U32), sb("idxf", [P, NSC, TOPK])
        cand = sb("cand", [P, PEER_HEADS, TOPK * TOPK])
        sv, si = sb("sv", [P, PEER_HEADS, TOPK]), sb("si", [P, PEER_HEADS, TOPK], U32)
        pick = sb("pick", [P, 2, P], U32)
        pickf = rest[:, 0, :].rearrange("p (w n) -> p w n", w=2)
        rows = sb("rows", [P, 2, P])
        ex, gate = sb("ex", [P, PEER_HEADS, TOPK]), sb("gate", [P, PEER_HEADS, TOPK])
        den, rden = sb("den", [P, PEER_HEADS]), sb("rden", [P, PEER_HEADS])
        tops = sb("tops", [P, 3, P])
        oh1, oh2 = sb("oh1", [P, 2, QUAD, P]), sb("oh2", [P, 2, QUAD, P])
        g = sb("g", [P, P, P])
        psums = [es.enter_context(nc.psum_tensor(f"{tag}ps{j}", [P, 2, 512], F32)) for j in range(2)]
        bank = [es.enter_context(nc.psum_tensor(f"{tag}bank{k}", [P, QUAD, P], F32)) for k in range(4)]
        ident, iota = m["mats"][:, IDENT, :], m["mats"][:, IOTA, :]
        block = es.enter_context(nc.Block())

        def quads(b):
            return range(3 * (b - 13), min(3 * (b - 12), NQ)) if b >= 13 else range(0)

        @block.sync
        def _(sp):
            credit(sp, split + mm_done + evac_done + made + taken + [scored, ready, turned, t_taken])
            credit(sp, stored + [g_stored], 16)

            def load(t, b):
                j = b % 2
                hold(sp, split[j], t * USES + (b // 2 + 1))
                sp.dma_start(raw[:, j], d["u"][l][bass.ds(t * TILE_BLOCKS + b, 1)].rearrange("o p n -> p (o n)")).then_inc(raw_full[j], 16)

            sp.dma_start(keys[:], d["keys"][l]).then_inc(keys_full, 16)
            with sp.Fori(0, TILES) as t:
                hold(sp, scored, t + 1)
                sp.dma_start(qt[:], q_dram[:, :, bass.ds(t * P, P)].rearrange("h p t -> p h t")).then_inc(q_full, 16)
                for b in range(TILE_BLOCKS):
                    load(t, b)
            for b in range(REST):
                load(TILES, b)

        @block.tensor
        def _(pe):
            def products(t, b):
                j = b % 2
                pe.wait_ge(split[j], t * USES + (b // 2 + 2))
                pe.wait_ge(evac_done[j], t * USES + (b // 2 + 1))
                block_products(nc, psums[j], j, whi, wlo, hi, lo).then_inc(mm_done[j], 1)

            pe.wait_ge(keys_full, 16)
            with pe.Fori(0, TILES) as t:
                for b in range(TILE_BLOCKS):
                    products(t, b)
                    if b == 0:
                        pe.wait_ge(q_full, (t + 1) * 16)
                        pe.wait_ge(t_taken, t + 1)
                        for j in range(2):
                            pe.wait_ge(taken[j], t * (NQ // 2) + 1)
                        for h in range(NSC):
                            mm = nc.tensor.matmul(bank[h // 4][:, h % 4, :], qt[:, h, :], keys[:, h, :], start=True, stop=True)
                        mm.then_inc(scored, 1)
                    if b == 12:
                        pe.wait_ge(ready, t + 2)
                        for w, src in enumerate((rows[:, 0, :], rows[:, 1, :], gate[:].rearrange("p h k -> p (h k)"))):
                            mm = nc.tensor.transpose(bank[2][:, w, :], src, ident)
                        mm.then_inc(turned, 1)
                    for q in quads(b):
                        j, n = q % 2, q // 2
                        pe.wait_ge(one1[j], t * (NQ // 2) + (n + 1))
                        pe.wait_ge(one2[j], t * (NQ // 2) + (n + 1))
                        pe.wait_ge(taken[j], t * (NQ // 2) + (n + 1))
                        for k in range(QUAD):
                            mm = nc.tensor.matmul(bank[j][:, k, :], oh1[:, j, k, :], oh2[:, j, k, :], start=True, stop=True)
                        mm.then_inc(made[j], 1)
            for b in range(REST):
                products(TILES, b)

        @block.scalar
        def _(act):
            def split_hi(t, b):
                j, n = b % 2, b // 2
                act.wait_ge(raw_full[j], t * (16 * USES) + 16 * (n + 1))
                act.wait_ge(mm_done[j], t * USES + (n + 1))
                nc.scalar.copy(whi[:, j, :], raw[:, j, :]).then_inc(hi_done[j], 1)

            def take(t, b):
                j, n = b % 2, b // 2
                act.wait_ge(mm_done[j], t * USES + (n + 2))
                act.wait_ge(stored[j], t * (16 * USES) + 16 * (n + 1))
                nc.scalar.activation(halves(a_out[:, j, :]), psums[j][:, :, 0:HALF], ACT.Gelu_apprx_tanh).then_inc(evac_done[j], 1)
                hold(act, evac_done[j], t * USES + (n + 2))
                act.dma_start(a_dram[bass.ds(t * TILE_BLOCKS + b, 1)].rearrange("o p n -> p (o n)"), a_out[:, j]).then_inc(stored[j], 16)

            split_hi(0, 0)
            with act.Fori(0, TILES) as t:
                for b in range(TILE_BLOCKS):
                    split_hi(t, b + 1)
                    take(t, b)
                    if b == 0:
                        act.wait_ge(ready, t + 1)
                        act.wait_ge(scored, t + 2)
                        for k in range(4):
                            nc.scalar.copy(sc[:, k * 512:(k + 1) * 512], bank[k][:].rearrange("p a b -> p (a b)")).then_inc(s_taken, 1)
                    if b == 9:
                        act.wait_ge(exp_ready, t + 1)
                        nc.scalar.activation(ex[:], ex[:], ACT.Exp).then_inc(exp_done, 1)
                    if b == 12:
                        act.wait_ge(turned, t + 2)
                        nc.scalar.copy(tops[:], bank[2][:, 0:3, :]).then_inc(t_taken, 1)
                        act.wait_ge(g_stored, (t + 1) * 16)
                    for q in quads(b):
                        j, n = q % 2, q // 2
                        act.wait_ge(made[j], t * (NQ // 2) + (n + 2))
                        nc.scalar.copy(g[:, :, q * QUAD:(q + 1) * QUAD].rearrange("p i t -> p t i"), bank[j][:]).then_inc(taken[j], 1)
                for j in range(2):
                    hold(act, taken[j], t * (NQ // 2) + (NQ // 2 + 1))
                act.dma_start(g_dram[:, :, bass.ds(t * P, P)].rearrange("i p t -> p i t"), g[:]).then_inc(g_stored, 16)
            for b in range(REST):
                if b + 1 < REST:
                    split_hi(TILES, b + 1)
                take(TILES, b)
            for j in range(2):
                act.wait_ge(stored[j], 16 * (P // 2 + 1))
            act.wait_ge(g_stored, 16 * (TILES + 1))

        @block.vector
        def _(dve):
            v = nc.vector

            def split_lo(t, b):
                j = b % 2
                dve.wait_ge(hi_done[j], t * USES + (b // 2 + 1))
                v.tensor_tensor(wlo[:, j, :], raw[:, j, :], whi[:, j, :].bitcast(F32), ALU.subtract).then_inc(split[j], 1)

            split_lo(0, 0)
            with dve.Fori(0, TILES) as t:
                st = LoopSteps(dve, steps, t, VEC_STEPS)

                def top16(values, scratch, out_v, out_i):
                    st.link(v.max(out_v[:, 0:8], values))
                    dve.nop(nofuse=True)
                    st.done(v.max_index(out_i[:, 0:8], out_v[:, 0:8], values))
                    st.link(v.match_replace(scratch, out_v[:, 0:8], values, NEG))
                    dve.nop(nofuse=True)
                    st.link(v.max(out_v[:, 8:16], scratch))
                    dve.nop(nofuse=True)
                    st.done(v.max_index(out_i[:, 8:16], out_v[:, 8:16], scratch))

                def choose(w):
                    st.link(v.tensor_tensor(eq, pickf[:, w, :].unsqueeze(2).to_broadcast([P, P, TOPK]),
                                            iota[:, 0:TOPK].unsqueeze(1).to_broadcast([P, P, TOPK]), ALU.is_equal))
                    eq4 = eq.rearrange("p (h k) a -> p h k a", h=PEER_HEADS)
                    st.link(v.tensor_tensor(eq4, eq4, idxf[:, w:NSC:2, :].unsqueeze(2).to_broadcast([P, PEER_HEADS, TOPK, TOPK]), ALU.mult))
                    if w == 0:
                        dve.wait_ge(turned, t + 1)
                    st.link(v.tensor_reduce(rows[:, w, :], eq, AX.X, ALU.add))

                for b in range(TILE_BLOCKS):
                    split_lo(t, b + 1)
                    if b == 1:
                        hold(dve, s_taken, (t + 1) * 4)
                    if 1 <= b <= 4:
                        for h in range(4 * (b - 1), 4 * b):
                            top16(sc[:, h * P:(h + 1) * P], rest[:, h % 2, 0:P], val[:, h], idx[:, h])
                    if b == 5:
                        st.wait()
                        st.done(v.tensor_copy(idxf[:], idx[:]))
                        v1 = val[:, 0:NSC:2, :].unsqueeze(3).to_broadcast([P, PEER_HEADS, TOPK, TOPK])
                        v2 = val[:, 1:NSC:2, :].unsqueeze(2).to_broadcast([P, PEER_HEADS, TOPK, TOPK])
                        st.link(v.tensor_tensor(cand[:].rearrange("p h (a b) -> p h a b", a=TOPK), v1, v2, ALU.add))
                        dve.nop(nofuse=True)
                    if 5 <= b <= 8:
                        for h in range(2 * (b - 5), 2 * (b - 4)):
                            top16(cand[:, h, :], rest[:, h % 2, :], sv[:, h], si[:, h])
                    if b == 9:
                        st.wait()
                        v.tensor_tensor(ex[:], sv[:], sv[:, :, 0:1].to_broadcast([P, PEER_HEADS, TOPK]), ALU.subtract).then_inc(exp_ready, 1)
                        flat = si[:].rearrange("p h k -> p (h k)")
                        st.done(v.tensor_single_scalar(pick[:, 0, :], flat, 4, op=ALU.logical_shift_right))
                        st.link(v.tensor_single_scalar(pick[:, 1, :], flat, TOPK - 1, op=ALU.bitwise_and))
                        st.link(v.tensor_copy(pickf, pick[:]))
                    if b in (10, 11):
                        choose(b - 10)
                    if b == 11:
                        dve.wait_ge(exp_done, t + 1)
                        st.link(v.tensor_reduce(den[:], ex[:], AX.X, ALU.add))
                        st.link(v.reciprocal(rden[:], den[:]))
                        v.tensor_tensor(gate[:], ex[:], rden[:].unsqueeze(2).to_broadcast([P, PEER_HEADS, TOPK]), ALU.mult).then_inc(ready, 1)
                    if b == 13:
                        dve.wait_ge(t_taken, t + 2)
                    for q in quads(b):
                        j, n, t0 = q % 2, q // 2, q * QUAD
                        dve.wait_ge(made[j], t * (NQ // 2) + (n + 1))
                        v.tensor_tensor(oh1[:, j], iota.unsqueeze(1).to_broadcast([P, QUAD, P]),
                                        tops[:, 0, t0:t0 + QUAD].unsqueeze(2).to_broadcast([P, QUAD, P]), ALU.is_equal).then_inc(one1[j], 1)
                        for k in range(QUAD):
                            last = v.tensor_scalar(oh2[:, j, k, :], iota, tops[:, 1, t0 + k:t0 + k + 1], tops[:, 2, t0 + k:t0 + k + 1],
                                                   ALU.is_equal, ALU.mult)
                        last.then_inc(one2[j], 1)
                st.close()
            for b in range(1, REST):
                split_lo(TILES, b)
    sm.close()


def experts_out_stage(nc, m, tag, v_dram, g_dram, a_dram, gate):
    sm = Sems(nc, tag)
    GRP = 4
    N_IT = P // (2 * GRP)
    v_full, g_full, v_hi, v_split, w_ready, w_hi, w_split, evac_done = (
        [sm(f"{x}{j}") for j in range(2)]
        for x in ("v_full", "g_full", "v_hi", "v_split", "w_ready", "w_hi", "w_split", "evac_done"))
    chunk_done = [[sm(f"chunk_done{g}{j}") for j in range(2)] for g in range(2)]
    with ExitStack() as es:
        sb = lambda n, shape, dt=F32: es.enter_context(nc.sbuf_tensor(tag + n, shape, dt))
        raw = sb("raw", [P, 2, D])
        vhi = sb("vhi", [P, 2 * GRP, D], F32R)
        vlo = sb("vlo", [P, 2 * GRP, D], F32R)
        ga = sb("ga", [P, 2, 2, T])
        w = sb("w", [P, 2, T])
        whi = sb("whi", [P, 2 * GRP, T], F32R)
        wlo = sb("wlo", [P, 2 * GRP, T], F32R)
        psums = [es.enter_context(nc.psum_tensor(f"{tag}ps{j}", [P, 2, 512], F32)) for j in range(2)]
        block = es.enter_context(nc.Block())

        @block.sync
        def _(sp):
            credit(sp, v_split + w_ready + w_split + evac_done + chunk_done[0] + chunk_done[1])
            with sp.Fori(0, N_IT) as i:
                for s in range(2 * GRP):
                    r, u = s % 2, i * GRP + s // 2
                    hold(sp, v_split[r], u + 1)
                    sp.dma_start(raw[:, r], v_dram[bass.ds(i * 2 * GRP + s, 1)].rearrange("o p n -> p (o n)")).then_inc(v_full[r], 16)
                    hold(sp, w_ready[r], u + 1)
                    for k, src in enumerate((g_dram, a_dram)):
                        sp.dma_start(ga[:, r, k], src[bass.ds(i * 2 * GRP + s, 1)].rearrange("o p n -> p (o n)")).then_inc(g_full[r], 16)

        @block.scalar
        def _(act):
            with act.Fori(0, N_IT) as i:
                for s in range(2 * GRP):
                    r, u = s % 2, i * GRP + s // 2
                    act.wait_ge(v_full[r], (u + 1) * 16)
                    act.wait_ge(chunk_done[s // GRP][1], i * (NC // 2) + 1)
                    nc.scalar.copy(vhi[:, s, :], raw[:, r, :]).then_inc(v_hi[r], 1)
                    act.wait_ge(w_ready[r], u + 2)
                    nc.scalar.copy(whi[:, s, :], w[:, r, :]).then_inc(w_hi[r], 1)

        @block.gpsimd
        def _(pool):
            with pool.Fori(0, N_IT) as i:
                for s in range(2 * GRP):
                    r, u = s % 2, i * GRP + s // 2
                    hold(pool, v_hi[r], u + 1)
                    nc.gpsimd.tensor_tensor(vlo[:, s, :], raw[:, r, :], vhi[:, s, :].bitcast(F32), ALU.subtract).then_inc(v_split[r], 1)

        @block.vector
        def _(dve):
            def prepare(i, s):
                r, u = s % 2, i * GRP + s // 2
                dve.wait_ge(g_full[r], (u + 1) * 32)
                dve.wait_ge(w_split[r], u + 1)
                nc.vector.tensor_tensor(w[:, r, :], ga[:, r, 0, :], ga[:, r, 1, :], ALU.mult).then_inc(w_ready[r], 1)
                dve.wait_ge(w_hi[r], u + 1)
                nc.vector.tensor_tensor(wlo[:, s, :], w[:, r, :], whi[:, s, :].bitcast(F32), ALU.subtract).then_inc(w_split[r], 1)

            def evacuate(i, grp, c):
                j, n = c % 2, (i * 2 + grp) * (NC // 2) + c // 2
                dve.wait_ge(chunk_done[grp][j], i * (NC // 2) + (c // 2 + 2))
                dve.wait_ge(evac_done[j], n + 1)
                for half, a, b, k in PIECES:
                    x = m["xT"][:, c, a:b]
                    last = nc.vector.scalar_tensor_tensor(out=x, in0=psums[j][:, half, a - half * HALF:b - half * HALF],
                                                          scalar=gate[:, c, k:k + 1], in1=x, op0=ALU.mult, op1=ALU.add)
                last.then_inc(evac_done[j], 1)

            for s in range(GRP):
                prepare(0, s)
            with dve.Fori(0, N_IT - 1) as i:
                for grp in range(2):
                    for b in range(GRP):
                        evacuate(i, grp, 2 * b)
                        evacuate(i, grp, 2 * b + 1)
                        prepare(i + grp, (1 - grp) * GRP + b)
            i = N_IT - 1
            for grp in range(2):
                for b in range(GRP):
                    if grp == 0:
                        prepare(i, GRP + b)
                for c in range(NC):
                    evacuate(i, grp, c)
            for j in range(2):
                dve.wait_ge(evac_done[j], N_IT * NC + 1)

        @block.tensor
        def _(pe):
            with pe.Fori(0, N_IT) as i:
                for grp in range(2):
                    for r in range(2):
                        u = i * GRP + (grp + 1) * (GRP // 2)
                        pe.wait_ge(w_split[r], u + 1)
                        pe.wait_ge(v_split[r], u + 1)
                    for c in range(NC):
                        j = c % 2
                        pe.wait_ge(evac_done[j], (i * 2 + grp) * (NC // 2) + (c // 2 + 1))
                        for k in range(2):
                            for q in range(GRP):
                                s = grp * GRP + q
                                for n, (x, y) in enumerate(((vhi, whi), (vhi, wlo), (vlo, whi))):
                                    mm = nc.tensor.matmul(psums[j][:, k, 0:HALF], x[:, s, c * P:(c + 1) * P], y[:, s, k * HALF:(k + 1) * HALF],
                                                          start=q == 0 and n == 0, stop=q == GRP - 1 and n == 2)
                        mm.then_inc(chunk_done[grp][j], 1)
    sm.close()


IDENT, IOTA, INCL, NMATS = 0, 1, 2, 4
STRICT, LEVEL = 0, 2
NMASKS = LEVEL + 2 * LEVELS


def constants():
    r, c = np.arange(P)[:, None], np.arange(P)[None, :]
    mats = [r == c, np.broadcast_to(c, (P, P)), r <= c, r >= c, r < c, r > c]
    for level in range(LEVELS):
        s = 1 << level
        pair = r // (2 * s) == c // (2 * s)
        lower = pair & (r // s % 2 == 1) & (c // s % 2 == 0)
        mats += [lower, lower.T]
    mats = np.stack(mats, 1).astype(np.float32)
    return np.ascontiguousarray(mats[:, :NMATS]), np.ascontiguousarray(mats[:, NMATS:])


def col_a(t):
    return t if t < S_CTX else t + PAD_A


def decay_stage(nc, m, d, hi, lo, lg, beta, gcol):
    sm = Sems(nc, "decay")
    full, wsplit, made, steps, act_steps, summed = (sm(x) for x in ("full", "wsplit", "made", "steps", "act_steps", "summed"))
    with nc.sbuf_tensor("wab", [P, NC, 16], F32) as wab, nc.sbuf_tensor("wabhi", [P, NC, 16], F32R) as wabhi, \
            nc.sbuf_tensor("wablo", [P, NC, 16], F32R) as wablo, nc.sbuf_tensor("alog", [P, 2, 8], F32) as alog, \
            nc.sbuf_tensor("alpha", [P, TILES, 8], F32) as alpha, nc.sbuf_tensor("abuf", [P, 3, TILES, 8], F32) as abuf, \
            nc.psum_tensor("abps", [P, TILES, 16], F32) as abps, nc.psum_tensor("gps", [P, TILES, 8], F32) as gps:
        with nc.Block() as block:
            @block.sync
            def _(sp):
                sp.dma_start(wab[:], d["w_ab"]).then_inc(full, 16)
                sp.dma_start(alog[:], d["alog"]).then_inc(full, 16)

            @block.tensor
            def _(pe):
                pe.wait_ge(wsplit, 2)
                for t in range(TILES):
                    for c in range(NC):
                        for n, (x, y) in enumerate(((hi, wabhi), (hi, wablo), (lo, wabhi))):
                            mm = nc.tensor.matmul(abps[:, t, :], x[:, c, t * P:(t + 1) * P], y[:, c, :],
                                                  start=c == 0 and n == 0, stop=c == NC - 1 and n == 2)
                mm.then_inc(made, 1)
                pe.wait_ge(steps, 5)
                for dr in range(2):
                    for t in range(TILES):
                        mm = nc.tensor.matmul(gps[:, t, dr * 4:dr * 4 + 4], m["mats"][:, INCL + dr, :], lg[:, t, dr * 4:dr * 4 + 4],
                                              start=True, stop=True)
                mm.then_inc(summed, 1)

            @block.scalar
            def _(act):
                st = Steps(act, act_steps)
                act.wait_ge(full, 32)
                nc.scalar.copy(wabhi[:], wab[:]).then_inc(wsplit, 1)
                act.wait_ge(steps, 1)
                st.link(nc.scalar.activation(abuf[:, 0], alpha[:], ACT.Abs))
                st.link(nc.scalar.activation(abuf[:, 0], abuf[:, 0], ACT.Exp, scale=-1.0))
                st.done(nc.scalar.activation(abuf[:, 1], abuf[:, 0], ACT.Ln, bias=1.0))
                st.done(nc.scalar.activation(abuf[:, 2, 0, :], alog[:, 0, :], ACT.Exp))
                st.done(nc.scalar.activation(beta[:], abps[:, :, 8:16], ACT.Sigmoid))
                st.wait()

            @block.vector
            def _(dve):
                st = Steps(dve, steps)
                dve.wait_ge(wsplit, 1)
                nc.vector.tensor_tensor(wablo[:], wab[:], wabhi[:].bitcast(F32), ALU.subtract).then_inc(wsplit, 1)
                dve.wait_ge(made, 1)
                st.link(nc.vector.tensor_tensor(alpha[:], abps[:, :, 0:8], alog[:, 1:2, :].to_broadcast([P, TILES, 8]), ALU.add))
                dve.wait_ge(act_steps, 1)
                st.link(nc.vector.tensor_scalar(alpha[:], alpha[:], 0.0, None, ALU.max))
                dve.wait_ge(act_steps, 5)
                st.link(nc.vector.tensor_tensor(alpha[:], alpha[:], abuf[:, 1], ALU.add))
                st.link(nc.vector.tensor_tensor(alpha[:], alpha[:], abuf[:, 2, 0:1, :].to_broadcast([P, TILES, 8]), ALU.mult))
                st.link(nc.vector.tensor_scalar(lg[:], alpha[:], -1.0, None, ALU.mult))
                dve.wait_ge(summed, 1)
                st.link(nc.vector.tensor_copy(gcol[:], gps[:]))
    sm.close()


def short_conv_stage(nc, m, d, src, dst):
    sm = Sems(nc, "conv")
    NB = 3 * HEADS
    N = LEN_A - TAPS_A + 1
    padded, full, conv, sq_ready, sq_used, var_ready, std_ready, inv_ready, normed, silued = (
        sm(x) for x in ("padded", "full", "conv", "sq_ready", "sq_used", "var_ready", "std_ready", "inv_ready", "normed", "silued"))
    with nc.sbuf_tensor("convw", [P, NB, TAPS_A], F32) as w, nc.sbuf_tensor("csq", [P, 2, N], F32) as sq, \
            nc.sbuf_tensor("cvar", [P, 2, T], F32) as var, nc.sbuf_tensor("cstd", [P, 2, T], F32) as std, \
            nc.psum_tensor("cA", [P, 512], F32) as cA, nc.psum_tensor("cB", [P, 512], F32) as cB, \
            nc.psum_tensor("cC", [P, 512], F32) as cC, nc.psum_tensor("cD", [P, 512], F32) as cD:
        psums = ((cA, cB), (cC, cD))
        with nc.Block() as block:
            @block.sync
            def _(sp):
                sp.dma_start(w[:], d["conv_w"]).then_inc(full, 16)

            @block.vector
            def _(dve):
                zeros = ((0, PAD_A), (PAD_A + S_CTX, 2 * PAD_A + S_CTX), (LEN_A - PAD_A, LEN_A))
                for a, e in zeros:
                    nc.vector.memset(src[:, :, a:e], 0.0).then_inc(padded, 1)
                dve.wait_ge(padded, 3)
                dve.wait_ge(full, 16)
                for tap in range(TAPS_A):
                    for b in range(NB):
                        x, wt = src[:, b, tap:tap + N], w[:, b, tap:tap + 1]
                        if tap == 0:
                            ins = nc.vector.tensor_scalar(dst[:, b, :], x, wt, None, ALU.mult)
                        else:
                            dve.wait_ge(conv, (tap - 1) * NB + b + 1)
                            ins = nc.vector.scalar_tensor_tensor(out=dst[:, b, :], in0=x, scalar=wt, in1=dst[:, b, :],
                                                                 op0=ALU.mult, op1=ALU.add)
                        ins.then_inc(conv, 1)
                for b in range(2 * HEADS):
                    j = b % 2
                    dve.wait_ge(sq_used, b + 1)
                    f = float(DK) if b < HEADS else 1.0
                    if b >= 2:
                        dve.wait_ge(std_ready, b - 1)
                    for (a0, a1), ps in zip(SEGS, psums[j]):
                        nc.vector.tensor_scalar(var[:, j, a0:a1], ps[:, 0:a1 - a0], f, f * EPS, ALU.mult, ALU.add).then_inc(var_ready, 1)
                    dve.wait_ge(std_ready, b + 1)
                    nc.vector.reciprocal(var[:, j, :], std[:, j, :]).then_inc(inv_ready, 1)
                    dve.wait_ge(inv_ready, b + 1)
                    for a0, a1 in SEGS:
                        x = dst[:, b, col_a(a0):col_a(a0) + a1 - a0]
                        nc.vector.tensor_tensor(x, x, var[:, j, a0:a1], ALU.mult).then_inc(normed, 1)
                dve.wait_ge(normed, 4 * HEADS)

            def root(act, b):
                act.wait_ge(var_ready, 2 * (b + 1))
                if b >= 2:
                    act.wait_ge(inv_ready, b - 1)
                nc.scalar.activation(std[:, b % 2, :], var[:, b % 2, :], ACT.Sqrt).then_inc(std_ready, 1)

            @block.scalar
            def _(act):
                for b in range(NB):
                    act.wait_ge(conv, NB * (TAPS_A - 1) + b + 1)
                    nc.scalar.activation(dst[:, b, :], dst[:, b, :], ACT.Silu).then_inc(silued, 1)
                for b in range(2 * HEADS):
                    act.wait_ge(silued, b + 1)
                    if b >= 2:
                        act.wait_ge(sq_used, b - 1)
                    nc.scalar.activation(sq[:, b % 2, :], dst[:, b, :], ACT.Square).then_inc(sq_ready, 1)
                    if b >= 1:
                        root(act, b - 1)
                root(act, 2 * HEADS - 1)
                act.wait_ge(silued, NB)

            @block.tensor
            def _(pe):
                for b in range(2 * HEADS):
                    pe.wait_ge(sq_ready, b + 1)
                    if b >= 2:
                        pe.wait_ge(var_ready, 2 * (b - 1))
                    for (a0, a1), ps in zip(SEGS, psums[b % 2]):
                        mm = nc.tensor.matmul(ps[:, 0:a1 - a0], m["ones"][:], sq[:, b % 2, col_a(a0):col_a(a0) + a1 - a0],
                                              start=True, stop=True)
                    mm.then_inc(sq_used, 1)
    sm.close()


def conformer_stage(nc, m, d, conf, hi, lo, first):
    sm = Sems(nc, "conf")
    NB = B_CH // P
    N = LEN_B - TAPS_B + 1
    full, sig, conv, sq_ready, sq_used, steps, act_steps, sum_done, centred, var_done, scaled, split = (
        sm(x) for x in ("full", "sig", "conv", "sq_ready", "sq_used", "steps", "act_steps", "sum_done", "centred",
                        "var_done", "scaled", "split"))
    with nc.sbuf_tensor("hh", [P, NB, LEN_B], F32) as hh, nc.sbuf_tensor("acc", [P, NB, N], F32) as acc, \
            nc.sbuf_tensor("bw", [P, NB, TAPS_B + 3], F32) as w, nc.sbuf_tensor("bsq", [P, 2, N], F32) as sq, \
            nc.sbuf_tensor("bmean", [P, N], F32) as mean, nc.sbuf_tensor("brstd", [P, N], F32) as rstd, \
            nc.sbuf_tensor("bout", [P, NB, T], F32) as out, \
            nc.psum_tensor("bA", [P, 512], F32) as bA, nc.psum_tensor("bB", [P, 512], F32) as bB:
        cols = ((0, 0, S_CTX), (S_CTX + PAD_B, S_CTX, T))
        with nc.Block() as block:
            @block.sync
            def _(sp):
                sp.dma_start(w[:], d["conf_w"]).then_inc(full, 16)

            @block.scalar
            def _(act):
                st = Steps(act, act_steps)
                for b in range(NB):
                    nc.scalar.activation(conf[:, NB + b, :], conf[:, NB + b, :], ACT.Sigmoid).then_inc(sig, 1)
                act.wait_ge(centred, NB)
                for b in range(NB):
                    if b >= 2:
                        act.wait_ge(sq_used, b - 1)
                    nc.scalar.activation(sq[:, b % 2, :], acc[:, b, :], ACT.Square).then_inc(sq_ready, 1)
                act.wait_ge(var_done, 2)
                st.link(nc.scalar.activation(mean[:], rstd[:], ACT.Sqrt))
                act.wait_ge(scaled, NB)
                for b in range(NB):
                    for c0, a, e in cols:
                        st.done(nc.scalar.activation(out[:, b, a:e], acc[:, b, c0:c0 + e - a], ACT.Silu))
                st.wait()
                for b in range(NB):
                    nc.scalar.copy(hi[:, first + b, :], out[:, b, :]).then_inc(split, 1)
                act.wait_ge(split, NB)

            @block.tensor
            def _(pe):
                for c0, a, e in cols:
                    ps = bA if a == 0 else bB
                    pe.wait_ge(conv, NB * (TAPS_B + 2) + 4)
                    for b in range(NB):
                        mm = nc.tensor.matmul(ps[:, 0:e - a], m["ones"][:], acc[:, b, c0:c0 + e - a], start=b == 0, stop=b == NB - 1)
                mm.then_inc(sum_done, 1)
                for b in range(NB):
                    pe.wait_ge(sq_ready, b + 1)
                    for c0, a, e in cols:
                        mm = nc.tensor.matmul((bA if a == 0 else bB)[:, 0:e - a], m["ones"][:], sq[:, b % 2, c0:c0 + e - a],
                                              start=b == 0, stop=b == NB - 1)
                    mm.then_inc(sq_used, 1)

            @block.vector
            def _(dve):
                st = Steps(dve, steps)
                v = nc.vector
                zeros = ((0, PAD_B), (PAD_B + S_CTX, 2 * PAD_B + S_CTX), (LEN_B - PAD_B, LEN_B))
                for a, e in zeros:
                    v.memset(hh[:, :, a:e], 0.0).then_inc(conv, 1)
                v.memset(rstd[:], 1.0).then_inc(conv, 1)
                dve.wait_ge(sig, NB)
                for b in range(NB):
                    for k, (a, e) in enumerate(SEGS):
                        c0 = a + PAD_B * (k + 1)
                        v.tensor_tensor(hh[:, b, c0:c0 + e - a], conf[:, b, a:e], conf[:, NB + b, a:e], ALU.mult).then_inc(conv, 1)
                dve.wait_ge(full, 16)
                base = 4 + 2 * NB
                dve.wait_ge(conv, base)
                for tap in range(TAPS_B):
                    for b in range(NB):
                        x, wt = hh[:, b, tap:tap + N], w[:, b, tap:tap + 1]
                        if tap == 0:
                            ins = v.tensor_scalar(acc[:, b, :], x, wt, w[:, b, TAPS_B:TAPS_B + 1], ALU.mult, ALU.add)
                        else:
                            dve.wait_ge(conv, base + (tap - 1) * NB + b + 1)
                            ins = v.scalar_tensor_tensor(out=acc[:, b, :], in0=x, scalar=wt, in1=acc[:, b, :], op0=ALU.mult, op1=ALU.add)
                        ins.then_inc(conv, 1)
                dve.wait_ge(conv, base + TAPS_B * NB)
                dve.wait_ge(sum_done, 1)
                for c0, a, e in cols:
                    st.done(v.tensor_scalar(mean[:, c0:c0 + e - a], (bA if a == 0 else bB)[:, 0:e - a], 1.0 / B_CH, None, ALU.mult))
                st.done(v.memset(mean[:, S_CTX:S_CTX + PAD_B], 0.0))
                st.wait()
                for b in range(NB):
                    v.tensor_tensor(acc[:, b, :], acc[:, b, :], mean[:], ALU.subtract).then_inc(centred, 1)
                dve.wait_ge(centred, NB)
                dve.wait_ge(sq_used, NB)
                for c0, a, e in cols:
                    v.tensor_scalar(rstd[:, c0:c0 + e - a], (bA if a == 0 else bB)[:, 0:e - a], 1.0 / B_CH, EPS,
                                    ALU.mult, ALU.add).then_inc(var_done, 1)
                dve.wait_ge(act_steps, 1)
                st.link(v.reciprocal(rstd[:], mean[:]))
                for b in range(NB):
                    st.done(v.tensor_tensor(acc[:, b, :], acc[:, b, :], rstd[:], ALU.mult))
                st.wait()
                for b in range(NB):
                    v.tensor_scalar(acc[:, b, :], acc[:, b, :], w[:, b, TAPS_B + 1:TAPS_B + 2], w[:, b, TAPS_B + 2:TAPS_B + 3],
                                    ALU.mult, ALU.add).then_inc(scaled, 1)
                for b in range(NB):
                    dve.wait_ge(split, b + 1)
                    st.done(v.tensor_tensor(lo[:, first + b, :], out[:, b, :], hi[:, first + b, :].bitcast(F32), ALU.subtract))
                st.wait()
    sm.close()


def tokens_stage(nc, m, qkv, tok):
    sm = Sems(nc, "tok")
    made, taken = ([sm(f"{x}{j}") for j in range(2)] for x in ("made", "taken"))
    with nc.psum_tensor("tA", [P, HEADS, P], F32) as tA, nc.psum_tensor("tB", [P, HEADS, P], F32) as tB:
        work = [(w, t) for w in range(2) for t in range(TILES)]
        with nc.Block() as block:
            @block.tensor
            def _(pe):
                for n, (w, t) in enumerate(work):
                    if n >= 2:
                        pe.wait_ge(taken[n % 2], n // 2)
                    c0 = col_a(t * P)
                    for h in range(HEADS):
                        mm = nc.tensor.transpose((tA, tB)[n % 2][:, h, :], qkv[:, (w + 1) * HEADS + h, c0:c0 + P], m["mats"][:, IDENT, :])
                    mm.then_inc(made[n % 2], 1)

            @block.scalar
            def _(act):
                for n, (w, t) in enumerate(work):
                    act.wait_ge(made[n % 2], n // 2 + 1)
                    nc.scalar.copy(tok[:, w, t], (tA, tB)[n % 2][:]).then_inc(taken[n % 2], 1)
                for j in range(2):
                    act.wait_ge(taken[j], len(work) // 2)
    sm.close()


def delta_stage(nc, m, d, qkv, tok, lg, beta, gcol, o_acc, state_out):
    sm = Sems(nc, "delta")
    names = ("full", "zeroed", "wide", "gsum", "prod", "diff", "gcopy", "exped", "decayed", "nmat", "ptmat", "scaled",
             "staged", "qt_mm", "qt", "xz_mm", "xz", "w_mm", "wneg", "u_mm", "u", "o_mm", "o_add", "s_mm", "s_new", "st_out", "small")
    full, zeroed, wide, gsum, prod, diff, gcopy, exped, decayed, nmat, ptmat, scaled, staged, qt_mm, qt_done, xz_mm, xz, w_mm, \
        wneg_done, u_mm, u_done, o_mm, o_add, s_mm, s_new, st_out, small = (sm(x) for x in names)
    masked_in = sm("masked_in")
    DH = 2 * HEADS
    with ExitStack() as es:
        sb = lambda n, shape, dt=F32: es.enter_context(nc.sbuf_tensor("dl_" + n, shape, dt))
        lgb, betab = sb("lgb", [P, DH, P]), sb("betab", [P, DH, P])
        egbc, dt_, nm, pt = sb("egbc", [P, DH, P]), sb("dt", [P, DH, P]), sb("nm", [P, DH, P]), sb("pt", [P, DH, P])
        X, Z, Qt = sb("X", [P, DH, P]), sb("Z", [P, DH, P]), sb("Qt", [P, DH, P])
        kb, vb, kdec, qdec = sb("kb", [P, DH, P]), sb("vb", [P, DH, P]), sb("kdec", [P, DH, P]), sb("qdec", [P, DH, P])
        wneg, u = lgb, betab
        states = (sb("sctx", [P, DH, P]), sb("sdec", [P, DH, P]))
        gl, kd, eg, egl, beg = (sb(n, [P, DH]) for n in ("gl", "kd", "eg", "egl", "beg"))
        masks = sb("masks", [P, NMASKS, P])
        banks = [es.enter_context(nc.psum_tensor(f"dl_ps{k}", [P, DH, P], F32)) for k in range(4)]
        gbc, bbc, kk, kq = banks
        ident = m["mats"][:, IDENT, :]
        mats = m["mats"]
        block = es.enter_context(nc.Block())
        units = [((t, TILES - t) if t else (0, 0), 1 if t else 0) for t in range(TILES)]
        heads = lambda dr: slice(dr * HEADS, (dr + 1) * HEADS)
        cols = lambda t: slice(col_a(t * P), col_a(t * P) + P)

        @block.sync
        def _(sp):
            sp.dma_start(masks[:], d["masks"]).then_inc(masked_in, 16)
            sp.dma_start(states[1][:], d["state"]).then_inc(full, 16)
            sp.wait_ge(s_new, DH)
            sp.dma_start(state_out.rearrange("k d v -> d k v"), states[0][:]).then_inc(st_out, 16)
            sp.wait_ge(st_out, 16)

        @block.tensor
        def _(pe):
            for n, (tiles, k) in enumerate(units):
                S = states[k]
                pe.wait_ge(wide, 4 * (n + 1))
                if n:
                    pe.wait_ge(o_add, 2 * n)
                    pe.wait_ge(s_new, DH * n)
                    pe.wait_ge(u_done, 2 * n)
                for dh in range(DH):
                    nc.tensor.matmul(gbc[:, dh, :], lgb[:, dh, :], mats[:, INCL + dh // HEADS, :], start=True, stop=True)
                    mm = nc.tensor.matmul(bbc[:, dh, :], betab[:, dh, :], ident, start=True, stop=True)
                mm.then_inc(gsum, 1)
                for dh in range(DH):
                    h, t = dh % HEADS, tiles[dh // HEADS]
                    kT = qkv[:, HEADS + h, cols(t)]
                    nc.tensor.matmul(kk[:, dh, :], kT, kT, start=True, stop=True)
                    mm = nc.tensor.matmul(kq[:, dh, :], kT, qkv[:, h, cols(t)], start=True, stop=True)
                mm.then_inc(prod, 1)
                for level in range(LEVELS):
                    a = n * LEVELS + level
                    pe.wait_ge(nmat, 4 * (n + 1))
                    pe.wait_ge(xz, 2 * (a + 1) + 2 * n)
                    for dh in range(DH):
                        mm = nc.tensor.matmul(gbc[:, dh, :], nm[:, dh, :], Z[:, dh, :], start=True, stop=True)
                    mm.then_inc(qt_mm, 1)
                    pe.wait_ge(qt_done, a + 1)
                    for dh in range(DH):
                        nc.tensor.matmul(bbc[:, dh, :], Qt[:, dh, :], X[:, dh, :], start=True, stop=True)
                        mm = nc.tensor.matmul(kk[:, dh, :], X[:, dh, :], Qt[:, dh, :], start=True, stop=True)
                    mm.then_inc(xz_mm, 1)
                pe.wait_ge(xz, 2 * (n + 1) * (LEVELS + 1))
                pe.wait_ge(scaled, 8 * (n + 1))
                pe.wait_ge(ptmat, n + 1)
                for dh in range(DH):
                    mm = nc.tensor.matmul(kq[:, dh, :], kb[:, dh, :], X[:, dh, :], start=True, stop=True)
                mm.then_inc(w_mm, 1)
                pe.wait_ge(wneg_done, n + 1)
                if n == 0:
                    pe.wait_ge(zeroed, 1)
                if n == 1:
                    pe.wait_ge(full, 16)
                for dh in range(DH):
                    nc.tensor.matmul(gbc[:, dh, :], X[:, dh, :], vb[:, dh, :], start=True, stop=False)
                    mm = nc.tensor.matmul(gbc[:, dh, :], wneg[:, dh, :], S[:, dh, :], start=False, stop=True)
                mm.then_inc(u_mm, 1)
                pe.wait_ge(u_done, 2 * (n + 1))
                for dh in range(DH):
                    nc.tensor.matmul(bbc[:, dh, :], S[:, dh, :], qdec[:, dh, :], start=True, stop=False)
                    mm = nc.tensor.matmul(bbc[:, dh, :], u[:, dh, :], pt[:, dh, :], start=False, stop=True)
                mm.then_inc(o_mm, 1)
                for dh in range(DH):
                    mm = nc.tensor.matmul(kk[:, dh, :], kdec[:, dh, :], u[:, dh, :], start=True, stop=True)
                mm.then_inc(s_mm, 1)

        @block.scalar
        def _(act):
            for n in range(TILES):
                act.wait_ge(gsum, n + 1)
                if n:
                    act.wait_ge(o_mm, n)
                act.wait_ge(decayed, 5 * n + 2)
                nc.scalar.activation(egbc[:], gbc[:], ACT.Exp).then_inc(exped, 1)
                act.wait_ge(gcopy, 3 * (n + 1))
                for x in (kd, eg, egl):
                    nc.scalar.activation(x[:], x[:], ACT.Exp).then_inc(exped, 1)
                act.wait_ge(diff, DH * (n + 1))
                nc.scalar.activation(dt_[:], dt_[:], ACT.Exp).then_inc(exped, 1)
                act.wait_ge(w_mm, n + 1)
                nc.scalar.mul(wneg[:], kq[:], -1.0).then_inc(wneg_done, 1)
                act.wait_ge(u_mm, n + 1)
                for dr in range(2):
                    nc.scalar.copy(u[:, heads(dr), :], gbc[:, heads(dr), :]).then_inc(u_done, 1)

        @block.gpsimd
        def _(pool):
            for n, (tiles, _) in enumerate(units):
                pool.wait_ge(small, n + 1)
                if n:
                    pool.wait_ge(s_mm, n)
                for dr in range(2):
                    t, hs = tiles[dr], heads(dr)
                    per = lambda x: x.unsqueeze(2).to_broadcast([P, HEADS, P])
                    nc.gpsimd.tensor_tensor(kb[:, hs, :], tok[:, 0, t], per(beg[:, hs]), ALU.mult).then_inc(scaled, 1)
                    nc.gpsimd.tensor_tensor(vb[:, hs, :], tok[:, 1, t], per(beta[:, t, hs]), ALU.mult).then_inc(scaled, 1)
                    nc.gpsimd.tensor_tensor(kdec[:, hs, :], tok[:, 0, t], per(kd[:, hs]), ALU.mult).then_inc(scaled, 1)
                    nc.gpsimd.tensor_tensor(qdec[:, hs, :], qkv[:, 0:HEADS, cols(t)], egbc[:, hs, :], ALU.mult).then_inc(scaled, 1)

        @block.vector
        def _(dve):
            v = nc.vector
            v.memset(states[0][:], 0.0).then_inc(zeroed, 1)
            v.memset(o_acc[:], 0.0).then_inc(zeroed, 1)
            dve.wait_ge(zeroed, 2)
            dve.wait_ge(masked_in, 16)
            for n, (tiles, k) in enumerate(units):
                S = states[k]
                for dr in range(2):
                    t, hs = tiles[dr], heads(dr)
                    for dst, src in ((lgb, lg), (betab, beta)):
                        v.tensor_copy(dst[:, hs, :], src[:, t, hs].unsqueeze(2).to_broadcast([P, HEADS, P])).then_inc(wide, 1)
                for x in (X, Z):
                    v.tensor_copy(x[:], ident.unsqueeze(1).to_broadcast([P, DH, P])).then_inc(xz, 1)
                dve.wait_ge(gsum, n + 1)
                for dh in range(DH):
                    t = tiles[dh // HEADS]
                    v.tensor_scalar(dt_[:, dh, :], gbc[:, dh, :], gcol[:, t, dh:dh + 1], 0.0, ALU.subtract, ALU.min).then_inc(diff, 1)
                v.tensor_copy(gl[:, 0:HEADS], gbc[:, 0:HEADS, P - 1]).then_inc(decayed, 1)
                v.tensor_copy(gl[:, HEADS:DH], gbc[:, HEADS:DH, 0]).then_inc(decayed, 1)
                for dr in range(2):
                    v.tensor_copy(eg[:, heads(dr)], gcol[:, tiles[dr], heads(dr)]).then_inc(decayed, 1)
                dve.wait_ge(decayed, 5 * n + 4)
                if n:
                    dve.wait_ge(scaled, 8 * n)
                v.tensor_tensor(kd[:], gl[:], eg[:], ALU.subtract).then_inc(gcopy, 1)
                v.tensor_copy(egl[:], gl[:]).then_inc(gcopy, 2)
                dve.wait_ge(exped, 5 * (n + 1))
                for dr in range(2):
                    v.tensor_tensor(beg[:, heads(dr)], eg[:, heads(dr)], beta[:, tiles[dr], heads(dr)], ALU.mult).then_inc(
                        *((small, 1) if dr else (decayed, 1)))
                masked = dt_[:].rearrange("p (r h) t -> p r h t", r=2)
                both = lambda a, mats=masks: mats[:, a:a + 2, :].unsqueeze(2).to_broadcast([P, 2, HEADS, P])
                v.tensor_tensor(masked, masked, both(INCL, m["mats"]), ALU.mult).then_inc(nmat, 1)
                dve.wait_ge(nmat, 4 * n + 1)
                dve.wait_ge(prod, n + 1)
                v.tensor_tensor(pt[:], dt_[:], kq[:], ALU.mult).then_inc(ptmat, 1)
                dve.wait_ge(ptmat, n + 1)
                v.tensor_tensor(dt_[:], dt_[:], kk[:], ALU.mult).then_inc(nmat, 1)
                dve.wait_ge(nmat, 4 * n + 2)
                v.tensor_tensor(masked, masked, both(STRICT), ALU.mult).then_inc(nmat, 1)
                dve.wait_ge(nmat, 4 * n + 3)
                v.tensor_tensor(nm[:], dt_[:], bbc[:], ALU.mult).then_inc(nmat, 1)
                for level in range(LEVELS):
                    a = n * LEVELS + level
                    dve.wait_ge(qt_mm, a + 1)
                    v.tensor_tensor(Qt[:].rearrange("p (r h) t -> p r h t", r=2), gbc[:].rearrange("p (r h) t -> p r h t", r=2),
                                    both(LEVEL + 2 * level), ALU.mult).then_inc(qt_done, 1)
                    dve.wait_ge(xz_mm, a + 1)
                    v.tensor_tensor(X[:], X[:], bbc[:], ALU.subtract).then_inc(xz, 1)
                    v.tensor_tensor(Z[:], Z[:], kk[:], ALU.subtract).then_inc(xz, 1)
                dve.wait_ge(o_mm, n + 1)
                for dr in range(2):
                    if n == 0 and dr:
                        dve.wait_ge(o_add, 1)
                    o = o_acc[:, :, tiles[dr] * P:(tiles[dr] + 1) * P]
                    v.tensor_tensor(o, o, bbc[:, heads(dr), :], ALU.add).then_inc(o_add, 1)
                if n == 1:
                    dve.wait_ge(full, 16)
                dve.wait_ge(s_mm, n + 1)
                for dh in range(DH):
                    v.scalar_tensor_tensor(out=S[:, dh, :], in0=S[:, dh, :], scalar=egl[:, dh:dh + 1], in1=kk[:, dh, :],
                                           op0=ALU.mult, op1=ALU.add).then_inc(s_new, 1)
                dve.wait_ge(s_new, DH * (n + 1))
                dve.wait_ge(o_add, 2 * (n + 1))
    sm.close()


def gated_norm_stage(nc, m, o_acc, z, hi, lo):
    sm = Sems(nc, "onorm")
    sq_ready, made, var_ready, std_ready, steps, out_ready, hi_ready, root_used = (
        sm(x) for x in ("sq_ready", "made", "var_ready", "std_ready", "steps", "out_ready", "hi_ready", "root_used"))
    with nc.sbuf_tensor("osq", [P, HEADS, T], F32) as sq, nc.sbuf_tensor("ovar", [P, HEADS, T], F32) as var, \
            nc.psum_tensor("oA", [P, 512], F32) as oA, nc.psum_tensor("oB", [P, 512], F32) as oB:
        with nc.Block() as block:
            @block.scalar
            def _(act):
                for h in range(HEADS):
                    nc.scalar.activation(sq[:, h, :], o_acc[:, h, :], ACT.Square).then_inc(sq_ready, 1)
                act.wait_ge(var_ready, 2 * HEADS)
                nc.scalar.activation(sq[:], var[:], ACT.Sqrt).then_inc(std_ready, 1)
                for h in range(HEADS):
                    act.wait_ge(out_ready, h + 1)
                    nc.scalar.copy(hi[:, h, :], o_acc[:, h, :]).then_inc(hi_ready, 1)

            @block.tensor
            def _(pe):
                for h in range(HEADS):
                    pe.wait_ge(sq_ready, h + 1)
                    if h:
                        pe.wait_ge(var_ready, 2 * h)
                    for (a, b), ps in zip(SEGS, (oA, oB)):
                        mm = nc.tensor.matmul(ps[:, 0:b - a], m["ones"][:], sq[:, h, a:b], start=True, stop=True)
                    mm.then_inc(made, 1)

            @block.vector
            def _(dve):
                st = Steps(dve, steps)
                v = nc.vector
                for h in range(HEADS):
                    dve.wait_ge(made, h + 1)
                    for (a, b), ps in zip(SEGS, (oA, oB)):
                        v.tensor_scalar(var[:, h, a:b], ps[:, 0:b - a], 1.0 / DK, EPS, ALU.mult, ALU.add).then_inc(var_ready, 1)
                dve.wait_ge(std_ready, 1)
                st.link(v.reciprocal(var[:], sq[:]))
                st.link(v.scalar_tensor_tensor(out=o_acc[:], in0=o_acc[:], scalar=m["gains"][:, NORM_A, 0:1], in1=var[:],
                                               op0=ALU.mult, op1=ALU.mult))
                for h in range(HEADS):
                    v.tensor_tensor(o_acc[:, h, :], o_acc[:, h, :], z[:, h, :], ALU.mult).then_inc(out_ready, 1)
                for h in range(HEADS):
                    dve.wait_ge(hi_ready, h + 1)
                    st.done(v.tensor_tensor(lo[:, h, :], o_acc[:, h, :], hi[:, h, :].bitcast(F32), ALU.subtract))
                st.wait()
    sm.close()


def fourier_stage(nc, m, d, hi, lo, out_hi, out_lo):
    sm = Sems(nc, "dft")
    full, dhi, dlo, one_mm, one_hi, one_lo, two_mm, two_hi, two_lo, two_out = (
        sm(x) for x in ("full", "dhi", "dlo", "one_mm", "one_hi", "one_lo", "two_mm", "two_hi", "two_lo", "two_out"))
    NCHAN, NCTX, NSEQ = 2 * P, 2 * P, 8 * S_DEC
    NALL = NCHAN + NCTX + NSEQ
    with ExitStack() as es:
        sb = lambda n, shape, dt=F32: es.enter_context(nc.sbuf_tensor("ft_" + n, shape, dt))
        dft, dfthi, dftlo = sb("dft", [P, NALL]), sb("dfthi", [P, NALL], F32R), sb("dftlo", [P, NALL], F32R)
        f1, f1hi, f1lo = sb("f1", [P, TILES, NCHAN]), sb("f1hi", [P, TILES, NCHAN], F32R), sb("f1lo", [P, TILES, NCHAN], F32R)
        f2 = sb("f2", [P, T])
        ps1 = [es.enter_context(nc.psum_tensor(f"ft_a{k}", [P, 2, NCHAN], F32)) for k in range(3)]
        psA = es.enter_context(nc.psum_tensor("ft_pa", [P, 128], F32))
        psB = es.enter_context(nc.psum_tensor("ft_pb", [P, 512], F32))
        block = es.enter_context(nc.Block())
        triple = lambda a, al, b, bl: ((a, b), (a, bl), (al, b))

        @block.sync
        def _(sp):
            sp.dma_start(dft[:], d["dft"]).then_inc(full, 16)

        @block.scalar
        def _(act):
            act.wait_ge(full, 16)
            nc.scalar.copy(dfthi[:], dft[:]).then_inc(dhi, 1)
            for g in range(NC):
                act.wait_ge(one_mm, g + 1)
                if g:
                    act.wait_ge(one_lo, g)
                for t in range(TILES):
                    nc.scalar.copy(f1[:, t, :], ps1[t // 2][:, t % 2, :]).then_inc(one_hi, 1)
                act.wait_ge(one_hi, 6 * g + 5)
                if g:
                    act.wait_ge(two_mm, g)
                nc.scalar.copy(f1hi[:], f1[:]).then_inc(one_hi, 1)
                act.wait_ge(two_mm, g + 1)
                if g:
                    act.wait_ge(two_lo, g)
                for (a, b), ps in zip(SEGS, (psA, psB)):
                    nc.scalar.copy(f2[:, a:b], ps[:, 0:b - a]).then_inc(two_out, 1)
                act.wait_ge(two_out, 2 * (g + 1))
                nc.scalar.copy(out_hi[:, g, :], f2[:]).then_inc(two_hi, 1)

        @block.vector
        def _(dve):
            dve.wait_ge(dhi, 1)
            nc.vector.tensor_tensor(dftlo[:], dft[:], dfthi[:].bitcast(F32), ALU.subtract).then_inc(dlo, 1)
            for g in range(NC):
                dve.wait_ge(one_hi, 6 * (g + 1))
                nc.vector.tensor_tensor(f1lo[:], f1[:], f1hi[:].bitcast(F32), ALU.subtract).then_inc(one_lo, 1)
                dve.wait_ge(two_hi, g + 1)
                nc.vector.tensor_tensor(out_lo[:, g, :], f2[:], out_hi[:, g, :].bitcast(F32), ALU.subtract).then_inc(two_lo, 1)
            dve.wait_ge(two_lo, NC)

        @block.tensor
        def _(pe):
            pe.wait_ge(dlo, 1)
            def channels(g):
                if g:
                    pe.wait_ge(one_hi, 6 * g - 1)
                for t in range(TILES):
                    for n, (x, y) in enumerate(triple(hi, lo, dfthi, dftlo)):
                        mm = nc.tensor.matmul(ps1[t // 2][:, t % 2, :], x[:, g, t * P:(t + 1) * P], y[:, 0:NCHAN],
                                              start=n == 0, stop=n == 2)
                mm.then_inc(one_mm, 1)

            channels(0)
            for g in range(NC):
                pe.wait_ge(one_lo, g + 1)
                if g:
                    pe.wait_ge(two_out, 2 * g)
                for k, ps in enumerate((psA, psB)):
                    tiles = range(1) if k == 0 else range(1, TILES)
                    prods = [(t, part, x, y) for t in tiles for part in range(2) for x, y in triple(f1hi, f1lo, dfthi, dftlo)]
                    for n, (t, part, x, y) in enumerate(prods):
                        if k == 0:
                            c0, w = NCHAN + part * P, P
                        else:
                            c0, w = NCHAN + NCTX + ((t - 1) * 2 + part) * S_DEC, S_DEC
                        mm = nc.tensor.matmul(ps[:, 0:w], x[:, t, part * P:(part + 1) * P], y[:, c0:c0 + w],
                                              start=n == 0, stop=n == len(prods) - 1)
                mm.then_inc(two_mm, 1)
                if g + 1 < NC:
                    channels(g + 1)
    sm.close()


NORM_A = 2 * DEPTH + 1


def build(nc, d, out, stop=None):
    with ExitStack() as top:
        sb = lambda es, n, shape, dt=F32: es.enter_context(nc.sbuf_tensor(n, shape, dt))
        m = {
            "xT": sb(top, "xT", [P, NC, T]),
            "mats": sb(top, "mats", [P, NMATS, P]),
            "ones": sb(top, "ones", [P, P]),
            "gains": sb(top, "gains", [P, 2 * DEPTH + 2, NC]),
            "mod": sb(top, "mod", [P, DEPTH, 6, NC, 2]),
            "amul": sb(top, "amul", [P, DEPTH, 2, NC, 2]),
        }
        hi, lo = sb(top, "hi", [P, NC, T], F32R), sb(top, "lo", [P, NC, T], F32R)
        q_dram = nc.dram_tensor("q_scratch", [NSC, P, T], F32, kind="Internal").ap()
        g_dram = nc.dram_tensor("g_scratch", [P, P, T], F32, kind="Internal").ap()
        a_dram = nc.dram_tensor("a_scratch", [P, P, T], F32, kind="Internal").ap()

        def norm(tag, l, n):
            norm_stage(nc, m, tag, lambda c, k: m["amul"][:, l, n, c, k:k + 1], lambda c, k: m["mod"][:, l, 3 * n, c, k:k + 1], (hi, lo))

        load_stage(nc, m, d)
        ada_stage(nc, m, d)
        if stop == "ada":
            return
        for l in range(DEPTH):
            norm(f"n1{l}", l, 0)
            if l % 2 == 0:
                even_mixer(nc, m, d, hi, lo, out["state"])
                w_out = d["w_out_ab"]
            else:
                fourier_stage(nc, m, d, hi, lo, hi, lo)
                w_out = d["w_out_c"]
            project_stage(nc, f"wo{l}", w_out, NC, hi, lo, False, add_to_x(nc, m, m["mod"][:, l, 2]))
            if stop == f"mix{l}":
                return
            norm(f"n2{l}", l, 1)
            peer(nc, m, d, f"p{l}", l, hi, lo, q_dram, g_dram, a_dram)
            if stop == f"peer{l}":
                return
        norm_stage(nc, m, "fin", lambda c, k: m["gains"][:, 2 * DEPTH, c:c + 1], lambda c, k: None, out["yT"])


def even_mixer(nc, m, d, hi, lo, state_out):
    with ExitStack() as es:
        sb = lambda e, n, shape, dt=F32: e.enter_context(nc.sbuf_tensor(n, shape, dt))
        qkv = sb(es, "qkv", [P, 3 * HEADS, LEN_A - TAPS_A + 1])
        z = sb(es, "z", [P, HEADS, T])
        lg, beta, gcol = (sb(es, n, [P, TILES, 2 * HEADS]) for n in ("lg", "beta", "gcol"))
        with ExitStack() as inner:
            raw = sb(inner, "qkvraw", [P, 3 * HEADS, LEN_A])
            conf = sb(inner, "conf", [P, 2 * B_CH // P, T])

            def padded(n, j, ps):
                for half, a, b, k in PIECES:
                    c0 = a + PAD_A * (k + 1)
                    last = nc.scalar.copy(raw[:, bass.ds(n, 1), c0:c0 + b - a].rearrange("p o t -> p (o t)"),
                                          ps[:, half, a - half * HALF:b - half * HALF])
                return last

            def silu_out(n, j, ps):
                return nc.scalar.activation(halves(z[:, bass.ds(n, 1), :].rearrange("p o t -> p (o t)")), ps[:, :, 0:HALF], ACT.Silu)

            project_stage(nc, "wqkv", d["w_qkv"], 3 * HEADS, hi, lo, True, padded)
            project_stage(nc, "wz", d["w_z"], HEADS, hi, lo, True, silu_out)
            project_stage(nc, "wcf", d["w_conf"], 2 * B_CH // P, hi, lo, True, copy_out(nc, conf))
            decay_stage(nc, m, d, hi, lo, lg, beta, gcol)
            short_conv_stage(nc, m, d, raw, qkv)
            conformer_stage(nc, m, d, conf, hi, lo, HEADS)
        with ExitStack() as inner:
            tok = sb(inner, "tok", [P, 2, TILES, HEADS, P])
            o_acc = sb(inner, "o_acc", [P, HEADS, T])
            tokens_stage(nc, m, qkv, tok)
            delta_stage(nc, m, d, qkv, tok, lg, beta, gcol, o_acc, state_out)
            gated_norm_stage(nc, m, o_acc, z, hi, lo)


def peer(nc, m, d, tag, l, hi, lo, q_dram, g_dram, a_dram):
    with nc.sbuf_tensor(tag + "q", [P, 2, T], F32) as q:
        def query_out(n, j, ps):
            return nc.scalar.copy(halves(q[:, j, :]), ps[:, :, 0:HALF])

        project_stage(nc, tag + "q", d["wq"][l], NSC, hi, lo, True, query_out, store=(q, q_dram))
    experts_in_stage(nc, m, tag + "u", d, l, hi, lo, q_dram, a_dram, g_dram)
    experts_out_stage(nc, m, tag + "v", d["v"][l], g_dram, a_dram, m["mod"][:, l, 5])


def blocks(w):
    w = np.asarray(w)
    *lead, k, n = w.shape
    w = w.reshape(*lead, k // P, P, n // P, P)
    return np.ascontiguousarray(np.moveaxis(w, -2, -4).swapaxes(-3, -2)).reshape(*lead, n // P, P, k)


def position_embedding():
    t = np.arange(S_DEC, dtype=np.float32)
    nf = D // 4
    freqs = np.exp(np.float32(-np.log(POS_BASE)) * np.arange(nf, dtype=np.float32) / np.float32(nf)).astype(np.float32)
    ar = ((t // GRID_W)[:, None] * freqs).astype(np.float32)
    ac = ((t % GRID_W)[:, None] * freqs).astype(np.float32)
    emb = np.concatenate([np.sin(ar), np.cos(ar), np.sin(ac), np.cos(ac)], 1).astype(np.float32)
    return chunked(emb.T)


def chunked(xT):
    return np.ascontiguousarray(xT.reshape(-1, P, xT.shape[1]).swapaxes(0, 1))


def dft_matrices():
    def pair(n, rows):
        a = 2 * np.pi * (np.outer(rows, np.arange(n)) % n) / n
        return np.cos(a) / np.sqrt(n), np.sin(a) / np.sqrt(n)
    c, s = pair(P, np.arange(P))
    parts = [c, -s, *pair(S_CTX, np.arange(S_CTX))]
    for t in range(S_DEC // P):
        parts += pair(S_DEC, np.arange(t * P, (t + 1) * P))
    return np.ascontiguousarray(np.concatenate(parts, 1).astype(np.float32))


def layout(x_prompt, x_sample, state_delta, c, c_ctx, ada_w, ada_b, norm1_g, norm2_g, w_in_ab, conv_qkv_w, a_log, dt_bias,
           delta_norm_g, conf_dw_w, conf_dw_b, conf_ln_g, conf_ln_b, w_out_ab, w_out_c, peer_wq, peer_k1, peer_k2,
           peer_u, peer_v, final_norm_g):
    A = HEADS * DK
    g = np.asarray
    col = lambda v: g(v).reshape(-1, P).T
    w_in = g(w_in_ab)[0]
    z0, ab0, cf0 = 3 * A, 4 * A, 4 * A + 4 * HEADS
    gains = np.stack([x for l in range(DEPTH) for x in (col(norm1_g[l]), col(norm2_g[l]))] + [col(final_norm_g)]
                     + [np.repeat(g(delta_norm_g)[0][:, None], NC, 1)], 1)
    keys = np.stack([g(peer_k1), g(peer_k2)], 2)
    u = g(peer_u).reshape(DEPTH, P, P, NC, P)
    v = g(peer_v).reshape(DEPTH, P, P, D)
    ac = np.ascontiguousarray
    return {
        "xT": chunked(np.concatenate([g(x_prompt)[0], g(x_sample)[0]], 0).T),
        "pos": position_embedding(),
        "mats": constants()[0],
        "masks": constants()[1],
        "dft": dft_matrices(),
        "gains": ac(gains),
        "cond": chunked(np.stack([g(c_ctx), g(c)[0]], 1)),
        "adab": ac(g(ada_b).reshape(DEPTH, 48, P).transpose(2, 0, 1)),
        "ada_w": ac(g(ada_w).reshape(DEPTH, NC, P, 12, 512).transpose(0, 3, 2, 1, 4)).reshape(DEPTH * 12, P, NC, 512),
        "w_qkv": blocks(w_in[:, 0:z0]),
        "w_z": blocks(w_in[:, z0:ab0]),
        "w_ab": chunked(w_in[:, ab0:cf0]),
        "w_conf": blocks(w_in[:, cf0:]),
        "alog": ac(np.broadcast_to(np.stack([g(a_log)[0].reshape(-1), g(dt_bias)[0].reshape(-1)]), (P, 2, 2 * HEADS))),
        "conv_w": chunked(g(conv_qkv_w)[0].T),
        "conf_w": chunked(np.concatenate([g(conf_dw_w)[0].T, g(conf_dw_b)[0][:, None], g(conf_ln_g)[0][:, None], g(conf_ln_b)[0][:, None]], 1)),
        "state": ac(g(state_delta)[0, 0].reshape(2 * HEADS, DK, DK).transpose(1, 0, 2)),
        "w_out_ab": blocks(g(w_out_ab)[0]),
        "w_out_c": blocks(g(w_out_c)[0]),
        "wq": blocks(peer_wq),
        "keys": ac(keys.transpose(0, 4, 1, 2, 3)).reshape(DEPTH, P, NSC, P),
        "u": ac(u.transpose(0, 2, 4, 3, 1)).reshape(DEPTH, P, P, D),
        "v": ac(v.transpose(0, 2, 1, 3)),
    }


def kernel(**inputs):
    import concourse.bacc as bacc
    from concourse.bass_utils import run_bass_kernel_spmd

    arrays = {f"in_{k}": a for k, a in layout(**inputs).items()}
    nc = bacc.Bacc("TRN2", target_bir_lowering=False, num_devices=1)
    d = {k[3:]: nc.dram_tensor(k, a.shape, mybir.dt.from_np(a.dtype), kind="ExternalInput").ap() for k, a in arrays.items()}
    out = {"yT": nc.dram_tensor("out_yT", (P, NC, T), F32, kind="ExternalOutput").ap(),
           "state": nc.dram_tensor("out_state", (2 * HEADS, DK, DK), F32, kind="ExternalOutput").ap()}
    build(nc, d, out)
    r = run_bass_kernel_spmd(nc, [arrays], core_ids=[0]).results[0]
    y = r["out_yT"].transpose(2, 1, 0).reshape(T, D)
    return (y[:S_CTX].reshape(1, S_CTX, D), y[S_CTX:].reshape(1, S_DEC, D),
            r["out_state"].reshape(1, 1, 2, HEADS, DK, DK))
```

```python
from contextlib import ExitStack

import numpy as np
import concourse.bass as bass
from concourse import mybir

F32 = mybir.dt.float32
F32R = mybir.dt.float32r
U32 = mybir.dt.uint32
ALU = mybir.AluOpType
ACT = mybir.ActivationFunctionType
AX = mybir.AxisListType

P = 128
D = 1024
NC = D // P
S_CTX, S_DEC = 128, 512
T = S_CTX + S_DEC
TILES = T // P
SEGS = ((0, S_CTX), (S_CTX, T))
HALF = T // 2
PIECES = ((0, 0, S_CTX, 0), (0, S_CTX, HALF, 1), (1, HALF, T, 1))
DEPTH = 2
EPS = 1e-6
HEADS = 4
DK = 128
TAPS_A = 7
TAPS_B = 31
PAD_A = TAPS_A // 2
PAD_B = TAPS_B // 2
LEN_A = T + 3 * PAD_A
LEN_B = T + 3 * PAD_B
B_CH = D // 2
PEER_HEADS = 8
TOPK = 16
NSC = 2 * PEER_HEADS
GRID_W = 64
POS_BASE = 10000.0
LEVELS = 7
NEG = -3.0e38


class Sems:

    def __init__(self, nc, stage):
        self.nc, self.stage, self.taken = nc, stage, []

    def __call__(self, name):
        self.taken.append(self.nc.alloc_semaphore(f"{self.stage}_{name}"))
        return self.taken[-1]

    def close(self):
        self.nc.clear_and_free_semaphores(self.taken)
        self.nc.all_engine_barrier()


class Steps:

    def __init__(self, eng, sem):
        self.eng, self.sem, self.n = eng, sem, 0

    def done(self, ins):
        ins.then_inc(self.sem, 1)
        self.n += 1
        return self.n

    def wait(self, n=None):
        self.eng.wait_ge(self.sem, self.n if n is None else n)

    def link(self, ins):
        self.done(ins)
        self.wait()


class LoopSteps(Steps):

    def __init__(self, eng, sem, t, per):
        super().__init__(eng, sem)
        self.t, self.per = t, per

    def wait(self, n=None):
        self.eng.wait_ge(self.sem, self.t * self.per + (self.n if n is None else n))

    def close(self):
        assert self.n == self.per, self.n


def hold(eng, sem, value):
    eng.wait_ge(sem, value)
    eng.nop(nofuse=True)


def load_stage(nc, m, d):
    sm = Sems(nc, "load")
    loaded, added = sm("loaded"), sm("added")
    with nc.sbuf_tensor("pos", [P, NC, S_DEC], F32) as pos:
        with nc.Block() as block:
            @block.sync
            def _(sp):
                for dst, src in ((m["xT"], d["xT"]), (m["mats"], d["mats"]), (m["gains"], d["gains"]),
                                 (pos, d["pos"])):
                    sp.dma_start(dst[:], src).then_inc(loaded, 16)

            @block.vector
            def _(dve):
                dve.wait_ge(loaded, 64)
                for c in range(NC):
                    x = m["xT"][:, c, S_CTX:T]
                    nc.vector.tensor_tensor(x, x, pos[:, c, :], ALU.add).then_inc(added, 1)
                nc.vector.memset(m["ones"][:], 1.0).then_inc(added, 1)
                dve.wait_ge(added, NC + 1)
    sm.close()


SLAB = 512
SLABS = 6 * D // SLAB
WINDOW = 2 * (2 * SLABS - 1)


class Modulation:

    def __init__(self, nc, sm, es, m, d, l, first, count):
        self.nc, self.m, self.d, self.l, self.first, self.count = nc, m, d, l, first, count
        self.full, self.used = ([sm(f"slab_{x}{j}") for j in range(2)] for x in ("full", "used"))
        self.rows_ready, self.turned, self.steps = sm("rows_ready"), sm("mod_turned"), sm("mod_steps")
        self.slab = es.enter_context(nc.sbuf_tensor(f"slab{l}{first}", [P, 2, NC, SLAB], F32))
        self.rows = es.enter_context(nc.sbuf_tensor(f"modrows{l}{first}", [P, SLAB], F32))
        self.sums = es.enter_context(nc.psum_tensor(f"modsums{l}{first}", [P, SLAB], F32))
        self.mod_ps = es.enter_context(nc.psum_tensor(f"modps{l}{first}", [P, SLAB // P, 2 * count], F32))

    def load(self, sp):
        for n in range(self.count):
            if n >= 2:
                sp.wait_ge(self.used[n % 2], n // 2)
            sp.dma_start(self.slab[:, n % 2], self.d["ada_w"][self.l * SLABS + self.first + n]).then_inc(self.full[n % 2], 16)

    def products(self, pe, slabs=None):
        for n in slabs or range(self.count):
            pe.wait_ge(self.full[n % 2], 16 * (n // 2 + 1))
            w0 = 2 * (SLABS - 1 - n)
            for c in range(NC):
                mm = self.nc.tensor.matmul(self.sums[0:2 * self.count, :], self.m["window"][:, c, w0:w0 + 2 * self.count],
                                           self.slab[:, n % 2, c, :], start=n == 0 and c == 0, stop=n == self.count - 1 and c == NC - 1)
            mm.then_inc(self.used[n % 2], 1)

    def take_rows(self, act):
        for s in self.used:
            act.wait_ge(s, self.count // 2)
        self.nc.scalar.copy(self.rows[0:2 * self.count, :], self.sums[0:2 * self.count, :]).then_inc(self.rows_ready, 1)

    def turn(self, pe):
        k = 2 * self.count
        pe.wait_ge(self.rows_ready, 1)
        for b in range(SLAB // P):
            mm = self.nc.tensor.transpose(self.mod_ps[:, b, :], self.rows[0:k, b * P:(b + 1) * P], self.m["mats"][0:k, IDENT, 0:k])
        mm.then_inc(self.turned, 1)

    def finish(self, dve):
        m, l, b = self.m, self.l, SLAB // P
        st = Steps(dve, self.steps)
        dve.wait_ge(self.turned, 1)
        cols = slice(b * self.first, b * (self.first + self.count))
        st.link(self.nc.vector.tensor_tensor(
            m["mod"][:, l].rearrange("p a c k -> p (a c) k")[:, cols].rearrange("p (n b) k -> p b n k", b=b),
            self.mod_ps[:].rearrange("p b (n k) -> p b n k", k=2),
            m["adab"][:, l, cols].rearrange("p (n b) -> p b n", b=b).unsqueeze(3).to_broadcast([P, b, self.count, 2]), ALU.add))
        parts = range(self.first * SLAB // D, (self.first + self.count) * SLAB // D)
        for n in range(2):
            if 1 + 3 * n in parts:
                st.link(self.nc.vector.scalar_tensor_tensor(
                    out=m["amul"][:, l, n], in0=m["mod"][:, l, 1 + 3 * n], scalar=1.0,
                    in1=m["gains"][:, 2 * l + n, :].unsqueeze(2).to_broadcast([P, NC, 2]), op0=ALU.add, op1=ALU.mult))


def ada_stage(nc, m, d):
    sm = Sems(nc, "ada")
    cond_full, cleared, cond_ready = sm("cond_full"), sm("cleared"), sm("cond_ready")
    with ExitStack() as es:
        cond = es.enter_context(nc.sbuf_tensor("cond", [P, NC, 2], F32))
        mod = Modulation(nc, sm, es, m, d, 0, 0, 2 * D // SLAB)
        block = es.enter_context(nc.Block())

        @block.sync
        def _(sp):
            sp.dma_start(cond[:], d["cond"]).then_inc(cond_full, 16)
            sp.dma_start(m["adab"][:], d["adab"]).then_inc(cond_full, 16)
            mod.load(sp)

        @block.scalar
        def _(act):
            act.wait_ge(cond_full, 32)
            act.wait_ge(cleared, 1)
            nc.scalar.activation(m["window"][:, :, WINDOW // 2 - 1:WINDOW // 2 + 1], cond[:], ACT.Silu).then_inc(cond_ready, 1)
            mod.take_rows(act)

        @block.tensor
        def _(pe):
            pe.wait_ge(cond_ready, 1)
            mod.products(pe)
            mod.turn(pe)

        @block.vector
        def _(dve):
            nc.vector.memset(m["window"][:], 0.0).then_inc(cleared, 1)
            mod.finish(dve)
    sm.close()


def sum_of_squares(nc, pe, ones, sq, sq_ready, sq_used, psums, n):
    for c in range(n):
        pe.wait_ge(sq_ready, c + 1)
        for (a, b), ps in zip(SEGS, psums):
            mm = nc.tensor.matmul(ps[:, 0:b - a], ones[:], sq[:, c % 2, a:b], start=c == 0, stop=c == n - 1)
        mm.then_inc(sq_used, 1)


def norm_stage(nc, m, tag, mul, add, out):
    sm = Sems(nc, tag)
    sq_ready, sq_used, var_ready, std_ready, steps = (sm(x) for x in ("sq_ready", "sq_used", "var_ready", "std_ready", "steps"))
    h_ready, hi_ready, h_used = sm("h_ready"), sm("hi_ready"), sm("h_used")
    xT = m["xT"]
    final = not isinstance(out, tuple)
    with nc.sbuf_tensor(tag + "sq", [P, 2, T], F32) as sq, nc.sbuf_tensor(tag + "var", [P, T], F32) as var, \
            nc.sbuf_tensor(tag + "rstd", [P, T], F32) as rstd, nc.sbuf_tensor(tag + "xn", [P, 2, T], F32) as xn, \
            nc.sbuf_tensor(tag + "h", [P, 2, T], F32) as h, \
            nc.psum_tensor(tag + "ssA", [P, 128], F32) as ssA, nc.psum_tensor(tag + "ssB", [P, 512], F32) as ssB:
        with nc.Block() as block:
            @block.scalar
            def _(act):
                for c in range(NC):
                    if c >= 2:
                        act.wait_ge(sq_used, c - 1)
                    nc.scalar.activation(sq[:, c % 2, :], xT[:, c, :], ACT.Square).then_inc(sq_ready, 1)
                act.wait_ge(var_ready, 2)
                nc.scalar.activation(rstd[:], var[:], ACT.Sqrt).then_inc(std_ready, 1)
                if not final:
                    for c in range(NC):
                        act.wait_ge(h_ready, 2 * (c + 1))
                        nc.scalar.copy(out[0][:, c, :], h[:, c % 2, :]).then_inc(hi_ready, 1)

            @block.tensor
            def _(pe):
                sum_of_squares(nc, pe, m["ones"], sq, sq_ready, sq_used, (ssA, ssB), NC)

            @block.vector
            def _(dve):
                st = Steps(dve, steps)
                dve.wait_ge(sq_used, NC)
                for (a, b), ps in zip(SEGS, (ssA, ssB)):
                    nc.vector.tensor_scalar(var[:, a:b], ps[:, 0:b - a], 1.0 / D, EPS, ALU.mult, ALU.add).then_inc(var_ready, 1)
                dve.wait_ge(std_ready, 1)
                st.link(nc.vector.reciprocal(var[:], rstd[:]))
                for c in range(NC):
                    st.link(nc.vector.tensor_tensor(xn[:, c % 2, :], xT[:, c, :], var[:], ALU.mult))
                    if c >= 2:
                        dve.wait_ge(h_used, (16 if final else 1) * (c - 1))
                    for k, (a, b) in enumerate(SEGS):
                        nc.vector.tensor_scalar(h[:, c % 2, a:b], xn[:, c % 2, a:b], mul(c, k), add(c, k),
                                                ALU.mult, ALU.add if add(c, k) is not None else ALU.bypass).then_inc(h_ready, 1)

            if final:
                @block.sync
                def _(sp):
                    for c in range(NC):
                        sp.wait_ge(h_ready, 2 * (c + 1))
                        sp.dma_start(out[:, c, :], h[:, c % 2, :]).then_inc(h_used, 16)
                        sp.wait_ge(h_used, 16 * (c + 1))
            else:
                @block.gpsimd
                def _(pool):
                    for c in range(NC):
                        pool.wait_ge(hi_ready, c + 1)
                        nc.gpsimd.tensor_tensor(out[1][:, c, :], h[:, c % 2, :], out[0][:, c, :].bitcast(F32),
                                                ALU.subtract).then_inc(h_used, 1)
                    pool.wait_ge(h_used, NC)
    sm.close()


def credit(eng, sems, n=1):
    for s in sems:
        eng.sem_inc(s, n)


def run_ahead(eng, n_it, prepare, take):
    prepare(0, 0)
    with eng.Fori(0, n_it - 1) as i:
        prepare(i, 1)
        take(i, 0)
        prepare(i + 1, 0)
        take(i, 1)
    prepare(n_it - 1, 1)
    take(n_it - 1, 0)
    take(n_it - 1, 1)


def block_products(nc, ps, j, whi, wlo, hi, lo, beside=()):
    beside, gap = list(beside), 2 * NC * 3 // max(len(beside), 1)
    for k in range(2):
        for c in range(NC):
            for n, (x, y) in enumerate(((whi, hi), (whi, lo), (wlo, hi))):
                if beside and ((k * NC + c) * 3 + n) % gap == gap - 1:
                    beside.pop(0)()
                mm = nc.tensor.matmul(ps[:, k, 0:HALF], x[:, j, c * P:(c + 1) * P], y[:, c, k * HALF:(k + 1) * HALF],
                                      start=c == 0 and n == 0, stop=c == NC - 1 and n == 2)
    return mm


def halves(x):
    return x.rearrange("p (k t) -> p k t", k=2)


def project_stage(nc, tag, w_dram, nb, hi, lo, on_act, evacuate, store=None, beside=None):
    sm = Sems(nc, tag)
    raw_full, hi_done, split, mm_done, evac_done = (
        [sm(f"{x}{j}") for j in range(2)] for x in ("raw_full", "hi_done", "split", "mm_done", "evac_done"))
    stored = [sm(f"stored{j}") for j in range(2)] if store is not None else None
    n_it = nb // 2
    other = beside(sm) if beside else None
    with nc.sbuf_tensor(tag + "raw", [P, 2, NC * P], F32) as raw, nc.sbuf_tensor(tag + "whi", [P, 2, NC * P], F32R) as whi, \
            nc.sbuf_tensor(tag + "wlo", [P, 2, NC * P], F32R) as wlo, \
            nc.psum_tensor(tag + "ps0", [P, 2, 512], F32) as ps0, nc.psum_tensor(tag + "ps1", [P, 2, 512], F32) as ps1:
        psums = (ps0, ps1)

        def take(eng, i, j):
            eng.wait_ge(mm_done[j], i + 2)
            if store is not None:
                eng.wait_ge(stored[j], (i + 1) * 16)
            eng.nop(nofuse=True)
            evacuate(i * 2 + j, j, psums[j]).then_inc(evac_done[j], 1)
            if store is not None:
                hold(eng, evac_done[j], i + 2)
                buf, dram = store
                eng.dma_start(dram[bass.ds(i * 2 + j, 1)].rearrange("o p n -> p (o n)"), buf[:, j]).then_inc(stored[j], 16)

        with nc.Block() as block:
            @block.sync
            def _(sp):
                credit(sp, split + mm_done + evac_done)
                if store is not None:
                    credit(sp, stored, 16)
                if other:
                    other.load(sp)
                with sp.Fori(0, n_it) as i:
                    for j in range(2):
                        hold(sp, split[j], i + 1)
                        sp.dma_start(raw[:, j], w_dram[bass.ds(i * 2 + j, 1)].rearrange("o p n -> p (o n)")).then_inc(raw_full[j], 16)

            @block.scalar
            def _(act):
                def split_hi(i, j):
                    act.wait_ge(raw_full[j], (i + 1) * 16)
                    act.wait_ge(mm_done[j], i + 1)
                    nc.scalar.copy(whi[:, j, :], raw[:, j, :]).then_inc(hi_done[j], 1)

                if on_act:
                    run_ahead(act, n_it, split_hi, lambda i, j: take(act, i, j))
                    for x in stored or ():
                        act.wait_ge(x, 16 * (n_it + 1))
                else:
                    with act.Fori(0, n_it) as i:
                        for j in range(2):
                            split_hi(i, j)

            @block.vector
            def _(dve):
                def split_lo(i, j):
                    dve.wait_ge(hi_done[j], i + 1)
                    nc.vector.tensor_tensor(wlo[:, j, :], raw[:, j, :], whi[:, j, :].bitcast(F32), ALU.subtract).then_inc(split[j], 1)

                if on_act:
                    if other:
                        other.start(dve)
                    with dve.Fori(0, n_it) as i:
                        for j in range(2):
                            split_lo(i, j)
                            if other:
                                other.step(dve, i, j)
                    if other:
                        other.finish(dve, n_it)
                else:
                    run_ahead(dve, n_it, split_lo, lambda i, j: take(dve, i, j))

            @block.tensor
            def _(pe):
                with pe.Fori(0, n_it) as i:
                    for j in range(2):
                        pe.wait_ge(split[j], i + 2)
                        pe.wait_ge(evac_done[j], i + 1)
                        block_products(nc, psums[j], j, whi, wlo, hi, lo).then_inc(mm_done[j], 1)
    sm.close()


def copy_out(nc, dst, first=0):
    def evacuate(n, j, ps):
        return nc.scalar.copy(halves(dst[:, bass.ds(n + first, 1), :].rearrange("p o t -> p (o t)")), ps[:, :, 0:HALF])
    return evacuate


def add_to_x(nc, m, gate):
    def evacuate(n, j, ps):
        for half, a, b, k in PIECES:
            x = m["xT"][:, bass.ds(n, 1), a:b].rearrange("p o t -> p (o t)")
            g = gate[:, bass.ds(n, 1), k:k + 1].rearrange("p o t -> p (o t)")
            last = nc.vector.scalar_tensor_tensor(out=x, in0=ps[:, half, a - half * HALF:b - half * HALF], scalar=g, in1=x,
                                                  op0=ALU.mult, op1=ALU.add)
        return last
    return evacuate


QUAD = 4
NQ = P // QUAD
QUADS = 5
STORES = 4
TILE_BLOCKS = 24
VEC_STEPS = 5 * NSC + 5 * PEER_HEADS + 13


def experts_in_stage(nc, m, tag, d, l, hi, lo, q_dram, a_dram, g_dram):
    sm = Sems(nc, tag)
    raw_full, hi_done, split, mm_done, evac_done, stored, one1, one2, made, taken = (
        [sm(f"{x}{j}") for j in range(2)]
        for x in ("raw_full", "hi_done", "split", "mm_done", "evac_done", "stored", "one1", "one2", "made", "taken"))
    keys_full, q_full, scored, s_taken, steps, exp_ready, exp_done, ready, turned, t_taken, g_stored = (
        sm(x) for x in ("keys_full", "q_full", "scored", "s_taken", "steps", "exp_ready", "exp_done", "ready", "turned",
                        "t_taken", "g_stored"))
    USES = TILE_BLOCKS // 2
    REST = P - TILES * TILE_BLOCKS
    with ExitStack() as es:
        sb = lambda n, shape, dt=F32: es.enter_context(nc.sbuf_tensor(tag + n, shape, dt))
        raw = sb("raw", [P, 2, D])
        whi, wlo = sb("whi", [P, 2, D], F32R), sb("wlo", [P, 2, D], F32R)
        a_out = sb("a_out", [P, 2, T])
        keys, qt = sb("keys", [P, NSC, P]), sb("qt", [P, NSC, P])
        sc = sb("sc", [P, NSC * P])
        eq = sc[:].rearrange("p (n a) -> p n a", a=TOPK)
        rest = sb("rest", [P, 2, 2 * P])
        val, idx, idxf = sb("val", [P, NSC, TOPK]), sb("idx", [P, NSC, TOPK], U32), sb("idxf", [P, NSC, TOPK])
        cand = sb("cand", [P, PEER_HEADS, TOPK * TOPK])
        sv, si = sb("sv", [P, PEER_HEADS, TOPK]), sb("si", [P, PEER_HEADS, TOPK], U32)
        pick = sb("pick", [P, 2, P], U32)
        pickf = rest[:, 0, :].rearrange("p (w n) -> p w n", w=2)
        rows = sb("rows", [P, 2, P])
        ex, gate = sb("ex", [P, PEER_HEADS, TOPK]), sb("gate", [P, PEER_HEADS, TOPK])
        den, rden = sb("den", [P, PEER_HEADS]), sb("rden", [P, PEER_HEADS])
        tops = sb("tops", [P, 3, P])
        oh1, oh2 = sb("oh1", [P, 2, QUAD, P]), sb("oh2", [P, 2, QUAD, P])
        g = sb("g", [P, P, P])
        psums = [es.enter_context(nc.psum_tensor(f"{tag}ps{j}", [P, 2, 512], F32)) for j in range(2)]
        bank = [es.enter_context(nc.psum_tensor(f"{tag}bank{k}", [P, QUAD, P], F32)) for k in range(4)]
        ident, iota = m["mats"][:, IDENT, :], m["mats"][:, IOTA, :]
        block = es.enter_context(nc.Block())

        def quads(b):
            return range(QUADS * (b - 13), min(QUADS * (b - 12), NQ)) if b >= 13 else range(0)

        @block.sync
        def _(sp):
            credit(sp, split + mm_done + evac_done + made + taken + [scored, ready, turned, t_taken])
            credit(sp, stored, 16)
            credit(sp, [g_stored], 16 * STORES)

            def load(t, b):
                j = b % 2
                hold(sp, split[j], t * USES + (b // 2 + 1))
                sp.dma_start(raw[:, j], d["u"][l][bass.ds(t * TILE_BLOCKS + b, 1)].rearrange("o p n -> p (o n)")).then_inc(raw_full[j], 16)

            with sp.Fori(0, TILES) as t:
                load(t, 0)
                load(t, 1)
                hold(sp, scored, t + 1)
                sp.dma_start(qt[:], q_dram[:, :, bass.ds(t * P, P)].rearrange("h p t -> p h t")).then_inc(q_full, 16)
                for b in range(2, TILE_BLOCKS):
                    load(t, b)
            for b in range(REST):
                load(TILES, b)

        @block.tensor
        def _(pe):
            def quad(t, q):
                j, n = q % 2, q // 2
                pe.wait_ge(one1[j], t * (NQ // 2) + (n + 1))
                pe.wait_ge(one2[j], t * (NQ // 2) + (n + 1))
                pe.wait_ge(taken[j], t * (NQ // 2) + (n + 1))
                for k in range(QUAD):
                    mm = nc.tensor.matmul(bank[j][:, k, :], oh1[:, j, k, :], oh2[:, j, k, :], start=True, stop=True)
                mm.then_inc(made[j], 1)

            def products(t, b):
                j = b % 2
                pe.wait_ge(split[j], t * USES + (b // 2 + 2))
                pe.wait_ge(evac_done[j], t * USES + (b // 2 + 1))
                block_products(nc, psums[j], j, whi, wlo, hi, lo, [lambda q=q: quad(t, q) for q in quads(b)]).then_inc(mm_done[j], 1)

            with pe.Fori(0, TILES) as t:
                for b in range(TILE_BLOCKS):
                    products(t, b)
                    if b == 0:
                        pe.wait_ge(keys_full, 16)
                        pe.wait_ge(q_full, (t + 1) * 16)
                        pe.wait_ge(t_taken, t + 1)
                        for j in range(2):
                            pe.wait_ge(taken[j], t * (NQ // 2) + 1)
                        for h in range(NSC):
                            mm = nc.tensor.matmul(bank[h // 4][:, h % 4, :], qt[:, h, :], keys[:, h, :], start=True, stop=True)
                        mm.then_inc(scored, 1)
                    if b == 12:
                        pe.wait_ge(ready, t + 2)
                        for w, src in enumerate((rows[:, 0, :], rows[:, 1, :], gate[:].rearrange("p h k -> p (h k)"))):
                            mm = nc.tensor.transpose(bank[2][:, w, :], src, ident)
                        mm.then_inc(turned, 1)
            for b in range(REST):
                products(TILES, b)

        @block.scalar
        def _(act):
            def split_hi(t, b):
                j, n = b % 2, b // 2
                act.wait_ge(raw_full[j], t * (16 * USES) + 16 * (n + 1))
                act.wait_ge(mm_done[j], t * USES + (n + 1))
                nc.scalar.copy(whi[:, j, :], raw[:, j, :]).then_inc(hi_done[j], 1)

            def take(t, b):
                j, n = b % 2, b // 2
                act.wait_ge(mm_done[j], t * USES + (n + 2))
                act.wait_ge(stored[j], t * (16 * USES) + 16 * (n + 1))
                nc.scalar.activation(halves(a_out[:, j, :]), psums[j][:, :, 0:HALF], ACT.Gelu_apprx_tanh).then_inc(evac_done[j], 1)
                hold(act, evac_done[j], t * USES + (n + 2))
                act.dma_start(a_dram[bass.ds(t * TILE_BLOCKS + b, 1)].rearrange("o p n -> p (o n)"), a_out[:, j]).then_inc(stored[j], 16)

            split_hi(0, 0)
            act.dma_start(keys[:], d["keys"][l]).then_inc(keys_full, 16)
            with act.Fori(0, TILES) as t:
                for b in range(TILE_BLOCKS):
                    split_hi(t, b + 1)
                    if b == 13:
                        act.wait_ge(g_stored, (t + 1) * (16 * STORES))
                    for q in quads(b):
                        j, n = q % 2, q // 2
                        act.wait_ge(made[j], t * (NQ // 2) + (n + 2))
                        nc.scalar.copy(g[:, :, q * QUAD:(q + 1) * QUAD].rearrange("p i t -> p t i"), bank[j][:]).then_inc(taken[j], 1)
                    take(t, b)
                    if b == 0:
                        act.wait_ge(ready, t + 1)
                        act.wait_ge(scored, t + 2)
                        for k in range(4):
                            nc.scalar.copy(sc[:, k * 512:(k + 1) * 512], bank[k][:].rearrange("p a b -> p (a b)")).then_inc(s_taken, 1)
                    if b == 9:
                        act.wait_ge(exp_ready, t + 1)
                        nc.scalar.activation(ex[:], ex[:], ACT.Exp).then_inc(exp_done, 1)
                    if b == 12:
                        act.wait_ge(turned, t + 2)
                        nc.scalar.copy(tops[:], bank[2][:, 0:3, :]).then_inc(t_taken, 1)
                    if b == TILE_BLOCKS - STORES:
                        for j in range(2):
                            hold(act, taken[j], t * (NQ // 2) + (NQ // 2 + 1))
                    if b >= TILE_BLOCKS - STORES:
                        i0 = (b - TILE_BLOCKS + STORES) * (P // STORES)
                        i1 = i0 + P // STORES
                        act.dma_start(g_dram[i0:i1, :, bass.ds(t * P, P)].rearrange("i p t -> p i t"), g[:, i0:i1]).then_inc(g_stored, 16)
            for b in range(REST):
                if b + 1 < REST:
                    split_hi(TILES, b + 1)
                take(TILES, b)
            for j in range(2):
                act.wait_ge(stored[j], 16 * (P // 2 + 1))
            act.wait_ge(g_stored, (16 * STORES) * (TILES + 1))

        @block.vector
        def _(dve):
            v = nc.vector

            def split_lo(t, b):
                j = b % 2
                dve.wait_ge(hi_done[j], t * USES + (b // 2 + 1))
                v.tensor_tensor(wlo[:, j, :], raw[:, j, :], whi[:, j, :].bitcast(F32), ALU.subtract).then_inc(split[j], 1)

            def one_hots(t, q):
                j, n, t0 = q % 2, q // 2, q * QUAD
                dve.wait_ge(made[j], t * (NQ // 2) + (n + 1))
                v.tensor_tensor(oh1[:, j], iota.unsqueeze(1).to_broadcast([P, QUAD, P]),
                                tops[:, 0, t0:t0 + QUAD].unsqueeze(2).to_broadcast([P, QUAD, P]), ALU.is_equal).then_inc(one1[j], 1)
                for k in range(QUAD):
                    last = v.tensor_scalar(oh2[:, j, k, :], iota, tops[:, 1, t0 + k:t0 + k + 1], tops[:, 2, t0 + k:t0 + k + 1],
                                           ALU.is_equal, ALU.mult)
                last.then_inc(one2[j], 1)

            split_lo(0, 0)
            with dve.Fori(0, TILES) as t:
                st = LoopSteps(dve, steps, t, VEC_STEPS)

                def top16(source, h0, out_v, out_i):
                    rows2 = [(source(h0 + e), rest[:, e, 0:source(h0 + e).shape[-1]], h0 + e) for e in range(2)]
                    for values, _, h in rows2:
                        st.done(v.max(out_v[:, h, 0:8], values))
                    st.wait()
                    dve.nop(nofuse=True)
                    for values, _, h in rows2:
                        st.done(v.max_index(out_i[:, h, 0:8], out_v[:, h, 0:8], values))
                    for values, scratch, h in rows2:
                        st.done(v.match_replace(scratch, out_v[:, h, 0:8], values, NEG))
                    st.wait()
                    dve.nop(nofuse=True)
                    for _, scratch, h in rows2:
                        st.done(v.max(out_v[:, h, 8:16], scratch))
                    st.wait()
                    dve.nop(nofuse=True)
                    for _, scratch, h in rows2:
                        st.done(v.max_index(out_i[:, h, 8:16], out_v[:, h, 8:16], scratch))

                def choose(w):
                    st.link(v.tensor_tensor(eq, pickf[:, w, :].unsqueeze(2).to_broadcast([P, P, TOPK]),
                                            iota[:, 0:TOPK].unsqueeze(1).to_broadcast([P, P, TOPK]), ALU.is_equal))
                    eq4 = eq.rearrange("p (h k) a -> p h k a", h=PEER_HEADS)
                    st.link(v.tensor_tensor(eq4, eq4, idxf[:, w:NSC:2, :].unsqueeze(2).to_broadcast([P, PEER_HEADS, TOPK, TOPK]), ALU.mult))
                    if w == 0:
                        dve.wait_ge(turned, t + 1)
                    st.link(v.tensor_reduce(rows[:, w, :], eq, AX.X, ALU.add))

                for b in range(TILE_BLOCKS):
                    if b == 13:
                        dve.wait_ge(t_taken, t + 2)
                    for q in quads(b)[:2]:
                        one_hots(t, q)
                    split_lo(t, b + 1)
                    if b == 1:
                        hold(dve, s_taken, (t + 1) * 4)
                    if 1 <= b <= 4:
                        for h in range(4 * (b - 1), 4 * b, 2):
                            top16(lambda h: sc[:, h * P:(h + 1) * P], h, val, idx)
                    if b == 5:
                        st.wait()
                        st.done(v.tensor_copy(idxf[:], idx[:]))
                        v1 = val[:, 0:NSC:2, :].unsqueeze(3).to_broadcast([P, PEER_HEADS, TOPK, TOPK])
                        v2 = val[:, 1:NSC:2, :].unsqueeze(2).to_broadcast([P, PEER_HEADS, TOPK, TOPK])
                        st.link(v.tensor_tensor(cand[:].rearrange("p h (a b) -> p h a b", a=TOPK), v1, v2, ALU.add))
                        dve.nop(nofuse=True)
                    if 5 <= b <= 8:
                        top16(lambda h: cand[:, h, :], 2 * (b - 5), sv, si)
                    if b == 9:
                        st.wait()
                        v.tensor_tensor(ex[:], sv[:], sv[:, :, 0:1].to_broadcast([P, PEER_HEADS, TOPK]), ALU.subtract).then_inc(exp_ready, 1)
                        flat = si[:].rearrange("p h k -> p (h k)")
                        st.done(v.tensor_single_scalar(pick[:, 0, :], flat, 4, op=ALU.logical_shift_right))
                        st.link(v.tensor_single_scalar(pick[:, 1, :], flat, TOPK - 1, op=ALU.bitwise_and))
                        st.link(v.tensor_copy(pickf, pick[:]))
                    if b in (10, 11):
                        choose(b - 10)
                    if b == 11:
                        dve.wait_ge(exp_done, t + 1)
                        st.link(v.tensor_reduce(den[:], ex[:], AX.X, ALU.add))
                        st.link(v.reciprocal(rden[:], den[:]))
                        v.tensor_tensor(gate[:], ex[:], rden[:].unsqueeze(2).to_broadcast([P, PEER_HEADS, TOPK]), ALU.mult).then_inc(ready, 1)
                    for q in quads(b)[2:]:
                        one_hots(t, q)
                st.close()
            for b in range(1, REST):
                split_lo(TILES, b)
    sm.close()


def experts_out_stage(nc, m, tag, v_dram, g_dram, a_dram, gate):
    sm = Sems(nc, tag)
    GRP = 4
    N_IT = P // (2 * GRP)
    v_full, g_full, v_hi, v_split, w_ready, w_hi, w_split, evac_done = (
        [sm(f"{x}{j}") for j in range(2)]
        for x in ("v_full", "g_full", "v_hi", "v_split", "w_ready", "w_hi", "w_split", "evac_done"))
    chunk_done = [[sm(f"chunk_done{g}{j}") for j in range(2)] for g in range(2)]
    with ExitStack() as es:
        sb = lambda n, shape, dt=F32: es.enter_context(nc.sbuf_tensor(tag + n, shape, dt))
        raw = sb("raw", [P, 2, D])
        vhi = sb("vhi", [P, 2 * GRP, D], F32R)
        vlo = sb("vlo", [P, 2 * GRP, D], F32R)
        ga = sb("ga", [P, 2, 2, T])
        w = sb("w", [P, 2, T])
        whi = sb("whi", [P, 2 * GRP, T], F32R)
        wlo = sb("wlo", [P, 2 * GRP, T], F32R)
        psums = [es.enter_context(nc.psum_tensor(f"{tag}ps{j}", [P, 2, 512], F32)) for j in range(2)]
        block = es.enter_context(nc.Block())

        @block.sync
        def _(sp):
            credit(sp, v_split + w_ready + w_split + evac_done + chunk_done[0] + chunk_done[1])
            with sp.Fori(0, N_IT) as i:
                for s in range(2 * GRP):
                    r, u = s % 2, i * GRP + s // 2
                    hold(sp, v_split[r], u + 1)
                    sp.dma_start(raw[:, r], v_dram[bass.ds(i * 2 * GRP + s, 1)].rearrange("o p n -> p (o n)")).then_inc(v_full[r], 16)
                    hold(sp, w_ready[r], u + 1)
                    for k, src in enumerate((g_dram, a_dram)):
                        sp.dma_start(ga[:, r, k], src[bass.ds(i * 2 * GRP + s, 1)].rearrange("o p n -> p (o n)")).then_inc(g_full[r], 16)

        @block.scalar
        def _(act):
            with act.Fori(0, N_IT) as i:
                for s in range(2 * GRP):
                    r, u = s % 2, i * GRP + s // 2
                    act.wait_ge(v_full[r], (u + 1) * 16)
                    act.wait_ge(chunk_done[s // GRP][1], i * (NC // 2) + 1)
                    nc.scalar.copy(vhi[:, s, :], raw[:, r, :]).then_inc(v_hi[r], 1)
                    act.wait_ge(w_ready[r], u + 2)
                    nc.scalar.copy(whi[:, s, :], w[:, r, :]).then_inc(w_hi[r], 1)

        @block.gpsimd
        def _(pool):
            with pool.Fori(0, N_IT) as i:
                for s in range(2 * GRP):
                    r, u = s % 2, i * GRP + s // 2
                    hold(pool, v_hi[r], u + 1)
                    nc.gpsimd.tensor_tensor(vlo[:, s, :], raw[:, r, :], vhi[:, s, :].bitcast(F32), ALU.subtract).then_inc(v_split[r], 1)

        @block.vector
        def _(dve):
            def prepare(i, s):
                r, u = s % 2, i * GRP + s // 2
                dve.wait_ge(g_full[r], (u + 1) * 32)
                dve.wait_ge(w_split[r], u + 1)
                nc.vector.tensor_tensor(w[:, r, :], ga[:, r, 0, :], ga[:, r, 1, :], ALU.mult).then_inc(w_ready[r], 1)
                dve.wait_ge(w_hi[r], u + 1)
                nc.vector.tensor_tensor(wlo[:, s, :], w[:, r, :], whi[:, s, :].bitcast(F32), ALU.subtract).then_inc(w_split[r], 1)

            def evacuate(i, grp, c):
                j, n = c % 2, (i * 2 + grp) * (NC // 2) + c // 2
                dve.wait_ge(chunk_done[grp][j], i * (NC // 2) + (c // 2 + 2))
                dve.wait_ge(evac_done[j], n + 1)
                for half, a, b, k in PIECES:
                    x = m["xT"][:, c, a:b]
                    last = nc.vector.scalar_tensor_tensor(out=x, in0=psums[j][:, half, a - half * HALF:b - half * HALF],
                                                          scalar=gate[:, c, k:k + 1], in1=x, op0=ALU.mult, op1=ALU.add)
                last.then_inc(evac_done[j], 1)

            for s in range(GRP):
                prepare(0, s)
            with dve.Fori(0, N_IT - 1) as i:
                for grp in range(2):
                    for b in range(GRP):
                        prepare(i + grp, (1 - grp) * GRP + b)
                        evacuate(i, grp, 2 * b)
                        evacuate(i, grp, 2 * b + 1)
            i = N_IT - 1
            for grp in range(2):
                for b in range(GRP):
                    if grp == 0:
                        prepare(i, GRP + b)
                    evacuate(i, grp, 2 * b)
                    evacuate(i, grp, 2 * b + 1)
            for j in range(2):
                dve.wait_ge(evac_done[j], N_IT * NC + 1)

        @block.tensor
        def _(pe):
            with pe.Fori(0, N_IT) as i:
                for grp in range(2):
                    for r in range(2):
                        u = i * GRP + (grp + 1) * (GRP // 2)
                        pe.wait_ge(w_split[r], u + 1)
                        pe.wait_ge(v_split[r], u + 1)
                    for c in range(NC):
                        j = c % 2
                        pe.wait_ge(evac_done[j], (i * 2 + grp) * (NC // 2) + (c // 2 + 1))
                        for k in range(2):
                            for q in range(GRP):
                                s = grp * GRP + q
                                for n, (x, y) in enumerate(((vhi, whi), (vhi, wlo), (vlo, whi))):
                                    mm = nc.tensor.matmul(psums[j][:, k, 0:HALF], x[:, s, c * P:(c + 1) * P], y[:, s, k * HALF:(k + 1) * HALF],
                                                          start=q == 0 and n == 0, stop=q == GRP - 1 and n == 2)
                        mm.then_inc(chunk_done[grp][j], 1)
    sm.close()


IDENT, IOTA, INCL, NMATS = 0, 1, 2, 4
STRICT, LEVEL = 0, 2
NMASKS = LEVEL + 2 * LEVELS


def constants():
    r, c = np.arange(P)[:, None], np.arange(P)[None, :]
    mats = [r == c, np.broadcast_to(c, (P, P)), r <= c, r >= c, r < c, r > c]
    for level in range(LEVELS):
        s = 1 << level
        pair = r // (2 * s) == c // (2 * s)
        lower = pair & (r // s % 2 == 1) & (c // s % 2 == 0)
        mats += [lower, lower.T]
    mats = np.stack(mats, 1).astype(np.float32)
    return np.ascontiguousarray(mats[:, :NMATS]), np.ascontiguousarray(mats[:, NMATS:])


def col_a(t):
    return t if t < S_CTX else t + PAD_A


def decay_stage(nc, m, d, hi, lo, lg, beta, gcol):
    sm = Sems(nc, "decay")
    full, wsplit, rows_made, rows_taken, made, steps, act_steps, summed = (
        sm(x) for x in ("full", "wsplit", "rows_made", "rows_taken", "made", "steps", "act_steps", "summed"))
    K = 4 * HEADS
    with nc.sbuf_tensor("wab", [P, NC, 16], F32) as wab, nc.sbuf_tensor("wabhi", [P, NC, 16], F32R) as wabhi, \
            nc.sbuf_tensor("wablo", [P, NC, 16], F32R) as wablo, nc.sbuf_tensor("alog", [P, 2, 8], F32) as alog, \
            nc.sbuf_tensor("alpha", [P, TILES, 8], F32) as alpha, nc.sbuf_tensor("abuf", [P, 3, TILES, 8], F32) as abuf, \
            nc.sbuf_tensor("abrows", [P, T], F32) as rows, nc.psum_tensor("abT", [P, 2, 512], F32) as abT, \
            nc.psum_tensor("abps", [P, TILES, 16], F32) as abps, nc.psum_tensor("gps", [P, TILES, 8], F32) as gps:
        with nc.Block() as block:
            @block.sync
            def _(sp):
                sp.dma_start(wab[:], d["w_ab"]).then_inc(full, 16)
                sp.dma_start(alog[:], d["alog"]).then_inc(full, 16)

            @block.tensor
            def _(pe):
                pe.wait_ge(wsplit, 2)
                for k in range(2):
                    for c in range(NC):
                        for n, (x, y) in enumerate(((wabhi, hi), (wabhi, lo), (wablo, hi))):
                            mm = nc.tensor.matmul(abT[0:K, k, 0:HALF], x[:, c, :], y[:, c, k * HALF:(k + 1) * HALF],
                                                  start=c == 0 and n == 0, stop=c == NC - 1 and n == 2)
                mm.then_inc(rows_made, 1)
                pe.wait_ge(rows_taken, 1)
                for t in range(TILES):
                    mm = nc.tensor.transpose(abps[:, t, :], rows[0:K, t * P:(t + 1) * P], m["mats"][0:K, IDENT, 0:K])
                mm.then_inc(made, 1)
                pe.wait_ge(steps, 5)
                for dr in range(2):
                    for t in range(TILES):
                        mm = nc.tensor.matmul(gps[:, t, dr * 4:dr * 4 + 4], m["mats"][:, INCL + dr, :], lg[:, t, dr * 4:dr * 4 + 4],
                                              start=True, stop=True)
                mm.then_inc(summed, 1)

            @block.scalar
            def _(act):
                st = Steps(act, act_steps)
                act.wait_ge(full, 32)
                nc.scalar.copy(wabhi[:], wab[:]).then_inc(wsplit, 1)
                act.wait_ge(rows_made, 1)
                nc.scalar.copy(halves(rows[0:K, :]), abT[0:K, :, 0:HALF]).then_inc(rows_taken, 1)
                act.wait_ge(steps, 1)
                st.link(nc.scalar.activation(abuf[:, 0], alpha[:], ACT.Abs))
                st.link(nc.scalar.activation(abuf[:, 0], abuf[:, 0], ACT.Exp, scale=-1.0))
                st.done(nc.scalar.activation(abuf[:, 1], abuf[:, 0], ACT.Ln, bias=1.0))
                st.done(nc.scalar.activation(abuf[:, 2, 0, :], alog[:, 0, :], ACT.Exp))
                st.done(nc.scalar.activation(beta[:], abps[:, :, 8:16], ACT.Sigmoid))
                st.wait()

            @block.vector
            def _(dve):
                st = Steps(dve, steps)
                dve.wait_ge(wsplit, 1)
                nc.vector.tensor_tensor(wablo[:], wab[:], wabhi[:].bitcast(F32), ALU.subtract).then_inc(wsplit, 1)
                dve.wait_ge(made, 1)
                st.link(nc.vector.tensor_tensor(alpha[:], abps[:, :, 0:8], alog[:, 1:2, :].to_broadcast([P, TILES, 8]), ALU.add))
                dve.wait_ge(act_steps, 1)
                st.link(nc.vector.tensor_scalar(alpha[:], alpha[:], 0.0, None, ALU.max))
                dve.wait_ge(act_steps, 5)
                st.link(nc.vector.tensor_tensor(alpha[:], alpha[:], abuf[:, 1], ALU.add))
                st.link(nc.vector.tensor_tensor(alpha[:], alpha[:], abuf[:, 2, 0:1, :].to_broadcast([P, TILES, 8]), ALU.mult))
                st.link(nc.vector.tensor_scalar(lg[:], alpha[:], -1.0, None, ALU.mult))
                dve.wait_ge(summed, 1)
                st.link(nc.vector.tensor_copy(gcol[:], gps[:]))
    sm.close()


class ShortConvolution:

    def __init__(self, nc, sm, d, src, dst, w):
        self.nc, self.d, self.src, self.dst, self.w = nc, d, src, dst, w
        self.full, self.padded, self.conv = sm("conv_full"), sm("padded"), sm("conv")

    def load(self, sp):
        sp.dma_start(self.w[:], self.d["conv_w"]).then_inc(self.full, 16)

    def start(self, dve):
        for a, e in ((0, PAD_A), (PAD_A + S_CTX, 2 * PAD_A + S_CTX), (LEN_A - PAD_A, LEN_A)):
            self.nc.vector.memset(self.src[:, :, a:e], 0.0).then_inc(self.padded, 1)
        dve.wait_ge(self.padded, 3)
        dve.wait_ge(self.full, 16)

    def step(self, dve, i, j):
        v, n = self.nc.vector, LEN_A - TAPS_A + 1
        half = (TAPS_A + 1) // 2
        for tap in range(j * half, min((j + 1) * half, TAPS_A)):
            if tap:
                hold(dve, self.conv, i * (2 * TAPS_A) + 2 * tap)
            for e in range(2):
                b = bass.ds(i * 2 + e, 1)
                flat = lambda ap: ap.rearrange("p o t -> p (o t)")
                x, wt, out = flat(self.src[:, b, tap:tap + n]), flat(self.w[:, b, tap:tap + 1]), flat(self.dst[:, b, :])
                if tap == 0:
                    ins = v.tensor_scalar(out, x, wt, None, ALU.mult)
                else:
                    ins = v.scalar_tensor_tensor(out=out, in0=x, scalar=wt, in1=out, op0=ALU.mult, op1=ALU.add)
                ins.then_inc(self.conv, 1)

    def finish(self, dve, n_it):
        dve.wait_ge(self.conv, n_it * 2 * TAPS_A)


EARLY_TAPS = 3


def qkv_norm_stage(nc, m, d, dst, zc, z, hh, acc, w):
    conf = zc[:, HEADS:, :]
    N_B = B_CH // P
    sm = Sems(nc, "conv")
    NB = 3 * HEADS
    N = LEN_A - TAPS_A + 1
    sq_ready, sq_used, var_ready, std_ready, inv_ready, normed, silued = (
        sm(x) for x in ("sq_ready", "sq_used", "var_ready", "std_ready", "inv_ready", "normed", "silued"))
    with nc.sbuf_tensor("csq", [P, 2, N], F32) as sq, \
            nc.sbuf_tensor("cvar", [P, 2, T], F32) as var, nc.sbuf_tensor("cstd", [P, 2, T], F32) as std, \
            nc.psum_tensor("cA", [P, 512], F32) as cA, nc.psum_tensor("cB", [P, 512], F32) as cB, \
            nc.psum_tensor("cC", [P, 512], F32) as cC, nc.psum_tensor("cD", [P, 512], F32) as cD, \
            ExitStack() as es:
        psums = ((cA, cB), (cC, cD))
        mod = Modulation(nc, sm, es, m, d, 0, 2 * D // SLAB, 4 * D // SLAB)
        w_full, sig, conv = sm("w_full"), sm("sig"), ConformerConvolution(nc, sm, hh, acc, w)
        with nc.Block() as block:
            @block.sync
            def _(sp):
                sp.dma_start(w[:], d["conf_w"]).then_inc(w_full, 16)
                mod.load(sp)

            @block.vector
            def _(dve):
                dve.wait_ge(sig, N_B)
                conv.gate(dve, conf)
                dve.wait_ge(w_full, 16)
                conv.taps(dve, range(EARLY_TAPS))
                for b in range(2 * HEADS):
                    j = b % 2
                    dve.wait_ge(sq_used, b + 1)
                    f = float(DK) if b < HEADS else 1.0
                    if b >= 2:
                        dve.wait_ge(std_ready, b - 1)
                    for (a0, a1), ps in zip(SEGS, psums[j]):
                        nc.vector.tensor_scalar(var[:, j, a0:a1], ps[:, 0:a1 - a0], f, f * EPS, ALU.mult, ALU.add).then_inc(var_ready, 1)
                    dve.wait_ge(std_ready, b + 1)
                    nc.vector.reciprocal(var[:, j, :], std[:, j, :]).then_inc(inv_ready, 1)
                    dve.wait_ge(inv_ready, b + 1)
                    for a0, a1 in SEGS:
                        x = dst[:, b, col_a(a0):col_a(a0) + a1 - a0]
                        nc.vector.tensor_tensor(x, x, var[:, j, a0:a1], ALU.mult).then_inc(normed, 1)
                    conv.taps(dve, range(EARLY_TAPS + b, EARLY_TAPS + b + 1))
                dve.wait_ge(normed, 4 * HEADS)
                mod.finish(dve)

            def root(act, b):
                act.wait_ge(var_ready, 2 * (b + 1))
                if b >= 2:
                    act.wait_ge(inv_ready, b - 1)
                nc.scalar.activation(std[:, b % 2, :], var[:, b % 2, :], ACT.Sqrt).then_inc(std_ready, 1)

            @block.scalar
            def _(act):
                for b in range(N_B):
                    nc.scalar.activation(conf[:, N_B + b, :], conf[:, N_B + b, :], ACT.Sigmoid).then_inc(sig, 1)
                for b in range(NB):
                    nc.scalar.activation(dst[:, b, :], dst[:, b, :], ACT.Silu).then_inc(silued, 1)
                nc.scalar.activation(z[:], zc[:, 0:HEADS, :], ACT.Silu).then_inc(silued, 1)
                for b in range(2 * HEADS):
                    act.wait_ge(silued, b + 1)
                    if b >= 2:
                        act.wait_ge(sq_used, b - 1)
                    nc.scalar.activation(sq[:, b % 2, :], dst[:, b, :], ACT.Square).then_inc(sq_ready, 1)
                    if b >= 1:
                        root(act, b - 1)
                root(act, 2 * HEADS - 1)
                mod.take_rows(act)
                act.wait_ge(silued, NB + 1)

            @block.tensor
            def _(pe):
                for b in range(2 * HEADS):
                    mod.products(pe, range(b, b + 1))
                    pe.wait_ge(sq_ready, b + 1)
                    if b >= 2:
                        pe.wait_ge(var_ready, 2 * (b - 1))
                    for (a0, a1), ps in zip(SEGS, psums[b % 2]):
                        mm = nc.tensor.matmul(ps[:, 0:a1 - a0], m["ones"][:], sq[:, b % 2, col_a(a0):col_a(a0) + a1 - a0],
                                              start=True, stop=True)
                    mm.then_inc(sq_used, 1)
                mod.turn(pe)
    sm.close()


class ConformerConvolution:

    def __init__(self, nc, sm, hh, acc, w):
        self.nc, self.hh, self.acc, self.w = nc, hh, acc, w
        self.sem, self.n = sm("conf_conv"), 0

    def gate(self, dve, conf):
        v, nb = self.nc.vector, B_CH // P
        for a, e in ((0, PAD_B), (PAD_B + S_CTX, 2 * PAD_B + S_CTX), (LEN_B - PAD_B, LEN_B)):
            v.memset(self.hh[:, :, a:e], 0.0).then_inc(self.sem, 1)
        for b in range(nb):
            for k, (a, e) in enumerate(SEGS):
                c0 = a + PAD_B * (k + 1)
                v.tensor_tensor(self.hh[:, b, c0:c0 + e - a], conf[:, b, a:e], conf[:, nb + b, a:e], ALU.mult).then_inc(self.sem, 1)
        self.n = 3 + 2 * nb
        dve.wait_ge(self.sem, self.n)

    def taps(self, dve, taps):
        v, nb, n = self.nc.vector, B_CH // P, LEN_B - TAPS_B + 1
        for tap in taps:
            for b in range(nb):
                x, wt, out = self.hh[:, b, tap:tap + n], self.w[:, b, tap:tap + 1], self.acc[:, b, :]
                if self.n >= nb:
                    dve.wait_ge(self.sem, self.n - nb + 1)
                if tap == 0:
                    ins = v.tensor_scalar(out, x, wt, self.w[:, b, TAPS_B:TAPS_B + 1], ALU.mult, ALU.add)
                else:
                    ins = v.scalar_tensor_tensor(out=out, in0=x, scalar=wt, in1=out, op0=ALU.mult, op1=ALU.add)
                ins.then_inc(self.sem, 1)
                self.n += 1


def conformer_stage(nc, m, d, out, hh, acc, w, hi, lo, first):
    sm = Sems(nc, "conf")
    NB = B_CH // P
    N = LEN_B - TAPS_B + 1
    taps_done, sq_ready, sq_used, steps, act_steps, sum_done, centred, var_done, scaled, split = (
        sm(x) for x in ("taps_done", "sq_ready", "sq_used", "steps", "act_steps", "sum_done", "centred",
                        "var_done", "scaled", "split"))
    with nc.sbuf_tensor("bsq", [P, 2, N], F32) as sq, \
            nc.sbuf_tensor("bmean", [P, N], F32) as mean, nc.sbuf_tensor("brstd", [P, N], F32) as rstd, \
            nc.psum_tensor("bA", [P, 512], F32) as bA, nc.psum_tensor("bB", [P, 512], F32) as bB, \
            ExitStack() as es:
        cols = ((0, 0, S_CTX), (S_CTX + PAD_B, S_CTX, T))
        conv = ConformerConvolution(nc, sm, hh, acc, w)
        mod = Modulation(nc, sm, es, m, d, 1, 0, SLABS)
        with nc.Block() as block:
            @block.sync
            def _(sp):
                mod.load(sp)

            @block.scalar
            def _(act):
                st = Steps(act, act_steps)
                act.wait_ge(centred, NB)
                for b in range(NB):
                    if b >= 2:
                        act.wait_ge(sq_used, b - 1)
                    nc.scalar.activation(sq[:, b % 2, :], acc[:, b, :], ACT.Square).then_inc(sq_ready, 1)
                act.wait_ge(var_done, 2)
                st.link(nc.scalar.activation(mean[:], rstd[:], ACT.Sqrt))
                act.wait_ge(scaled, NB)
                for b in range(NB):
                    for c0, a, e in cols:
                        st.done(nc.scalar.activation(out[:, b, a:e], acc[:, b, c0:c0 + e - a], ACT.Silu))
                st.wait()
                for b in range(NB):
                    nc.scalar.copy(hi[:, first + b, :], out[:, b, :]).then_inc(split, 1)
                mod.take_rows(act)
                act.wait_ge(split, NB)

            @block.tensor
            def _(pe):
                mod.products(pe, range(0, 8))
                pe.wait_ge(taps_done, 1)
                for c0, a, e in cols:
                    for b in range(NB):
                        mm = nc.tensor.matmul((bA if a == 0 else bB)[:, 0:e - a], m["ones"][:], acc[:, b, c0:c0 + e - a],
                                              start=b == 0, stop=b == NB - 1)
                mm.then_inc(sum_done, 1)
                mod.products(pe, range(8, 9))
                for b in range(NB):
                    pe.wait_ge(sq_ready, b + 1)
                    for c0, a, e in cols:
                        mm = nc.tensor.matmul((bA if a == 0 else bB)[:, 0:e - a], m["ones"][:], sq[:, b % 2, c0:c0 + e - a],
                                              start=b == 0, stop=b == NB - 1)
                    mm.then_inc(sq_used, 1)
                mod.products(pe, range(9, SLABS))
                mod.turn(pe)

            @block.vector
            def _(dve):
                st = Steps(dve, steps)
                v = nc.vector
                conv.taps(dve, range(EARLY_TAPS + 2 * HEADS, TAPS_B))
                dve.wait_ge(conv.sem, conv.n)
                v.memset(rstd[:], 1.0).then_inc(taps_done, 1)
                dve.wait_ge(sum_done, 1)
                for c0, a, e in cols:
                    st.done(v.tensor_scalar(mean[:, c0:c0 + e - a], (bA if a == 0 else bB)[:, 0:e - a], 1.0 / B_CH, None, ALU.mult))
                st.done(v.memset(mean[:, S_CTX:S_CTX + PAD_B], 0.0))
                st.wait()
                for b in range(NB):
                    v.tensor_tensor(acc[:, b, :], acc[:, b, :], mean[:], ALU.subtract).then_inc(centred, 1)
                dve.wait_ge(centred, NB)
                dve.wait_ge(sq_used, NB)
                for c0, a, e in cols:
                    v.tensor_scalar(rstd[:, c0:c0 + e - a], (bA if a == 0 else bB)[:, 0:e - a], 1.0 / B_CH, EPS,
                                    ALU.mult, ALU.add).then_inc(var_done, 1)
                dve.wait_ge(act_steps, 1)
                st.link(v.reciprocal(rstd[:], mean[:]))
                for b in range(NB):
                    st.done(v.tensor_tensor(acc[:, b, :], acc[:, b, :], rstd[:], ALU.mult))
                st.wait()
                for b in range(NB):
                    v.tensor_scalar(acc[:, b, :], acc[:, b, :], w[:, b, TAPS_B + 1:TAPS_B + 2], w[:, b, TAPS_B + 2:TAPS_B + 3],
                                    ALU.mult, ALU.add).then_inc(scaled, 1)
                for b in range(NB):
                    dve.wait_ge(split, b + 1)
                    st.done(v.tensor_tensor(lo[:, first + b, :], out[:, b, :], hi[:, first + b, :].bitcast(F32), ALU.subtract))
                st.wait()
                mod.finish(dve)
    sm.close()


def tokens_stage(nc, m, qkv, tok):
    sm = Sems(nc, "tok")
    made, taken = ([sm(f"{x}{j}") for j in range(2)] for x in ("made", "taken"))
    with nc.psum_tensor("tA", [P, HEADS, P], F32) as tA, nc.psum_tensor("tB", [P, HEADS, P], F32) as tB:
        work = [(w, t) for w in range(2) for t in range(TILES)]
        with nc.Block() as block:
            @block.tensor
            def _(pe):
                for n, (w, t) in enumerate(work):
                    if n >= 2:
                        pe.wait_ge(taken[n % 2], n // 2)
                    c0 = col_a(t * P)
                    for h in range(HEADS):
                        mm = nc.tensor.transpose((tA, tB)[n % 2][:, h, :], qkv[:, (w + 1) * HEADS + h, c0:c0 + P], m["mats"][:, IDENT, :])
                    mm.then_inc(made[n % 2], 1)

            @block.scalar
            def _(act):
                for n, (w, t) in enumerate(work):
                    act.wait_ge(made[n % 2], n // 2 + 1)
                    nc.scalar.copy(tok[:, w, t], (tA, tB)[n % 2][:]).then_inc(taken[n % 2], 1)
                for j in range(2):
                    act.wait_ge(taken[j], len(work) // 2)
    sm.close()


def delta_stage(nc, m, d, qkv, tok, lg, beta, gcol, o_acc, state_out):
    sm = Sems(nc, "delta")
    names = ("full", "zeroed", "wide", "gsum", "prod", "diff", "gcopy", "exped", "decayed", "nmat", "ptmat", "scaled",
             "qt_mm", "qt", "xz_mm", "xz", "w_mm", "wneg", "u_mm", "u", "o_mm", "o_add", "s_mm", "s_new", "st_out", "small")
    full, zeroed, wide, gsum, prod, diff, gcopy, exped, decayed, nmat, ptmat, scaled, qt_mm, qt_done, xz_mm, xz, w_mm, \
        wneg_done, u_mm, u_done, o_mm, o_add, s_mm, s_new, st_out, small = (sm(x) for x in names)
    masked_in, causal = sm("masked_in"), sm("causal")
    DH = 2 * HEADS
    with ExitStack() as es:
        sb = lambda n, shape, dt=F32: es.enter_context(nc.sbuf_tensor("dl_" + n, shape, dt))
        lgb, betab = sb("lgb", [P, DH, P]), sb("betab", [P, DH, P])
        egbc, dt_, nm, pt = sb("egbc", [P, DH, P]), sb("dt", [P, DH, P]), sb("nm", [P, DH, P]), sb("pt", [P, DH, P])
        X, Z, Qt = sb("X", [P, DH, P]), sb("Z", [P, DH, P]), sb("Qt", [P, DH, P])
        kb, vb, kdec, qdec = sb("kb", [P, DH, P]), sb("vb", [P, DH, P]), sb("kdec", [P, DH, P]), sb("qdec", [P, DH, P])
        wneg, u = dt_, egbc
        states = (sb("sctx", [P, DH, P]), sb("sdec", [P, DH, P]))
        gl, kd, eg, egl, beg = (sb(n, [P, DH]) for n in ("gl", "kd", "eg", "egl", "beg"))
        masks = sb("masks", [P, NMASKS, P])
        banks = [es.enter_context(nc.psum_tensor(f"dl_ps{k}", [P, DH, P], F32)) for k in range(4)]
        gbc, bbc, kk, kq = banks
        ident = m["mats"][:, IDENT, :]
        mats = m["mats"]
        block = es.enter_context(nc.Block())
        units = [((t, TILES - t) if t else (0, 0), 1 if t else 0) for t in range(TILES)]
        heads = lambda dr: slice(dr * HEADS, (dr + 1) * HEADS)
        both_dh = lambda dr: range(dr * HEADS, (dr + 1) * HEADS)
        cols = lambda t: slice(col_a(t * P), col_a(t * P) + P)

        def xz_count(n, level, dr):
            return 4 * (n * (LEVELS + 1) + level) + (2 * (dr + 1) if level else 4)

        @block.sync
        def _(sp):
            sp.dma_start(masks[:], d["masks"]).then_inc(masked_in, 16)
            sp.dma_start(states[1][:], d["state"]).then_inc(full, 16)
            sp.wait_ge(s_new, DH)
            sp.dma_start(state_out.rearrange("k d v -> d k v"), states[0][:]).then_inc(st_out, 16)
            sp.wait_ge(st_out, 16)

        @block.tensor
        def _(pe):
            for n, (tiles, k) in enumerate(units):
                S = states[k]
                pe.wait_ge(wide, 4 * (n + 1))
                if n:
                    pe.wait_ge(u_done, 2 * n)
                for dh in range(DH):
                    mm = nc.tensor.matmul(gbc[:, dh, :], lgb[:, dh, :], mats[:, INCL + dh // HEADS, :], start=True, stop=True)
                mm.then_inc(gsum, 1)
                if n:
                    pe.wait_ge(o_add, 2 * n)
                for dh in range(DH):
                    nc.tensor.matmul(bbc[:, dh, :], betab[:, dh, :], ident, start=True, stop=True)
                if n:
                    pe.wait_ge(s_new, DH * n)
                for dh in range(DH):
                    h, t = dh % HEADS, tiles[dh // HEADS]
                    kT = qkv[:, HEADS + h, cols(t)]
                    nc.tensor.matmul(kk[:, dh, :], kT, kT, start=True, stop=True)
                    mm = nc.tensor.matmul(kq[:, dh, :], kT, qkv[:, h, cols(t)], start=True, stop=True)
                mm.then_inc(prod, 1)
                pe.wait_ge(nmat, 4 * (n + 1))
                pe.wait_ge(exped, 5 * n + 2)
                for level in range(LEVELS):
                    a = n * LEVELS + level
                    for dr in range(2):
                        pe.wait_ge(xz, xz_count(n, level, dr))
                        for dh in both_dh(dr):
                            mm = nc.tensor.matmul(gbc[:, dh, :], nm[:, dh, :], Z[:, dh, :], start=True, stop=True)
                        mm.then_inc(qt_mm, 1)
                    for dr in range(2):
                        pe.wait_ge(qt_done, 2 * a + dr + 1)
                        for dh in both_dh(dr):
                            mm = nc.tensor.matmul(bbc[:, dh, :], Qt[:, dh, :], X[:, dh, :], start=True, stop=True)
                            if level < LEVELS - 1:
                                mm = nc.tensor.matmul(kk[:, dh, :], X[:, dh, :], Qt[:, dh, :], start=True, stop=True)
                        mm.then_inc(xz_mm, 1)
                pe.wait_ge(scaled, 8 * (n + 1))
                pe.wait_ge(ptmat, n + 1)
                for dr in range(2):
                    pe.wait_ge(xz, xz_count(n, LEVELS, dr))
                    for dh in both_dh(dr):
                        mm = nc.tensor.matmul(kq[:, dh, :], kb[:, dh, :], X[:, dh, :], start=True, stop=True)
                    mm.then_inc(w_mm, 1)
                if n == 0:
                    pe.wait_ge(zeroed, 1)
                if n == 1:
                    pe.wait_ge(full, 16)
                for dr in range(2):
                    pe.wait_ge(wneg_done, 2 * n + dr + 1)
                    for dh in both_dh(dr):
                        nc.tensor.matmul(gbc[:, dh, :], X[:, dh, :], vb[:, dh, :], start=True, stop=False)
                        mm = nc.tensor.matmul(gbc[:, dh, :], wneg[:, dh, :], S[:, dh, :], start=False, stop=True)
                    mm.then_inc(u_mm, 1)
                for dr in range(2):
                    pe.wait_ge(u_done, 2 * n + dr + 1)
                    for dh in both_dh(dr):
                        nc.tensor.matmul(bbc[:, dh, :], S[:, dh, :], qdec[:, dh, :], start=True, stop=False)
                        mm = nc.tensor.matmul(bbc[:, dh, :], u[:, dh, :], pt[:, dh, :], start=False, stop=True)
                    mm.then_inc(o_mm, 1)
                for dr in range(2):
                    for dh in both_dh(dr):
                        mm = nc.tensor.matmul(kk[:, dh, :], kdec[:, dh, :], u[:, dh, :], start=True, stop=True)
                    mm.then_inc(s_mm, 1)

        @block.scalar
        def _(act):
            for n in range(TILES):
                act.wait_ge(gsum, n + 1)
                if n:
                    act.wait_ge(o_mm, 2 * n)
                act.wait_ge(diff, DH * (n + 1))
                nc.scalar.activation(dt_[:], dt_[:], ACT.Exp).then_inc(exped, 1)
                act.wait_ge(decayed, 5 * n + 2)
                if n:
                    act.wait_ge(s_mm, 2 * n)
                nc.scalar.activation(egbc[:], gbc[:], ACT.Exp).then_inc(exped, 1)
                act.wait_ge(gcopy, 3 * (n + 1))
                for x in (kd, eg, egl):
                    nc.scalar.activation(x[:], x[:], ACT.Exp).then_inc(exped, 1)
                for dr in range(2):
                    act.wait_ge(w_mm, 2 * n + dr + 1)
                    nc.scalar.mul(wneg[:, heads(dr), :], kq[:, heads(dr), :], -1.0).then_inc(wneg_done, 1)
                for dr in range(2):
                    act.wait_ge(u_mm, 2 * n + dr + 1)
                    nc.scalar.copy(u[:, heads(dr), :], gbc[:, heads(dr), :]).then_inc(u_done, 1)

        @block.gpsimd
        def _(pool):
            for n, (tiles, _) in enumerate(units):
                pool.wait_ge(small, n + 1)
                if n:
                    pool.wait_ge(s_mm, 2 * n)
                for dr in range(2):
                    t, hs = tiles[dr], heads(dr)
                    per = lambda x: x.unsqueeze(2).to_broadcast([P, HEADS, P])
                    nc.gpsimd.tensor_tensor(kb[:, hs, :], tok[:, 0, t], per(beg[:, hs]), ALU.mult).then_inc(scaled, 1)
                    nc.gpsimd.tensor_tensor(vb[:, hs, :], tok[:, 1, t], per(beta[:, t, hs]), ALU.mult).then_inc(scaled, 1)
                    nc.gpsimd.tensor_tensor(kdec[:, hs, :], tok[:, 0, t], per(kd[:, hs]), ALU.mult).then_inc(scaled, 1)
                    nc.gpsimd.tensor_tensor(qdec[:, hs, :], qkv[:, 0:HEADS, cols(t)], egbc[:, hs, :], ALU.mult).then_inc(scaled, 1)

        @block.vector
        def _(dve):
            v = nc.vector

            def widen(tiles):
                for dr in range(2):
                    t, hs = tiles[dr], heads(dr)
                    for dst, src in ((lgb, lg), (betab, beta)):
                        v.tensor_copy(dst[:, hs, :], src[:, t, hs].unsqueeze(2).to_broadcast([P, HEADS, P])).then_inc(wide, 1)

            widen(units[0][0])
            v.memset(states[0][:], 0.0).then_inc(zeroed, 1)
            v.memset(o_acc[:], 0.0).then_inc(zeroed, 1)
            dve.wait_ge(zeroed, 2)
            dve.wait_ge(masked_in, 16)
            for n, (tiles, k) in enumerate(units):
                S = states[k]
                dve.wait_ge(gsum, n + 1)
                for dh in range(DH):
                    t = tiles[dh // HEADS]
                    v.tensor_scalar(dt_[:, dh, :], gbc[:, dh, :], gcol[:, t, dh:dh + 1], 0.0, ALU.subtract, ALU.min).then_inc(diff, 1)
                v.tensor_copy(gl[:, 0:HEADS], gbc[:, 0:HEADS, P - 1]).then_inc(decayed, 1)
                v.tensor_copy(gl[:, HEADS:DH], gbc[:, HEADS:DH, 0]).then_inc(decayed, 1)
                for dr in range(2):
                    v.tensor_copy(eg[:, heads(dr)], gcol[:, tiles[dr], heads(dr)]).then_inc(decayed, 1)
                dve.wait_ge(decayed, 5 * n + 4)
                if n:
                    dve.wait_ge(scaled, 8 * n)
                v.tensor_tensor(kd[:], gl[:], eg[:], ALU.subtract).then_inc(gcopy, 1)
                v.tensor_copy(egl[:], gl[:]).then_inc(gcopy, 2)
                for x in (X, Z):
                    v.tensor_copy(x[:], ident.unsqueeze(1).to_broadcast([P, DH, P])).then_inc(xz, 2)
                by_dir = lambda x: x[:].rearrange("p (r h) t -> p r h t", r=2)
                both = lambda a, mats=masks: mats[:, a:a + 2, :].unsqueeze(2).to_broadcast([P, 2, HEADS, P])
                dve.wait_ge(prod, n + 1)
                v.tensor_tensor(by_dir(nm), by_dir(kk), both(STRICT), ALU.mult).then_inc(nmat, 1)
                dve.wait_ge(nmat, 4 * n + 1)
                v.tensor_tensor(nm[:], nm[:], bbc[:], ALU.mult).then_inc(nmat, 1)
                dve.wait_ge(nmat, 4 * n + 2)
                dve.wait_ge(exped, 5 * n + 1)
                v.tensor_tensor(nm[:], nm[:], dt_[:], ALU.mult).then_inc(nmat, 2)
                dve.wait_ge(exped, 5 * (n + 1))
                for dr in range(2):
                    v.tensor_tensor(beg[:, heads(dr)], eg[:, heads(dr)], beta[:, tiles[dr], heads(dr)], ALU.mult).then_inc(
                        *((small, 1) if dr else (decayed, 1)))
                dve.wait_ge(nmat, 4 * n + 4)
                v.tensor_tensor(by_dir(dt_), by_dir(dt_), both(INCL, m["mats"]), ALU.mult).then_inc(causal, 1)
                dve.wait_ge(causal, n + 1)
                v.tensor_tensor(pt[:], dt_[:], kq[:], ALU.mult).then_inc(ptmat, 1)
                for level in range(LEVELS):
                    a = n * LEVELS + level
                    for dr in range(2):
                        hs = heads(dr)
                        dve.wait_ge(qt_mm, 2 * a + dr + 1)
                        mask = masks[:, LEVEL + 2 * level + dr, :].unsqueeze(1).to_broadcast([P, HEADS, P])
                        v.tensor_tensor(Qt[:, hs, :], gbc[:, hs, :], mask, ALU.mult).then_inc(qt_done, 1)
                    for dr in range(2):
                        hs = heads(dr)
                        dve.wait_ge(xz_mm, 2 * a + dr + 1)
                        dve.wait_ge(xz, xz_count(n, level, dr))
                        v.tensor_tensor(X[:, hs, :], X[:, hs, :], bbc[:, hs, :], ALU.subtract).then_inc(xz, 1 if level < LEVELS - 1 else 2)
                        if level < LEVELS - 1:
                            v.tensor_tensor(Z[:, hs, :], Z[:, hs, :], kk[:, hs, :], ALU.subtract).then_inc(xz, 1)
                if n + 1 < TILES:
                    widen(units[n + 1][0])
                for dr in range(2):
                    dve.wait_ge(o_mm, 2 * n + dr + 1)
                    if n == 0 and dr:
                        dve.wait_ge(o_add, 1)
                    o = o_acc[:, :, tiles[dr] * P:(tiles[dr] + 1) * P]
                    v.tensor_tensor(o, o, bbc[:, heads(dr), :], ALU.add).then_inc(o_add, 1)
                if n == 1:
                    dve.wait_ge(full, 16)
                for dh in range(DH):
                    dve.wait_ge(s_mm, 2 * n + dh // HEADS + 1)
                    v.scalar_tensor_tensor(out=S[:, dh, :], in0=S[:, dh, :], scalar=egl[:, dh:dh + 1], in1=kk[:, dh, :],
                                           op0=ALU.mult, op1=ALU.add).then_inc(s_new, 1)
                dve.wait_ge(s_new, DH * (n + 1))
                dve.wait_ge(o_add, 2 * (n + 1))
    sm.close()


def gated_norm_stage(nc, m, o_acc, z, hi, lo):
    sm = Sems(nc, "onorm")
    sq_ready, made, var_ready, std_ready, steps, out_ready, hi_ready, root_used = (
        sm(x) for x in ("sq_ready", "made", "var_ready", "std_ready", "steps", "out_ready", "hi_ready", "root_used"))
    with nc.sbuf_tensor("osq", [P, HEADS, T], F32) as sq, nc.sbuf_tensor("ovar", [P, HEADS, T], F32) as var, \
            nc.psum_tensor("oA", [P, 512], F32) as oA, nc.psum_tensor("oB", [P, 512], F32) as oB:
        with nc.Block() as block:
            @block.scalar
            def _(act):
                for h in range(HEADS):
                    nc.scalar.activation(sq[:, h, :], o_acc[:, h, :], ACT.Square).then_inc(sq_ready, 1)
                act.wait_ge(var_ready, 2 * HEADS)
                nc.scalar.activation(sq[:], var[:], ACT.Sqrt).then_inc(std_ready, 1)
                for h in range(HEADS):
                    act.wait_ge(out_ready, h + 1)
                    nc.scalar.copy(hi[:, h, :], o_acc[:, h, :]).then_inc(hi_ready, 1)

            @block.tensor
            def _(pe):
                for h in range(HEADS):
                    pe.wait_ge(sq_ready, h + 1)
                    if h:
                        pe.wait_ge(var_ready, 2 * h)
                    for (a, b), ps in zip(SEGS, (oA, oB)):
                        mm = nc.tensor.matmul(ps[:, 0:b - a], m["ones"][:], sq[:, h, a:b], start=True, stop=True)
                    mm.then_inc(made, 1)

            @block.vector
            def _(dve):
                st = Steps(dve, steps)
                v = nc.vector
                for h in range(HEADS):
                    dve.wait_ge(made, h + 1)
                    for (a, b), ps in zip(SEGS, (oA, oB)):
                        v.tensor_scalar(var[:, h, a:b], ps[:, 0:b - a], 1.0 / DK, EPS, ALU.mult, ALU.add).then_inc(var_ready, 1)
                dve.wait_ge(std_ready, 1)
                st.link(v.reciprocal(var[:], sq[:]))
                st.link(v.scalar_tensor_tensor(out=o_acc[:], in0=o_acc[:], scalar=m["gains"][:, NORM_A, 0:1], in1=var[:],
                                               op0=ALU.mult, op1=ALU.mult))
                for h in range(HEADS):
                    v.tensor_tensor(o_acc[:, h, :], o_acc[:, h, :], z[:, h, :], ALU.mult).then_inc(out_ready, 1)
                for h in range(HEADS):
                    dve.wait_ge(hi_ready, h + 1)
                    st.done(v.tensor_tensor(lo[:, h, :], o_acc[:, h, :], hi[:, h, :].bitcast(F32), ALU.subtract))
                st.wait()
    sm.close()


def fourier_stage(nc, m, d, hi, lo, out_hi, out_lo):
    sm = Sems(nc, "dft")
    full, dhi, dlo, one_mm, one_hi, one_lo, two_mm, two_hi, two_lo, two_out = (
        sm(x) for x in ("full", "dhi", "dlo", "one_mm", "one_hi", "one_lo", "two_mm", "two_hi", "two_lo", "two_out"))
    NCHAN, NCTX, NSEQ = 2 * P, 2 * P, 8 * S_DEC
    NALL = NCHAN + NCTX + NSEQ
    with ExitStack() as es:
        sb = lambda n, shape, dt=F32: es.enter_context(nc.sbuf_tensor("ft_" + n, shape, dt))
        dft, dfthi, dftlo = sb("dft", [P, NALL]), sb("dfthi", [P, NALL], F32R), sb("dftlo", [P, NALL], F32R)
        f1 = sb("f1", [P, TILES, NCHAN])
        f1hi, f1lo = sb("f1hi", [P, 2, TILES, NCHAN], F32R), sb("f1lo", [P, 2, TILES, NCHAN], F32R)
        f2 = sb("f2", [P, T])
        ps1 = [es.enter_context(nc.psum_tensor(f"ft_a{k}", [P, 2, NCHAN], F32)) for k in range(3)]
        psA = es.enter_context(nc.psum_tensor("ft_pa", [P, 128], F32))
        psB = es.enter_context(nc.psum_tensor("ft_pb", [P, 512], F32))
        block = es.enter_context(nc.Block())
        triple = lambda a, al, b, bl: ((a, b), (a, bl), (al, b))

        @block.sync
        def _(sp):
            sp.dma_start(dft[:], d["dft"]).then_inc(full, 16)

        @block.scalar
        def _(act):
            act.wait_ge(full, 16)
            nc.scalar.copy(dfthi[:], dft[:]).then_inc(dhi, 1)
            for g in range(NC + 1):
                if g < NC:
                    act.wait_ge(one_mm, g + 1)
                    if g:
                        act.wait_ge(one_lo, g)
                    for t in range(TILES):
                        nc.scalar.copy(f1[:, t, :], ps1[t // 2][:, t % 2, :]).then_inc(one_hi, 1)
                    act.wait_ge(one_hi, 6 * g + 5)
                    if g >= 2:
                        act.wait_ge(two_mm, g - 1)
                    nc.scalar.copy(f1hi[:, g % 2], f1[:]).then_inc(one_hi, 1)
                if g:
                    act.wait_ge(two_mm, g)
                    if g >= 2:
                        act.wait_ge(two_lo, g - 1)
                    for (a, b), ps in zip(SEGS, (psA, psB)):
                        nc.scalar.copy(f2[:, a:b], ps[:, 0:b - a]).then_inc(two_out, 1)
                    act.wait_ge(two_out, 2 * g)
                    nc.scalar.copy(out_hi[:, g - 1, :], f2[:]).then_inc(two_hi, 1)

        @block.vector
        def _(dve):
            dve.wait_ge(dhi, 1)
            nc.vector.tensor_tensor(dftlo[:], dft[:], dfthi[:].bitcast(F32), ALU.subtract).then_inc(dlo, 1)
            for g in range(NC + 1):
                if g < NC:
                    dve.wait_ge(one_hi, 6 * (g + 1))
                    nc.vector.tensor_tensor(f1lo[:, g % 2], f1[:], f1hi[:, g % 2].bitcast(F32), ALU.subtract).then_inc(one_lo, 1)
                if g:
                    dve.wait_ge(two_hi, g)
                    nc.vector.tensor_tensor(out_lo[:, g - 1, :], f2[:], out_hi[:, g - 1, :].bitcast(F32), ALU.subtract).then_inc(two_lo, 1)
            dve.wait_ge(two_lo, NC)

        @block.tensor
        def _(pe):
            pe.wait_ge(dlo, 1)
            def channels(g):
                if g:
                    pe.wait_ge(one_hi, 6 * g - 1)
                for t in range(TILES):
                    for n, (x, y) in enumerate(triple(hi, lo, dfthi, dftlo)):
                        mm = nc.tensor.matmul(ps1[t // 2][:, t % 2, :], x[:, g, t * P:(t + 1) * P], y[:, 0:NCHAN],
                                              start=n == 0, stop=n == 2)
                mm.then_inc(one_mm, 1)

            channels(0)
            for g in range(NC):
                if g + 1 < NC:
                    channels(g + 1)
                pe.wait_ge(one_lo, g + 1)
                if g:
                    pe.wait_ge(two_out, 2 * g)
                for k, ps in enumerate((psA, psB)):
                    tiles = range(1) if k == 0 else range(1, TILES)
                    prods = [(t, part, x, y) for t in tiles for part in range(2) for x, y in triple(f1hi, f1lo, dfthi, dftlo)]
                    for n, (t, part, x, y) in enumerate(prods):
                        if k == 0:
                            c0, w = NCHAN + part * P, P
                        else:
                            c0, w = NCHAN + NCTX + ((t - 1) * 2 + part) * S_DEC, S_DEC
                        mm = nc.tensor.matmul(ps[:, 0:w], x[:, g % 2, t, part * P:(part + 1) * P], y[:, c0:c0 + w],
                                              start=n == 0, stop=n == len(prods) - 1)
                mm.then_inc(two_mm, 1)
    sm.close()


NORM_A = 2 * DEPTH + 1


def build(nc, d, out, stop=None):
    with ExitStack() as top:
        sb = lambda es, n, shape, dt=F32: es.enter_context(nc.sbuf_tensor(n, shape, dt))
        m = {
            "xT": sb(top, "xT", [P, NC, T]),
            "mats": sb(top, "mats", [P, NMATS, P]),
            "ones": sb(top, "ones", [P, P]),
            "gains": sb(top, "gains", [P, 2 * DEPTH + 2, NC]),
            "mod": sb(top, "mod", [P, DEPTH, 6, NC, 2]),
            "amul": sb(top, "amul", [P, DEPTH, 2, NC, 2]),
        }
        hi, lo = sb(top, "hi", [P, NC, T], F32R), sb(top, "lo", [P, NC, T], F32R)
        q_dram = nc.dram_tensor("q_scratch", [NSC, P, T], F32, kind="Internal").ap()
        g_dram = nc.dram_tensor("g_scratch", [P, P, T], F32, kind="Internal").ap()
        a_dram = nc.dram_tensor("a_scratch", [P, P, T], F32, kind="Internal").ap()

        def norm(tag, l, n):
            norm_stage(nc, m, tag, lambda c, k: m["amul"][:, l, n, c, k:k + 1], lambda c, k: m["mod"][:, l, 3 * n, c, k:k + 1], (hi, lo))

        load_stage(nc, m, d)
        early = top.enter_context(ExitStack())
        m["window"], m["adab"] = sb(early, "window", [P, NC, WINDOW]), sb(early, "adab", [P, DEPTH, 6 * NC])
        ada_stage(nc, m, d)
        if stop == "ada":
            return
        for l in range(DEPTH):
            norm(f"n1{l}", l, 0)
            if l % 2 == 0:
                even_mixer(nc, m, d, hi, lo, out["state"])
                early.close()
                w_out = d["w_out_ab"]
            else:
                fourier_stage(nc, m, d, hi, lo, hi, lo)
                w_out = d["w_out_c"]
            project_stage(nc, f"wo{l}", w_out, NC, hi, lo, False, add_to_x(nc, m, m["mod"][:, l, 2]))
            if stop == f"mix{l}":
                return
            norm(f"n2{l}", l, 1)
            peer(nc, m, d, f"p{l}", l, hi, lo, q_dram, g_dram, a_dram)
            if stop == f"peer{l}":
                return
        norm_stage(nc, m, "fin", lambda c, k: m["gains"][:, 2 * DEPTH, c:c + 1], lambda c, k: None, out["yT"])


def even_mixer(nc, m, d, hi, lo, state_out):
    with ExitStack() as es:
        sb = lambda e, n, shape, dt=F32: e.enter_context(nc.sbuf_tensor(n, shape, dt))
        qkv = sb(es, "qkv", [P, 3 * HEADS, LEN_A - TAPS_A + 1])
        z = sb(es, "z", [P, HEADS, T])
        lg, beta, gcol = (sb(es, n, [P, TILES, 2 * HEADS]) for n in ("lg", "beta", "gcol"))
        with ExitStack() as inner:
            zc = sb(inner, "zc", [P, HEADS + 2 * B_CH // P, T])
            before = inner.enter_context(ExitStack())
            raw = sb(before, "qkvraw", [P, 3 * HEADS, LEN_A])
            taps = sb(before, "convw", [P, 3 * HEADS, TAPS_A])

            def padded(n, j, ps):
                for half, a, b, k in PIECES:
                    c0 = a + PAD_A * (k + 1)
                    last = nc.scalar.copy(raw[:, bass.ds(n, 1), c0:c0 + b - a].rearrange("p o t -> p (o t)"),
                                          ps[:, half, a - half * HALF:b - half * HALF])
                return last

            project_stage(nc, "wqkv", d["w_qkv"], 3 * HEADS, hi, lo, True, padded)
            project_stage(nc, "wzc", d["w_zc"], HEADS + 2 * B_CH // P, hi, lo, True, copy_out(nc, zc),
                          beside=lambda sm: ShortConvolution(nc, sm, d, raw, qkv, taps))
            before.close()
            decay_stage(nc, m, d, hi, lo, lg, beta, gcol)
            hh, acc = sb(inner, "hh", [P, B_CH // P, LEN_B]), sb(inner, "acc", [P, B_CH // P, LEN_B - TAPS_B + 1])
            w = sb(inner, "conf_w", [P, B_CH // P, TAPS_B + 3])
            qkv_norm_stage(nc, m, d, qkv, zc, z, hh, acc, w)
            conformer_stage(nc, m, d, zc[:, HEADS:HEADS + B_CH // P, :], hh, acc, w, hi, lo, HEADS)
        with ExitStack() as inner:
            tok = sb(inner, "tok", [P, 2, TILES, HEADS, P])
            o_acc = sb(inner, "o_acc", [P, HEADS, T])
            tokens_stage(nc, m, qkv, tok)
            delta_stage(nc, m, d, qkv, tok, lg, beta, gcol, o_acc, state_out)
            gated_norm_stage(nc, m, o_acc, z, hi, lo)


def peer(nc, m, d, tag, l, hi, lo, q_dram, g_dram, a_dram):
    with nc.sbuf_tensor(tag + "q", [P, 2, T], F32) as q:
        def query_out(n, j, ps):
            return nc.scalar.copy(halves(q[:, j, :]), ps[:, :, 0:HALF])

        project_stage(nc, tag + "q", d["wq"][l], NSC, hi, lo, True, query_out, store=(q, q_dram))
    experts_in_stage(nc, m, tag + "u", d, l, hi, lo, q_dram, a_dram, g_dram)
    experts_out_stage(nc, m, tag + "v", d["v"][l], g_dram, a_dram, m["mod"][:, l, 5])


def blocks(w):
    w = np.asarray(w)
    *lead, k, n = w.shape
    w = w.reshape(*lead, k // P, P, n // P, P)
    return np.ascontiguousarray(np.moveaxis(w, -2, -4).swapaxes(-3, -2)).reshape(*lead, n // P, P, k)


def position_embedding():
    t = np.arange(S_DEC, dtype=np.float32)
    nf = D // 4
    freqs = np.exp(np.float32(-np.log(POS_BASE)) * np.arange(nf, dtype=np.float32) / np.float32(nf)).astype(np.float32)
    ar = ((t // GRID_W)[:, None] * freqs).astype(np.float32)
    ac = ((t % GRID_W)[:, None] * freqs).astype(np.float32)
    emb = np.concatenate([np.sin(ar), np.cos(ar), np.sin(ac), np.cos(ac)], 1).astype(np.float32)
    return chunked(emb.T)


def chunked(xT):
    return np.ascontiguousarray(xT.reshape(-1, P, xT.shape[1]).swapaxes(0, 1))


def dft_matrices():
    def pair(n, rows):
        a = 2 * np.pi * (np.outer(rows, np.arange(n)) % n) / n
        return np.cos(a) / np.sqrt(n), np.sin(a) / np.sqrt(n)
    c, s = pair(P, np.arange(P))
    parts = [c, -s, *pair(S_CTX, np.arange(S_CTX))]
    for t in range(S_DEC // P):
        parts += pair(S_DEC, np.arange(t * P, (t + 1) * P))
    return np.ascontiguousarray(np.concatenate(parts, 1).astype(np.float32))


def layout(x_prompt, x_sample, state_delta, c, c_ctx, ada_w, ada_b, norm1_g, norm2_g, w_in_ab, conv_qkv_w, a_log, dt_bias,
           delta_norm_g, conf_dw_w, conf_dw_b, conf_ln_g, conf_ln_b, w_out_ab, w_out_c, peer_wq, peer_k1, peer_k2,
           peer_u, peer_v, final_norm_g):
    A = HEADS * DK
    g = np.asarray
    col = lambda v: g(v).reshape(-1, P).T
    w_in = g(w_in_ab)[0]
    z0, ab0, cf0 = 3 * A, 4 * A, 4 * A + 4 * HEADS
    gains = np.stack([x for l in range(DEPTH) for x in (col(norm1_g[l]), col(norm2_g[l]))] + [col(final_norm_g)]
                     + [np.repeat(g(delta_norm_g)[0][:, None], NC, 1)], 1)
    keys = np.stack([g(peer_k1), g(peer_k2)], 2)
    u = g(peer_u).reshape(DEPTH, P, P, NC, P)
    v = g(peer_v).reshape(DEPTH, P, P, D)
    ac = np.ascontiguousarray
    return {
        "xT": chunked(np.concatenate([g(x_prompt)[0], g(x_sample)[0]], 0).T),
        "pos": position_embedding(),
        "mats": constants()[0],
        "masks": constants()[1],
        "dft": dft_matrices(),
        "gains": ac(gains),
        "cond": chunked(np.stack([g(c_ctx), g(c)[0]], 1)),
        "adab": ac(g(ada_b).reshape(DEPTH, 48, P).transpose(2, 0, 1)),
        "ada_w": ac(g(ada_w).reshape(DEPTH, NC, P, 12, 512).transpose(0, 3, 2, 1, 4)).reshape(DEPTH * 12, P, NC, 512),
        "w_qkv": blocks(w_in[:, 0:z0]),
        "w_zc": blocks(np.concatenate([w_in[:, z0:ab0], w_in[:, cf0:]], 1)),
        "w_ab": chunked(w_in[:, ab0:cf0]),
        "alog": ac(np.broadcast_to(np.stack([g(a_log)[0].reshape(-1), g(dt_bias)[0].reshape(-1)]), (P, 2, 2 * HEADS))),
        "conv_w": chunked(g(conv_qkv_w)[0].T),
        "conf_w": chunked(np.concatenate([g(conf_dw_w)[0].T, g(conf_dw_b)[0][:, None], g(conf_ln_g)[0][:, None], g(conf_ln_b)[0][:, None]], 1)),
        "state": ac(g(state_delta)[0, 0].reshape(2 * HEADS, DK, DK).transpose(1, 0, 2)),
        "w_out_ab": blocks(g(w_out_ab)[0]),
        "w_out_c": blocks(g(w_out_c)[0]),
        "wq": blocks(peer_wq),
        "keys": ac(keys.transpose(0, 4, 1, 2, 3)).reshape(DEPTH, P, NSC, P),
        "u": ac(u.transpose(0, 2, 4, 3, 1)).reshape(DEPTH, P, P, D),
        "v": ac(v.transpose(0, 2, 1, 3)),
    }


def kernel(**inputs):
    import concourse.bacc as bacc
    from concourse.bass_utils import run_bass_kernel_spmd

    arrays = {f"in_{k}": a for k, a in layout(**inputs).items()}
    nc = bacc.Bacc("TRN2", target_bir_lowering=False, num_devices=1)
    d = {k[3:]: nc.dram_tensor(k, a.shape, mybir.dt.from_np(a.dtype), kind="ExternalInput").ap() for k, a in arrays.items()}
    out = {"yT": nc.dram_tensor("out_yT", (P, NC, T), F32, kind="ExternalOutput").ap(),
           "state": nc.dram_tensor("out_state", (2 * HEADS, DK, DK), F32, kind="ExternalOutput").ap()}
    build(nc, d, out)
    r = run_bass_kernel_spmd(nc, [arrays], core_ids=[0]).results[0]
    y = r["out_yT"].transpose(2, 1, 0).reshape(T, D)
    return (y[:S_CTX].reshape(1, S_CTX, D), y[S_CTX:].reshape(1, S_DEC, D),
            r["out_state"].reshape(1, 1, 2, HEADS, DK, DK))
```
